# Optimizing a Trainium2 kernel written in Bass

```python
import jax, jax.numpy as jnp
from jax import lax
import numpy as np

D_MODEL = 1024
BATCH = 1
SEQ = 1024
DEPTH = 1

N_META = 16
EPS = 1e-6
POOL_WINDOWS = (2, 4, 8, 16)
N_POOL_GROUPS = 4
D_POOL = D_MODEL // 2
POOL_GROUP = D_POOL // N_POOL_GROUPS
N_HEADS = 8
D_LAT = D_MODEL // 8
N_IDX_HEADS = 8
D_IDX = 32
INDEX_SCALE = (N_IDX_HEADS ** -0.5) * (D_IDX ** -0.5)
ATTN_SCALE = D_LAT ** -0.5
Q_BLOCK = 128
TOP_K_MAX = 256
D_CONV = D_MODEL // 2
CONV_WIDTH = 3
N_BRANCH = 3
D_FF = -(-8 * D_MODEL // (3 * 256)) * 256
SPLITS = (D_POOL, N_HEADS * D_LAT, D_LAT, N_IDX_HEADS * D_IDX, D_IDX,
          N_IDX_HEADS, D_CONV, D_CONV, D_CONV, N_BRANCH * D_MODEL)
N_IN = sum(SPLITS)


def rms_norm(x, g):
    xf = x.astype(jnp.float32)
    y = xf * lax.rsqrt(jnp.mean(xf * xf, axis=-1, keepdims=True) + EPS)
    return (y * g.astype(jnp.float32)).astype(x.dtype)

def split_columns(p):
    offs, acc = [], 0
    for s in SPLITS[:-1]:
        acc += s
        offs.append(acc)
    return jnp.split(p, offs, axis=-1)

def pool_mixer(u, pool_w, pool_scale):
    B, L, _ = u.shape
    uf = u.astype(jnp.float32)
    cs = lax.cumsum(uf, axis=1)
    pos1 = jnp.arange(1, L + 1)
    outs = []
    for g, w in enumerate(POOL_WINDOWS):
        csg = cs[..., g * POOL_GROUP:(g + 1) * POOL_GROUP]
        shifted = jnp.pad(csg, ((0, 0), (w, 0), (0, 0)))[:, :L]
        count = jnp.minimum(pos1, w).astype(jnp.float32)[None, :, None]
        mean = (csg - shifted) / count
        outs.append(mean - uf[..., g * POOL_GROUP:(g + 1) * POOL_GROUP])
    pooled = jnp.stack(outs, axis=2).astype(u.dtype)
    mixed = jnp.einsum('blgc,gcd->blgd', pooled, pool_w).reshape(B, L, D_POOL)
    return mixed * pool_scale

def dsa_attention(q, qi, wi, c, ki):
    B, L = q.shape[0], q.shape[1]
    k_top = min(TOP_K_MAX, SEQ // 4)
    nb = -(-L // Q_BLOCK)
    Lp = nb * Q_BLOCK
    pad = Lp - L

    def to_blocks(a):
        a = jnp.pad(a, [(0, 0), (0, pad)] + [(0, 0)] * (a.ndim - 2))
        return jnp.moveaxis(a.reshape(B, nb, Q_BLOCK, *a.shape[2:]), 1, 0)

    kpos = jnp.arange(L, dtype=jnp.int32)
    qpos = jnp.arange(Lp, dtype=jnp.int32).reshape(nb, Q_BLOCK)
    wi = wi * INDEX_SCALE

    def block(args):
        qb, qib, wb, pb = args
        s = jnp.einsum('bqhd,bkd->bqhk', qib, ki).astype(jnp.float32)
        score = jnp.einsum('bqhk,bqh->bqk', jax.nn.relu(s), wb.astype(jnp.float32))
        causal = kpos[None, None, :] <= pb[None, :, None]
        score = jnp.where(causal, score, -jnp.inf)
        _, sel = lax.top_k(score, k_top)
        c_sel = jax.vmap(lambda cb, ib: cb[ib])(c, sel)
        logits = jnp.einsum('bqhd,bqkd->bqhk', qb, c_sel).astype(jnp.float32) * ATTN_SCALE
        valid = (sel <= pb[None, :, None])[:, :, None, :]
        p = jax.nn.softmax(jnp.where(valid, logits, -jnp.inf), axis=-1).astype(c.dtype)
        return jnp.einsum('bqhk,bqkd->bqhd', p, c_sel)

    out = lax.map(block, (to_blocks(q), to_blocks(qi), to_blocks(wi), qpos))
    out = jnp.moveaxis(out, 0, 1).reshape(B, Lp, N_HEADS * D_LAT)
    return out[:, :L]

def short_conv_mixer(b_gate, c_gate, u, conv_w):
    v = c_gate * u
    rhs = conv_w.reshape(CONV_WIDTH, 1, D_CONV)
    y = lax.conv_general_dilated(v, rhs, window_strides=(1,),
                                 padding=[(CONV_WIDTH - 1, 0)],
                                 dimension_numbers=('NWC', 'WIO', 'NWC'),
                                 feature_group_count=D_CONV)
    return b_gate * y

def hybrid_layer(h, norm1_g, w_in, b_gate, pool_w, pool_scale, w_a, kv_norm_g,
                 w_b, conv_w, w_c, w_o, norm2_g, w_gate_up, w_down):
    B, L, _ = h.shape
    xn = rms_norm(h, norm1_g)
    p = xn @ w_in
    (u_pool, q, c_lat, q_idx, k_idx, w_idx, cb, cc, cu, g_raw) = split_columns(p)
    y_a = pool_mixer(u_pool, pool_w, pool_scale) @ w_a
    c_lat = rms_norm(c_lat, kv_norm_g)
    attn = dsa_attention(q.reshape(B, L, N_HEADS, D_LAT),
                         q_idx.reshape(B, L, N_IDX_HEADS, D_IDX),
                         w_idx, c_lat, k_idx)
    y_b = attn @ w_b
    y_c = short_conv_mixer(cb, cc, cu, conv_w) @ w_c
    g = jax.nn.sigmoid(g_raw + b_gate).reshape(B, L, N_BRANCH, D_MODEL)
    m = g[:, :, 0] * y_a + g[:, :, 1] * y_b + g[:, :, 2] * y_c
    h = h + m @ w_o
    hn = rms_norm(h, norm2_g)
    gate, up = jnp.split(hn @ w_gate_up, 2, axis=-1)
    return h + (jax.nn.silu(gate) * up) @ w_down

def first_inputs(seed: int = 0) -> dict:
    key = jax.random.key(seed)
    ks = jax.random.split(key, 20)
    f32 = jnp.float32

    def nrm(k, shape, fan):
        return jax.random.normal(k, shape, f32) * (fan ** -0.5)

    def gain(k, shape):
        return 1.0 + 0.1 * jax.random.normal(k, shape, f32)

    return {
        "x": jax.random.normal(ks[0], (BATCH, SEQ, D_MODEL), f32),
        "meta": jax.random.normal(ks[1], (N_META, D_MODEL), f32),
        "norm1_g": gain(ks[2], (DEPTH, D_MODEL)),
        "w_in": nrm(ks[3], (DEPTH, D_MODEL, N_IN), D_MODEL),
        "b_gate": 0.01 * jax.random.normal(ks[4], (DEPTH, N_BRANCH * D_MODEL), f32),
        "pool_w": nrm(ks[5], (DEPTH, N_POOL_GROUPS, POOL_GROUP, POOL_GROUP), POOL_GROUP),
        "pool_scale": gain(ks[6], (DEPTH, D_POOL)),
        "w_a": nrm(ks[7], (DEPTH, D_POOL, D_MODEL), D_POOL),
        "kv_norm_g": gain(ks[8], (DEPTH, D_LAT)),
        "w_b": nrm(ks[9], (DEPTH, N_HEADS * D_LAT, D_MODEL), N_HEADS * D_LAT),
        "conv_w": nrm(ks[10], (DEPTH, CONV_WIDTH, D_CONV), CONV_WIDTH),
        "w_c": nrm(ks[11], (DEPTH, D_CONV, D_MODEL), D_CONV),
        "w_o": nrm(ks[12], (DEPTH, D_MODEL, D_MODEL), D_MODEL),
        "norm2_g": gain(ks[13], (DEPTH, D_MODEL)),
        "w_gate_up": nrm(ks[14], (DEPTH, D_MODEL, 2 * D_FF), D_MODEL),
        "w_down": nrm(ks[15], (DEPTH, D_FF, D_MODEL), D_FF),
        "final_g": gain(ks[16], (D_MODEL,)),
    }

def first_block(x, meta, norm1_g, w_in, b_gate, pool_w, pool_scale, w_a, kv_norm_g,
              w_b, conv_w, w_c, w_o, norm2_g, w_gate_up, w_down, final_g):
    B = x.shape[0]
    meta_b = jnp.broadcast_to(meta[None], (B, N_META, D_MODEL)).astype(x.dtype)
    h = jnp.concatenate([meta_b, x], axis=1)
    for l in range(DEPTH):
        h = hybrid_layer(h, norm1_g[l], w_in[l], b_gate[l], pool_w[l], pool_scale[l],
                         w_a[l], kv_norm_g[l], w_b[l], conv_w[l], w_c[l], w_o[l],
                         norm2_g[l], w_gate_up[l], w_down[l])
    return rms_norm(h, final_g)[:, N_META:]


MEM_LEN = 256
HEAD_DIM = 64
CHUNK = 128
A_GROUPS = 4
A_WIDTH = D_MODEL // 2
A_GROUP_W = A_WIDTH // A_GROUPS
SWA_HEADS = 4
SWA_KV_HEADS = 2
SWA_WIDTH = SWA_HEADS * HEAD_DIM
SWA_KV_WIDTH = SWA_KV_HEADS * HEAD_DIM
WINDOW = 128
MEM_HEADS = 4
MEM_WIDTH = MEM_HEADS * HEAD_DIM
MIX_WIDTH = A_WIDTH + SWA_WIDTH + MEM_WIDTH
IN_WIDTH = 2 * A_WIDTH + SWA_WIDTH + 2 * SWA_KV_WIDTH + MEM_WIDTH + MIX_WIDTH
N_BUCKETS = 32
MAX_DISTANCE = 128
NEG = -1e30


def rms_norm_2(x, g):
    xf = x.astype(jnp.float32)
    y = xf * lax.rsqrt(jnp.mean(xf * xf, axis=-1, keepdims=True) + EPS)
    return (y * g.astype(jnp.float32)).astype(x.dtype)

def t5_causal_buckets(dist):
    n = np.maximum(dist, 0)
    max_exact = N_BUCKETS // 2
    large = max_exact + (np.log(np.maximum(n, 1) / max_exact) / np.log(MAX_DISTANCE / max_exact)
                         * (N_BUCKETS - max_exact)).astype(np.int32)
    large = np.minimum(large, N_BUCKETS - 1)
    return np.where(n < max_exact, n, large).astype(np.int32)

def chunked_spatial_gating(u, v, v_g, v_b, w_s, b_s):
    b, s, _ = u.shape
    nc = s // CHUNK
    vg = v.reshape(b, s, A_GROUPS, A_GROUP_W).astype(jnp.float32)
    mu = jnp.mean(vg, axis=-1, keepdims=True)
    var = jnp.mean(jnp.square(vg - mu), axis=-1, keepdims=True)
    vg = (vg - mu) * lax.rsqrt(var + EPS)
    vg = vg * v_g.reshape(A_GROUPS, A_GROUP_W).astype(jnp.float32) + v_b.reshape(A_GROUPS, A_GROUP_W).astype(jnp.float32)
    vc = vg.astype(v.dtype).reshape(b, nc, CHUNK, A_GROUPS, A_GROUP_W)
    causal = jnp.tril(jnp.ones((CHUNK, CHUNK), dtype=w_s.dtype))
    w = w_s * causal[None]
    sv = jnp.einsum('gts,bnsgc->bntgc', w, vc) + b_s.T[None, None, :, :, None]
    return u * sv.reshape(b, s, A_WIDTH)

def sliding_window_attention(q, k, v, sinks, rel_bias):
    b, s, hq, dh = q.shape
    nb = s // CHUNK
    g = hq // SWA_KV_HEADS
    qb = q.reshape(b, nb, CHUNK, SWA_KV_HEADS, g, dh)

    def band(t):
        tb = t.reshape(b, nb, CHUNK, SWA_KV_HEADS, dh)
        prev = jnp.pad(tb, ((0, 0), (1, 0), (0, 0), (0, 0), (0, 0)))[:, :-1]
        return jnp.concatenate([prev, tb], axis=2)

    kb, vb = band(k), band(v)
    logits = jnp.einsum('bnqhgd,bnjhd->bnhgqj', qb, kb).astype(jnp.float32) * (dh ** -0.5)

    qi = np.arange(CHUNK)[:, None]
    kj = np.arange(2 * CHUNK)[None, :]
    dist = qi + CHUNK - kj
    blk = np.arange(nb)[:, None, None]
    valid = (dist >= 0) & (dist < WINDOW) & (blk * CHUNK + kj - CHUNK >= 0)
    buckets = t5_causal_buckets(dist)
    bias = rel_bias.astype(jnp.float32)[buckets]
    bias = jnp.transpose(bias, (2, 0, 1)).reshape(SWA_KV_HEADS, g, CHUNK, 2 * CHUNK)

    logits = jnp.where(valid[None, :, None, None], logits + bias[None, None], NEG)
    sink = sinks.astype(jnp.float32).reshape(1, 1, SWA_KV_HEADS, g, 1, 1)
    m = jnp.maximum(jnp.max(logits, axis=-1, keepdims=True), sink)
    p = jnp.exp(logits - m)
    probs = p / (jnp.sum(p, axis=-1, keepdims=True) + jnp.exp(sink - m))
    out = jnp.einsum('bnhgqj,bnjhd->bnqhgd', probs.astype(v.dtype), vb)
    return out.reshape(b, s, hq * dh)

def memory_cross_attention(q, mem_k, mem_v):
    b, s, h, dh = q.shape
    logits = jnp.einsum('bshd,bmhd->bhsm', q, mem_k).astype(jnp.float32) * (dh ** -0.5)
    probs = jax.nn.softmax(logits, axis=-1)
    out = jnp.einsum('bhsm,bmhd->bshd', probs.astype(mem_v.dtype), mem_v)
    return out.reshape(b, s, h * dh)

def second_inputs(seed: int = 0) -> dict:
    key = jax.random.key(seed)
    ks = jax.random.split(key, 16)
    f32 = jnp.float32
    x = jax.random.normal(ks[0], (BATCH, SEQ, D_MODEL), f32)
    mem = jax.random.normal(ks[1], (BATCH, MEM_LEN, D_MODEL), f32)
    pre_norm_g = 1.0 + 0.05 * jax.random.normal(ks[2], (DEPTH, D_MODEL), f32)
    post_norm_g = 1.0 + 0.05 * jax.random.normal(ks[3], (DEPTH, D_MODEL), f32)
    mem_norm_g = 1.0 + 0.05 * jax.random.normal(ks[4], (DEPTH, D_MODEL), f32)
    w_in = jax.random.normal(ks[5], (DEPTH, D_MODEL, IN_WIDTH), f32) * D_MODEL ** -0.5
    w_mem_kv = jax.random.normal(ks[6], (DEPTH, D_MODEL, 2 * MEM_WIDTH), f32) * D_MODEL ** -0.5
    v_norm_g = 1.0 + 0.05 * jax.random.normal(ks[7], (DEPTH, A_WIDTH), f32)
    v_norm_b = 0.02 * jax.random.normal(ks[8], (DEPTH, A_WIDTH), f32)
    w_spatial = jax.random.normal(ks[9], (DEPTH, A_GROUPS, CHUNK, CHUNK), f32) * CHUNK ** -0.5
    b_spatial = 1.0 + 0.1 * jax.random.normal(ks[10], (DEPTH, A_GROUPS, CHUNK), f32)
    attn_sinks = 0.5 * jax.random.normal(ks[11], (DEPTH, SWA_HEADS), f32)
    rel_bias = 0.5 * jax.random.normal(ks[12], (N_BUCKETS, SWA_HEADS), f32)
    w_out = jax.random.normal(ks[13], (DEPTH, MIX_WIDTH, D_MODEL), f32) * MIX_WIDTH ** -0.5
    return {"x": x, "mem": mem, "pre_norm_g": pre_norm_g, "post_norm_g": post_norm_g,
            "mem_norm_g": mem_norm_g, "w_in": w_in, "w_mem_kv": w_mem_kv,
            "v_norm_g": v_norm_g, "v_norm_b": v_norm_b, "w_spatial": w_spatial,
            "b_spatial": b_spatial, "attn_sinks": attn_sinks, "rel_bias": rel_bias,
            "w_out": w_out}

def second_block(x, mem, pre_norm_g, post_norm_g, mem_norm_g, w_in, w_mem_kv, v_norm_g, v_norm_b,
              w_spatial, b_spatial, attn_sinks, rel_bias, w_out):
    b, s, _ = x.shape
    m_len = mem.shape[1]
    split_at = np.cumsum([A_WIDTH, A_WIDTH, SWA_WIDTH, SWA_KV_WIDTH, SWA_KV_WIDTH, MEM_WIDTH]).tolist()
    for layer in range(DEPTH):
        h = rms_norm_2(x, pre_norm_g[layer])
        proj = h @ w_in[layer]
        a_u, a_v, sq, sk, sv, mq, z = jnp.split(proj, split_at, axis=-1)

        y_a = chunked_spatial_gating(jax.nn.gelu(a_u), jax.nn.gelu(a_v), v_norm_g[layer],
                                     v_norm_b[layer], w_spatial[layer], b_spatial[layer])

        y_b = sliding_window_attention(sq.reshape(b, s, SWA_HEADS, HEAD_DIM),
                                       sk.reshape(b, s, SWA_KV_HEADS, HEAD_DIM),
                                       sv.reshape(b, s, SWA_KV_HEADS, HEAD_DIM),
                                       attn_sinks[layer], rel_bias)

        mkv = rms_norm_2(mem, mem_norm_g[layer]) @ w_mem_kv[layer]
        mk, mv = jnp.split(mkv, 2, axis=-1)
        y_c = memory_cross_attention(mq.reshape(b, s, MEM_HEADS, HEAD_DIM),
                                     mk.reshape(b, m_len, MEM_HEADS, HEAD_DIM),
                                     mv.reshape(b, m_len, MEM_HEADS, HEAD_DIM))

        y = jnp.concatenate([y_a, y_b, y_c], axis=-1) * jax.nn.silu(z)
        x = x + rms_norm_2(y @ w_out[layer], post_norm_g[layer])
    return x


def setup_inputs(seed=0):
    out = dict(first_inputs(seed))
    for name, value in second_inputs(seed + 1).items():
        if name != "x":
            out[name + "_2"] = value
    return out


def reference(
    x, meta, norm1_g, w_in, b_gate, pool_w, pool_scale, w_a, kv_norm_g, w_b, conv_w, w_c, w_o,
    norm2_g, w_gate_up, w_down, final_g, mem_2, pre_norm_g_2, post_norm_g_2, mem_norm_g_2,
    w_in_2, w_mem_kv_2, v_norm_g_2, v_norm_b_2, w_spatial_2, b_spatial_2, attn_sinks_2,
    rel_bias_2, w_out_2,
):
    x = first_block(
        x, meta, norm1_g, w_in, b_gate, pool_w, pool_scale, w_a, kv_norm_g, w_b, conv_w, w_c,
        w_o, norm2_g, w_gate_up, w_down, final_g,
    )
    return second_block(
        x, mem_2, pre_norm_g_2, post_norm_g_2, mem_norm_g_2, w_in_2, w_mem_kv_2, v_norm_g_2,
        v_norm_b_2, w_spatial_2, b_spatial_2, attn_sinks_2, rel_bias_2, w_out_2,
    )


_drawn_inputs = setup_inputs


def setup_inputs(seed=0):
    import zlib

    import numpy as np

    out = dict(_drawn_inputs(seed))
    spreads = {}
    factors = {'b_gate': 8.0,
     'kv_norm_g': 3.459,
     'mem_norm_g_2': 8.0,
     'v_norm_g_2': 17.576,
     'v_norm_b_2': 41.808,
     'attn_sinks_2': 129.772,
     'b_spatial_2': 5.51,
     'rel_bias_2': 28.044}
    for name, (base, spread) in spreads.items():
        noise = np.random.default_rng([zlib.crc32(name.encode()), seed]).standard_normal(out[name].shape)
        drawn = base * np.exp(spread * noise) if base else spread * noise
        out[name] = __import__('jax').numpy.asarray(drawn.astype(out[name].dtype))
    for name, factor in factors.items():
        out[name] = (out[name] * factor).astype(out[name].dtype)
    return out
```

```python
from contextlib import ExitStack

import numpy as np
import concourse.bass as bass
from concourse import mybir

ALU = mybir.AluOpType
ACT = mybir.ActivationFunctionType
F32 = mybir.dt.float32
F32R = mybir.dt.float32r

P = 128
D = 1024
KD = D // P
S = 1024
META = 16
T = S + META
EPS = 1e-6
HEADS = 8
TOP_K = 256
IDX_SCALE = (8 ** -0.5) * (32 ** -0.5)
ATTN_SCALE = P ** -0.5
D_FF = 2816
FC = D_FF // P
BANK = 512
NB = S // P
MEM = 256
DH = 64
NEG = -1e30
SWA_SPAN = 3 * P
SENT = -3.4e38
FILL = -3.0e38

FULL = [(0, 352), (352, 352), (704, 336)]
REAL = [(META, BANK), (META + BANK, BANK)]
HALF = [(0, BANK), (BANK, BANK)]

U0, Q0, C0, QI0, KI0, CB0, CC0, CU0, G0 = 0, 512, 1536, 1664, 1920, 1960, 2472, 2984, 3496


AU2, AV2, SQ2, SK2, SV2, MQ2, Z2 = 0, 512, 1024, 1280, 1408, 1536, 1792


def block_keys(b):
    return META + P * (b + 1)


def pieces(b):
    n = block_keys(b)
    if n <= BANK:
        return [(0, 1, n)]
    if n <= 2 * BANK:
        return [(0, 2, n // 2)]
    return [(0, 2, 352), (704, 1, n - 704)]


def linear_plan():
    panels, tiles = [], []

    def panel(key, n_tiles):
        panels.append(key)
        tiles.extend((key, j) for j in range(n_tiles))

    panel(("c", 0), 3)
    panel(("kw", 0), 3)
    for m in range(2):
        panel(("qi", m), 2)
    tiles.extend((("csum", 0), j) for j in range(3))
    tiles.append((("wtok", 0), 0))
    for m in range(4):
        panel(("u", m), 3)
        if m == 1:
            tiles.extend((("ctok", 0), j) for j in range(3))
    panel(("poolw", 0), 8)
    for m in range(KD):
        panel(("q", m), 2)
    for m in range(KD):
        panel(("g0", m), 2)
        panel(("wa", m), 2)
    for m in range(4):
        panel(("cc", m), 3)
        panel(("cu", m), 3)
        panel(("cb", m), 2)
    for m in range(KD):
        panel(("g2", m), 2)
        panel(("wc", m), 2)
    for m in range(KD):
        panel(("g1", m), 2)
    for m in range(KD):
        panel(("wb", m), 2)
    for m in range(KD):
        panel(("wo", m), 2)
    return panels, tiles


def second_plan():
    panels, ticks = [], []

    def panel(key, n):
        panels.append(key)
        ticks.extend((key, j) for j in range(n))

    for m in range(4):
        panel(("av", m), 2)
    for m in range(4):
        panel(("au", m), 2)
    for m in range(2):
        panel(("mk", m), 1)
    for m in range(2):
        panel(("mv", m), 1)
    panel(("sk", 0), 2)
    panel(("sv", 0), 2)
    for m in range(2):
        panel(("sq", m), 2)
    for m in range(2):
        panel(("mq", m), 2)
    for m in (4, 5, 6, 7, 0, 1, 2, 3):
        panel(("z", m), 2 if m >= 4 else 4)
    for n in range(2 * KD):
        panel(("wout", n), NB if n % KD == KD - 1 else 1)
    upper = [("x2", n) for n in range(16)] + [("mem", n) for n in range(4)] + [("wsp", 0), ("rb", 0)]
    upper += [("av", n) for n in range(NB)] + [("flip", 0), ("flip", 1), ("mvt", 0)]
    upper += [("sp", n) for n in range(8)] + [("svt", 0), ("svt", 1)]
    return panels, ticks, upper


def bucket_table():
    table = np.zeros((64, SWA_SPAN), np.float32)
    for i in range(SWA_SPAN):
        dist = 2 * P - 1 - i
        if not 0 <= dist < P:
            table[32, i] = 1.0
            continue
        large = 16 + int(np.log(max(dist, 1) / 16) / np.log(128 / 16) * 16)
        table[dist if dist < 16 else min(large, 31), i] = 1.0
    return table


def build(nc, I, out, scratch):
    PANELS, TILES = linear_plan()
    PANEL_AT = {key: p for p, key in enumerate(PANELS)}
    TILE_AT = {key: n for n, key in enumerate(TILES)}
    THROUGH = {p: max(n for (key, _), n in TILE_AT.items() if key == PANELS[p]) + 1 for p in range(len(PANELS))}
    WIDTH = {"wa": 512, "wc": 512, "poolw": 512}

    PB, L0 = len(PANELS), len(TILES)
    PANELS2, TICKS2, UPPER = second_plan()
    PB2, L2 = PB + 3 * FC, L0 + 20 * FC
    AT2 = {key: PB2 + n for n, key in enumerate(PANELS2)}
    TICK2 = {key: L2 + n for n, key in enumerate(TICKS2)}
    THROUGH2 = {key: max(n for (k_, _), n in TICK2.items() if k_ == key) + 1 for key in PANELS2}
    UP_AT = {key: n for n, key in enumerate(UPPER)}

    def width(p):
        if PB <= p < PB2:
            return KD * P
        if p >= PB2:
            return BANK if PANELS2[p - PB2][0] == "wout" else KD * P
        return WIDTH.get(PANELS[p][0], KD * P)

    def through(p):
        if p < PB:
            return THROUGH[p]
        if p < PB2:
            off = p - PB
            return {0: L0 + 2, 1: L0 + 4, 3 * FC - 1: L2, 3 * FC - 2: L2 - 16}[off]
        return THROUGH2[PANELS2[p - PB2]]

    def gu_at(it, par):
        return 40 * it + (L0 + 20 * par - 16)

    def panel_no(it, off):
        return 6 * it + (PB + off)

    def loads_of(it, off):
        return 3 * it + ((PB + off) // 2 + 1)

    q_scratch, g1_scratch, x2_scratch, rb_scratch = scratch["q"], scratch["g1"], scratch["x2"], scratch["rb"]
    w_in2 = I["w_in_2"][0]

    def second_source(key):
        kind, m = key
        if kind == "wout":
            return I["w_out_2"][0][P * (m % KD):P * (m % KD) + P, BANK * (m // KD):BANK * (m // KD) + BANK]
        if kind in ("mk", "mv"):
            w, c = I["w_mem_kv_2"][0], P * m + (MEM if kind == "mv" else 0)
        else:
            w, c = w_in2, {"av": AV2, "au": AU2, "sk": SK2, "sv": SV2, "sq": SQ2, "mq": MQ2, "z": Z2}[kind] + P * m
        return w[:, c:c + P].rearrange("(k p) c -> p k c", p=P)
    w_in = I["w_in"][0]

    def panel_source(key):
        kind, m = key
        cols = {"c": C0, "kw": KI0, "qi": QI0 + P * m, "u": U0 + P * m, "q": Q0 + P * m, "cb": CB0 + P * m,
                "cc": CC0 + P * m, "cu": CU0 + P * m, "g0": G0 + P * m, "g1": G0 + D + P * m, "g2": G0 + 2 * D + P * m}
        if kind in cols:
            w, c = w_in, cols[kind]
        elif kind == "poolw":
            return I["pool_w"][0].rearrange("g c d -> c g d")
        else:
            w, c = I[{"wa": "w_a", "wb": "w_b", "wc": "w_c", "wo": "w_o"}[kind]][0], P * m
        return w[:, c:c + P].rearrange("(k p) c -> p k c", p=P)

    with ExitStack() as ctx:
        at = [1152]

        def place(name, shape, dt, offset=None):
            if offset is None:
                offset = at[0]
                at[0] += -(-int(np.prod(shape[1:])) * 4 // 32) * 32
            return nc.alloc_sbuf_tensor_at(name, shape, dt, offset=offset)

        def sem(name):
            return ctx.enter_context(nc.semaphore(name))

        x_hi = place("x_hi", [P, KD, T], F32R)
        x_lo = place("x_lo", [P, KD, T], F32R)
        w_raw = place("w_raw", [P, 2, KD * P], F32)
        w_hi = place("w_hi", [P, 2, KD * P], F32R)
        w_lo = place("w_lo", [P, 2, KD * P], F32R)
        SC_AT = [sum(block_keys(a) for a in range(b)) for b in range(NB + 1)]
        score = place("score", [P, SC_AT[NB]], F32)
        c_hi = place("c_hi", [P, T], F32R)
        c_lo = place("c_lo", [P, T], F32R)
        ck_hi = place("ck_hi", [P, 9, P], F32R)
        ck_lo = place("ck_lo", [P, 9, P], F32R)
        RA = at[0]
        at[0] += 4 * 2 * T * 4
        RB = at[0]
        at[0] += KD * S * 4
        ident = place("ident", [P, P], F32)
        ones = place("ones", [P, P], F32)
        vec = place("vec", [P, 89], F32)
        w_tok = place("w_tok", [P, NB, 8], F32)
        ss = place("ss", [P, 9], F32)
        rstd = place("rstd", [P, 9], F32)
        best = place("best", [P, 2, 8], F32)
        causal = place("causal", [P, P], F32)
        row_max = place("row_max", [P, 2, 8], F32)
        neg_max = place("neg_max", [P, 2, 4], F32)
        row_sum = place("row_sum", [P, 2, 4], F32)
        inv_sum = place("inv_sum", [P, 2, 4], F32)
        anti = place("anti", [P, P], F32)
        relb = place("relb", [64, P], F32)
        nst = place("nst", [P, 6, 8], F32)
        gfg = place("gfg", [P, KD], F32)
        sink_n = place("sink_n", [P, 4], F32)
        sink = place("sink", [P, 4], F32)
        bst = place("bst", [P, 2, 4, 6], F32)
        bag = place("bag", [P, 2, 4, 2], F32)
        vrs = place("vrs", [P, 2, 4], F32)
        mem_ss = place("mem_ss", [P, 2], F32)
        mx2 = place("mx2", [P, 2, 4], F32)
        nm2 = place("nm2", [P, 2, 4], F32)
        se2 = place("se2", [P, 2, 4], F32)
        rs2 = place("rs2", [P, 2, 4], F32)
        osum = place("osum", [P, 3, NB], F32)
        turn = place("turn", [P, 4], F32)
        ST = at[0]
        VEC = {}
        rows = 0
        for name in ("norm1_g", "norm2_g", "final_g", "pre_norm_g_2", "post_norm_g_2", "mem_norm_g_2", "b_gate",
                     "pool_scale", "conv_w", "kv_norm_g"):
            VEC[name] = rows
            rows += int(np.prod(I[name].shape)) // P

        def v(name, n):
            return vec[:, VEC[name] + n:VEC[name] + n + 1]

        x_tok = place("x_tok", [P, 9, D], F32, RA)
        qi_hi = place("qi_hi", [P, 2, S], F32R, RA)
        qi_lo = place("qi_lo", [P, 2, S], F32R, RA + 8 * S)
        ki_hi = place("ki_hi", [P, T], F32R, RA + 16 * S)
        ki_lo = place("ki_lo", [P, T], F32R, RA + 16 * S + 4 * T)
        ki_f = place("ki_f", [P, T], F32, RA + 16 * S + 8 * T)
        pool_hi = place("pool_hi", [P, 4, S], F32R, RB)
        pool_lo = place("pool_lo", [P, 4, S], F32R, RB + 16 * S)
        br_hi = place("br_hi", [P, 4, S], F32R, RA)
        br_lo = place("br_lo", [P, 4, S], F32R, RA + 16 * S)
        mix = place("mix", [P, KD, S], F32, RB)
        logit = place("logit", [P, 2, 4, T], F32, RA)
        x_res = place("x_res", [P, KD, D], F32, RA)
        vec_rows = place("vec_rows", [P, P], F32, ST)
        junk = place("junk", [P, 2, D], F32, ST + 512)
        relu_s = place("relu_s", [P, 2, T], F32, ST)
        u_s = place("u_s", [P, 2, T], F32, ST + 8 * T)
        sum_s = place("sum_s", [P, 2, T], F32, ST + 16 * T)
        w_row = place("w_row", [P, S], F32, ST + 24 * T)
        c_raw = place("c_raw", [P, T], F32, RB + 20224)
        c_rs = place("c_rs", [P, T], F32, RB + 20224 + 4 * T)
        c_sq = place("c_sq", [P, T], F32, RB + 20224 + 8 * T)
        stage = place("stage", [P, 2, S], F32, ST)
        y_s = place("y_s", [P, 2, S], F32, ST + 8 * S)
        mix_s = place("mix_s", [P, 2, BANK], F32, ST + 16 * S)
        cv = place("cv", [P, 6, T], F32, ST)
        q_f = place("q_f", [P, HEADS, P], F32, ST)
        q_hi = place("q_hi", [P, 2, HEADS, P], F32R, ST + 4 * S)
        q_lo = place("q_lo", [P, 2, HEADS, P], F32R, ST + 12 * S)
        pt_hi = place("pt_hi", [P, 2, BANK], F32R, ST + 20 * S)
        pt_lo = place("pt_lo", [P, 2, BANK], F32R, ST + 24 * S)
        g1_s = place("g1_s", [P, 2, S], F32, ST)
        gy_s = place("gy_s", [P, 2, BANK], F32, ST + 8 * S)

        n_acc = place("n_acc", [P, 2, S], F32, ST)
        n_sq = place("n_sq", [P, 2, 2, S], F32, ST + 8 * S)
        n_diag2 = place("n_diag2", [P, S], F32, ST + 8 * S)
        n_st = place("n_st", [P, 2, S], F32, ST + 16 * S)
        n_diag = place("n_diag", [P, S], F32, ST + 24 * S)
        silu_s = place("silu_s", [P, S], F32, RA)
        a_f = place("a_f", [P, S], F32, RA + 4 * S)
        a_hi = place("a_hi", [P, 2, S], F32R, RA + 8 * S)
        a_lo = place("a_lo", [P, 2, S], F32R, RA + 16 * S)
        RS = 1152 + 2 * KD * T * 4 + 6 * KD * P * 4
        x2_s = place("x2_s", [P, 2, S], F32, RA + 24 * S)
        memt_hi = place("memt_hi", [P, KD, MEM], F32R, RA)
        memt_lo = place("memt_lo", [P, KD, MEM], F32R, RA + 8 * S)
        vln_lo = place("vln_lo", [P, NB, BANK], F32R, RA + 16 * S)
        vd_hi = place("vd_hi", [P, NB, 2, P], F32R, RA)
        vd_lo = place("vd_lo", [P, NB, 2, P], F32R, RA + 8 * S)
        kd_hi = place("kd_hi", [P, 2, S], F32R, RA + 16 * S)
        kd_lo = place("kd_lo", [P, 2, S], F32R, RA + 24 * S)
        wy = place("wy", [P, NB, BANK], F32, RA)
        av_s = place("av_s", [P, 4, S], F32, RB)
        vln_hi = place("vln_hi", [P, NB, BANK], F32R, RB + 16 * S)
        mq_hi = place("mq_hi", [P, 2, S], F32R, RB)
        mq_lo = place("mq_lo", [P, 2, S], F32R, RB + 8 * S)
        sq_hi = place("sq_hi", [P, 2, S], F32R, RB + 16 * S)
        sq_lo = place("sq_lo", [P, 2, S], F32R, RB + 24 * S)
        x2_tok = place("x2_tok", [P, NB, D], F32, RB)
        yz = place("yz", [P, KD, S], F32, RS)
        mem_tok = place("mem_tok", [P, 2, D], F32, RS + 16 * S)
        kd_f = place("kd_f", [P, 2, S], F32, RS + 16 * S)
        vgb = place("vgb", [P, BANK], F32, RS + 24 * S)
        vbb = place("vbb", [P, BANK], F32, RS + 26 * S)
        bsp = place("bsp", [P, 4, P], F32, RS + 28 * S)
        sv_f = place("sv_f", [P, S], F32, RS + 24 * S)
        w_sp = place("w_sp", [P, 4, P], F32, RS + 32 * S)
        onehot = place("onehot", [64, SWA_SPAN], F32, RS + 34 * S)
        o_s = place("o_s", [P, 4, D], F32, RS)
        mk_hi = place("mk_hi", [P, 2, MEM], F32R, ST)
        mk_lo = place("mk_lo", [P, 2, MEM], F32R, ST + 2 * S)
        mv_hi = place("mv_hi", [P, 2, MEM], F32R, ST + 4 * S)
        mv_lo = place("mv_lo", [P, 2, MEM], F32R, ST + 6 * S)
        bias = place("bias", [P, 4, 2 * P], F32, ST + 8 * S)
        wt_hi = place("wt_hi", [P, 4, P], F32R, ST + 12 * S)
        wt_lo = place("wt_lo", [P, 4, P], F32R, ST + 14 * S)
        vn_s = place("vn_s", [P, 2, BANK], F32, ST + 16 * S)
        mv_f = place("mv_f", [P, 2, MEM], F32, ST + 20 * S)
        rb_s = place("rb_s", [4, SWA_SPAN], F32, ST + 22 * S)
        btoe = place("btoe", [P, 4, 2 * P], F32, ST + 24 * S)
        p_s = place("p_s", [P, 2, 4, 2 * P], F32, ST + 12 * S)
        p2_hi = place("p2_hi", [P, 2, BANK], F32R, ST + 20 * S)
        p2_lo = place("p2_lo", [P, 2, BANK], F32R, ST + 24 * S)
        z_s = place("z_s", [P, BANK], F32, RS + 32 * S)
        assert ST + 28 * S <= 229344
        pg = place("pg", [P, D], F32, ST + 12 * S)
        sq_junk = place("sq_junk", [P, 2, BANK], F32, ST + 16 * S)

        ps = ctx.enter_context(nc.psum_tensor("ps", [P, 8, BANK], F32))

        x_load = [sem(f"x_load{r}") for r in range(9)]
        vec_load, const_ready, vec_full, vec_ready = sem("vec_load"), sem("const_ready"), sem("vec_full"), sem("vec_ready")
        raw_load = [sem("raw_load0"), sem("raw_load1")]
        whi_done, wlo_done, lin_full, pair_full = sem("whi_done"), sem("wlo_done"), sem("lin_full"), sem("pair_full")
        sq_done, ms_done, inv_done, rt_done, xs_done = sem("sq_done"), sem("ms_done"), sem("inv_done"), sem("rt_done"), sem("xs_done")
        xt_full, xhi_done, xlo_done = sem("xt_full"), sem("xhi_done"), sem("xlo_done")
        csq_done, craw_done, cms_done, cinv_done = sem("csq_done"), sem("craw_done"), sem("cms_done"), sem("cinv_done")
        crt_done, cn_done, chi_done, clo_done = sem("crt_done"), sem("cn_done"), sem("chi_done"), sem("clo_done")
        ckhi_done, cklo_done, wtok_done = sem("ckhi_done"), sem("cklo_done"), sem("wtok_done")
        kif_done, kihi_done, kilo_done, ki_copies = sem("kif_done"), sem("kihi_done"), sem("kilo_done"), sem("ki_copies")
        qihi_done, qilo_done = sem("qihi_done"), sem("qilo_done")
        relu_done, score_acc, topk_step, mask_ready = sem("relu_done"), sem("score_acc"), sem("topk_step"), sem("mask_ready")
        u_done, pool_step, pool_sub, pooled_done = sem("u_done"), sem("pool_step"), sem("pool_sub"), sem("pooled_done")
        mixf_done, brhi_done, brlo_done = sem("mixf_done"), sem("brhi_done"), sem("brlo_done")
        q_copied, q_store = sem("q_copied"), [sem("q_store0"), sem("q_store1")]
        gate_done, y_done, gated, gate_used = sem("gate_done"), sem("y_done"), sem("gated"), sem("gate_used")
        cv_in, cv_v, cv_tap, cv_step, cv_sum = sem("cv_in"), sem("cv_v"), sem("cv_tap"), sem("cv_step"), sem("cv_sum")
        g1_done, g1_store = sem("g1_done"), [sem("g1_store0"), sem("g1_store1")]
        q_load, qhi_done, qlo_done = sem("q_load"), sem("qhi_done"), sem("qlo_done")
        masked, nm_done, exp_done, inv_step, norm_done = sem("masked"), sem("nm_done"), sem("exp_done"), sem("inv_step"), sem("norm_done")
        trans_full, pthi_done, ptlo_done, pv_step = sem("trans_full"), sem("pthi_done"), sem("ptlo_done"), sem("pv_step")
        ohi_done, olo_done = sem("ohi_done"), sem("olo_done")
        g1_load, gy_done, m_acc = [sem("g1_load0"), sem("g1_load1")], sem("gy_done"), sem("m_acc")
        mhi_done, mlo_done, xres_load, h_done = sem("mhi_done"), sem("mlo_done"), sem("xres_load"), sem("h_done")

        sqa_done, sqb_done, acca_done, accb_done, stat_full, nst_step = sem("sqa_done"), sem("sqb_done"), sem("acca_done"), sem("accb_done"), sem("stat_full"), sem("nst_step")
        nrt_done, diag_done, rs_full, upper_free, nhi_done, nlo_done = sem("nrt_done"), sem("diag_done"), sem("rs_full"), sem("upper_free"), sem("nhi_done"), sem("nlo_done")
        x2_done, silu_done, af_done, ahi_done, alo_done = sem("x2_done"), sem("silu_done"), sem("af_done"), sem("ahi_done"), sem("alo_done")
        c2_load, mem_load, msq_done, mst_step, mrt_done, ms_scaled = sem("c2_load"), sem("mem_load"), sem("msq_done"), sem("mst_step"), sem("mrt_done"), sem("ms_scaled")
        wsp_done = sem("wsp_done")
        rb_store, rb_load = sem("rb_store"), sem("rb_load")
        ln_step = sem("ln_step")

        kd_copies = sem("kd_copies")

        zt_done, b_done = sem("zt_done"), sem("b_done")
        mx_step, pn_step, pt_full = sem("mx_step"), sem("pn_step"), sem("pt_full")
        pvg_done = sem("pvg_done")
        os_step, osrt_done = sem("os_step"), sem("osrt_done")
        oa_done, ob_done, pg_load, rb_const = sem("oa_done"), sem("ob_done"), sem("pg_load"), sem("rb_const")
        vn_ready, mx_step2, on_done, sink_done = sem("vn_ready"), sem("mx_step2"), sem("on_done"), sem("sink_done")
        x2_store, x2_load, o_store = [sem("x2_store0"), sem("x2_store1")], sem("x2_load"), [sem(f"o_store{n}") for n in range(4)]

        XGROUPS = [(0, [0, 1, 2, 3], BANK), (BANK, [4, 5, 6, 7], BANK), (2 * BANK, [8], META)]

        def tile_rows(r):
            return P if r < 8 else META

        UNITS = [(b, pc, h) for b in range(NB) for pc in range(len(pieces(b))) for h in range(HEADS)]
        SCORED = {b: max(n for n, u in enumerate(UNITS) if u[0] == b) + 1 for b in range(NB)}
        TOPK_PAIRS = [(1,), (2, 3), (4, 5), (6, 7)]
        MASK_AT = {b: n for n, b in enumerate([0] + [b for pair in TOPK_PAIRS for b in pair])}
        GROUPS = [(b, g) for b in range(NB) for g in range(2)]
        LOGITS = [(b, g, h, pc) for b, g in GROUPS for h in range(4) for pc in range(len(pieces(b)))]
        LOGITS_TO = [sum(4 * len(pieces(b)) for b, _ in GROUPS[:n + 1]) for n in range(len(GROUPS))]
        CHUNKS_TO = [sum(b + 2 for b, _ in GROUPS[:n + 1]) for n in range(len(GROUPS))]

        x2_copied, X2_0 = craw_done, 3
        memhi_done, MEMHI_0 = csq_done, 3
        wthi_done, WTHI_0 = chi_done, 1
        rb_done, RB_0 = crt_done, 1
        av_done, AV_0 = u_done, 3 * 4
        lnrt_done, LNRT_0 = rt_done, 3
        vlnhi_done, VLNHI_0 = xhi_done, 3 * KD
        bias_done, BIAS_0 = wtok_done, 1
        au_done, AU_0 = mixf_done, 8
        mkhi_done, MKHI_0 = kihi_done, 1
        mvf_done, MVF_0 = kif_done, 3
        mvthi_done, MVTHI_0 = ckhi_done, 3
        skf_done, SKF_0 = q_copied, 2 * KD
        svf_done, SVF_0 = g1_done, 2 * KD
        svhi_done, SVHI_0 = brhi_done, 12
        sqhi_done, SQHI_0 = qihi_done, 4
        mqhi_done, MQHI_0 = qhi_done, NB
        zs_done, ZS_0 = gate_done, 4 * KD
        zsilu_done, ZSILU_0 = y_done, 4 * KD
        e2_done, E2_0 = exp_done, 4 * len(GROUPS)
        p2hi_done, P2HI_0 = pthi_done, CHUNKS_TO[-1]
        yhi_done, YHI_0 = mhi_done, KD
        wy_done, WY_0 = cv_in, 32
        wysq_done, WYSQ_0 = sq_done, 9
        ysq_done, YSQ_0 = cv_tap, 12
        kdhi_done, KDHI_0 = ohi_done, len(GROUPS)
        memlo_done, MEMLO_0 = ms_done, 3
        wtlo_done, WTLO_0 = clo_done, 1
        mklo_done, MKLO_0 = kilo_done, 1
        mvtlo_done, MVTLO_0 = cklo_done, 3
        sp_sum, SPSUM_0 = masked, LOGITS_TO[-1]
        sp_done, SP_0 = m_acc, 2 * KD
        svlo_done, SVLO_0 = olo_done, len(GROUPS)
        sqlo_done, SQLO_0 = qilo_done, 4
        mqlo_done, MQLO_0 = norm_done, 4 * len(GROUPS)
        vn_sub, VSUB_0 = xs_done, 9
        vn_done, VN_0 = gy_done, 2 * KD
        xn_done, XN_0 = cn_done, 1
        nm2_done, NM2_0 = nm_done, len(GROUPS)
        pn_done, PN_0 = score_acc, len(UNITS)
        p2lo_done, P2LO_0 = ptlo_done, CHUNKS_TO[-1]
        yloa_done, YLOA_0 = mlo_done, KD
        vlnlo_done, VLNLO_0 = pooled_done, 4
        kdlo_done, KDLO_0 = brlo_done, 12
        ylob_done, YLOB_0 = qlo_done, NB
        pv_full, PV_0 = pv_step, CHUNKS_TO[-1]
        up_full, UP_0 = xt_full, 24
        lg_full, LG_0 = pair_full, len(UNITS) + LOGITS_TO[-1]

        def released2(key, j):
            kind, m = key
            if kind == "z":
                return (zs_done, ZS_0 + 2 * (m - 4) + j + 1) if m >= 4 else (zsilu_done, ZSILU_0 + 4 * m + j + 1)
            s, before, per = {"av": (av_done, AV_0, 2), "au": (au_done, AU_0, 2), "mk": (mklo_done, MKLO_0, 1), "mv": (mvf_done, MVF_0, 1),
                              "sk": (skf_done, SKF_0, 4), "sv": (svf_done, SVF_0, 2), "sq": (sqlo_done, SQLO_0, 2),
                              "mq": (mqlo_done, MQLO_0, 2)}[kind]
            return s, before + per * m + (2 * j + 2 if kind == "sk" else j + 1)

        LINEAR2 = [key for key in TICKS2 if key[0][0] != "wout"]
        LIN_AT = {key: n for n, key in enumerate(LINEAR2)}

        def up_released(key):
            kind, n = key
            return {"x2": (x2_copied, X2_0 + n + 1), "mem": (memlo_done, MEMLO_0 + 2 * n + 2), "wsp": (wtlo_done, WTLO_0 + 1),
                    "rb": (rb_done, RB_0 + 1), "av": (vn_sub, VSUB_0 + 4 * n + 4), "flip": (bias_done, BIAS_0 + n + 1),
                    "mvt": (mvtlo_done, MVTLO_0 + 1), "sp": (sp_sum, SPSUM_0 + n + 1), "svt": (svlo_done, SVLO_0 + 2 * n + 2)}[kind]

        UNITS2 = [(b, kind) for b in range(NB) for kind in range(2)]

        def key_chunks(n):
            return [1] if n == 0 else [0, 1]

        TURN_AT = {t: i for i, t in enumerate((n, kc) for n in range(len(UNITS2)) for kc in key_chunks(n))}

        def released(key, j):
            kind, m = key
            if kind in ("g0", "g2"):
                return gate_done, 2 * (m + (KD if kind == "g2" else 0)) + j + 1
            if kind in ("wa", "wc"):
                return y_done, 2 * (m + (KD if kind == "wc" else 0)) + j + 1
            if kind in ("cc", "cu", "cb"):
                return cv_in, 8 * m + {"cc": 0, "cu": 3, "cb": 6}[kind] + j + 1
            s, per = {"c": (craw_done, 3), "kw": (kif_done, 3), "qi": (qilo_done, 2), "csum": (cms_done, 3),
                      "ctok": (cklo_done, 3), "wtok": (wtok_done, 1), "u": (u_done, 3), "poolw": (mixf_done, 8),
                      "q": (q_copied, 2), "g1": (g1_done, 2), "wb": (gy_done, 2), "wo": (h_done, 2)}[kind]
            return s, per * m + j + 1

        def pair(n, nch, w):
            a = 4 + 2 * (n % 2)
            return ps[:, a:a + nch, 0:w]

        def wide(ap, nch):
            return ap.rearrange("p (n w) -> p n w", n=nch)

        block = ctx.enter_context(nc.Block())

        @block.sync
        def _(sp):
            meta, x = I["meta"], I["x"][0]
            sp.dma_start(x_tok[0:META, 0, :], meta).then_inc(x_load[0], 16)
            sp.dma_start(x_tok[META:P, 0, :], x[0:P - META, :]).then_inc(x_load[0], 16)
            for r in range(1, 9):
                sp.dma_start(x_tok[0:tile_rows(r), r, :], x[P * r - META:P * r - META + tile_rows(r), :]).then_inc(x_load[r], 16)
            for name, row in VEC.items():
                n = int(np.prod(I[name].shape)) // P
                a = I[name]
                a = a.rearrange("(n p) -> n p", p=P) if len(a.shape) == 1 else (
                    a[0].rearrange("(n p) -> n p", p=P) if len(a.shape) == 2 else a[0].rearrange("t (n p) -> (t n) p", p=P))
                sp.dma_start(vec_rows[row:row + n, :], a).then_inc(vec_load, 16)

            def load(p, src):
                if p >= 2:
                    sp.wait_ge(wlo_done, p - 1)
                dst = w_raw[:, p % 2, 0:width(p)]
                sp.dma_start(dst.rearrange("p (k c) -> p k c", c=P) if len(src.shape) == 3 else dst, src).then_inc(raw_load[p % 2], 16)

            for p, key in enumerate(PANELS):
                load(p, panel_source(key))
                if key == ("qi", 1):
                    sp.wait_ge(kif_done, 3)
                    for j in range(1, 4):
                        sp.dma_start(ki_f[32 * j:32 * j + 32, :], ki_f[0:32, :]).then_inc(ki_copies, 16)
                if key == ("wb", 1):
                    sp.wait_ge(q_store[0], 64)
                    sp.wait_ge(q_store[1], 64)
                    sp.wait_ge(g1_store[0], 64)
                    sp.wait_ge(g1_store[1], 64)
                    for b in range(NB):
                        if b >= 1:
                            sp.wait_ge(qlo_done, b)
                        sp.dma_start(q_f[:, :, :], q_scratch[:, :, P * b:P * b + P].rearrange("h d t -> d h t")).then_inc(q_load, 16)
                    sp.wait_ge(olo_done, 16)
                    for m in range(2):
                        sp.dma_start(g1_s[:, m, :], g1_scratch[m]).then_inc(g1_load[m], 16)
                    sp.dma_start(x_res[:, :, :], x.rearrange("(r p) d -> p r d", p=P)).then_inc(xres_load, 16)
                if key[0] == "wb" and key[1] >= 2:
                    sp.wait_ge(m_acc, 2 * (key[1] - 1))
                    sp.dma_start(g1_s[:, key[1] % 2, :], g1_scratch[key[1]]).then_inc(g1_load[key[1] % 2], 16)
            sp.wait_ge(rb_const, 4)
            sp.dma_start(relb[0:32, 0:4], I["rel_bias_2"]).then_inc(c2_load, 16)
            sp.dma_start(onehot[:, :], I["bucket_table"]).then_inc(c2_load, 16)
            sp.dma_start(w_sp[:, :, :], I["w_spatial_2"][0].rearrange("g t s -> t g s")).then_inc(c2_load, 16)
            sp.dma_start(vgb[:, :], I["v_norm_g_2"][0].partition_broadcast(P)).then_inc(c2_load, 16)
            sp.dma_start(vbb[:, :], I["v_norm_b_2"][0].partition_broadcast(P)).then_inc(c2_load, 16)
            sp.dma_start(bsp[:, :, :], I["b_spatial_2"][0].partition_broadcast(P)).then_inc(c2_load, 16)
            sp.dma_start(sink_n[:, :], I["attn_sinks_2"][0].partition_broadcast(P)).then_inc(c2_load, 16)
            sp.dma_start(mem_tok[:, :, :], I["mem_2"][0].rearrange("(r p) d -> p r d", p=P)).then_inc(mem_load, 16)

            w_gu, w_dn = I["w_gate_up"][0], I["w_down"][0]

            def load_mlp(it, off, src):
                sp.wait_ge(wlo_done, panel_no(it, off) - 1)
                sl = (PB + off) % 2
                dst = w_raw[:, sl, :]
                sp.dma_start(dst.rearrange("p (k c) -> p k c", c=P) if len(src.shape) == 3 else dst, src).then_inc(raw_load[sl], 16)

            def gate_up(c, half):
                return w_gu[:, bass.ds(c * P + half * D_FF, P)].rearrange("(k p) c -> p k c", p=P)

            def mlp_chunk(it, par):
                c = 2 * it + par
                load_mlp(it, 3 * par + 2, gate_up(c + 1, 0))
                load_mlp(it, 3 * par + 3, gate_up(c + 1, 1))
                load_mlp(it, 3 * par + 4, w_dn[bass.ds(c * P, P), :])

            load_mlp(0, 0, gate_up(0, 0))
            load_mlp(0, 1, gate_up(0, 1))
            with sp.Fori(0, (FC - 2) // 2) as it:
                for par in range(2):
                    mlp_chunk(it, par)
            mlp_chunk((FC - 2) // 2, 0)
            load_mlp(0, 3 * FC - 1, w_dn[P * (FC - 1):P * FC, :])

            for key in PANELS2:
                load(AT2[key], second_source(key))
                if key == ("sq", 0):
                    sp.wait_ge(skf_done, SKF_0 + 4)
                    sp.dma_start(kd_f[DH:P, 0, :], kd_f[0:DH, 0, :]).then_inc(kd_copies, 16)
                    sp.dma_start(kd_f[0:DH, 1, :], kd_f[DH:P, 1, :]).then_inc(kd_copies, 16)
                if key == ("wout", 2):
                    sp.wait_ge(x2_store[0], 64)
                    sp.wait_ge(x2_store[1], 64)
                    sp.wait_ge(lg_full, LG_0 + len(UNITS2))
                    sp.dma_start(x2_tok[:, :, :], x2_scratch.rearrange("(r p) d -> p r d", p=P)).then_inc(x2_load, 16)
                    sp.wait_ge(pt_full, len(TURN_AT))
                    sp.dma_start(pg[:, :], I["post_norm_g_2"][0].partition_broadcast(P)).then_inc(pg_load, 16)
            for b in range(NB):
                sp.wait_ge(oa_done, b + 1)
                sp.wait_ge(ob_done, b + 1)
                sp.dma_start(out[0, P * b:P * b + P, :], o_s[:, b % 4, :]).then_inc(o_store[b % 4], 16)
            for n in range(4):
                sp.wait_ge(o_store[n], 32)

        @block.tensor
        def _(pe):
            def open_tile(n):
                if n >= 4:
                    pe.wait_ge(*released(*TILES[n - 4]))
                return n % 4

            def product(key, rhs_hi, rhs_lo, chunks, kd=KD, extra=None, ready=None):
                p = PANEL_AT[key]
                s = p % 2
                pe.wait_ge(wlo_done, p + 1)
                for j, (t0, n) in enumerate(chunks):
                    b = open_tile(TILE_AT[key, j])
                    for k in range(kd):
                        if ready is not None and j == 0:
                            pe.wait_ge(ready, k + 1)
                        for i, (w, r) in enumerate(((w_hi, rhs_hi), (w_hi, rhs_lo), (w_lo, rhs_hi))):
                            mm = pe.matmul(ps[:, b, 0:n], w[:, s, P * k:P * k + P], r[:, k, t0:t0 + n],
                                           start=k == 0 and i == 0, stop=k == kd - 1 and i == 2 and extra is None)
                    if extra is not None:
                        mm = extra(j, b)
                    mm.then_inc(lin_full, 1)

            pe.wait_ge(const_ready, 5)
            pe.wait_ge(vec_load, 16 * 10)
            pe.transpose(ps[:, 7, 0:rows], vec_rows[0:rows, :], ident[0:rows, 0:rows]).then_inc(vec_full, 1)
            n = 0
            for t0, tiles, w in XGROUPS:
                pe.wait_ge(xs_done, tiles[-1] + 1)
                for c in range(KD):
                    if n >= 4:
                        pe.wait_ge(xlo_done, n - 3)
                    for r in tiles:
                        k = tile_rows(r)
                        mm = pe.transpose(ps[:, n % 4, P * (r % 4):P * (r % 4) + k], x_tok[0:k, r, P * c:P * c + P], ident[0:k, 0:k])
                    mm.then_inc(xt_full, 1)
                    n += 1
            pe.wait_ge(xlo_done, 24)
            product(("c", 0), x_hi, x_lo, FULL)
            product(("kw", 0), x_hi, x_lo, FULL)
            for m in range(2):
                product(("qi", m), x_hi, x_lo, REAL)
            for j, (t0, w) in enumerate(FULL):
                b = open_tile(TILE_AT[("csum", 0), j])
                pe.wait_ge(csq_done, j + 1)
                pe.matmul(ps[:, b, 0:w], ones[:, :], c_sq[:, t0:t0 + w], start=True, stop=True).then_inc(lin_full, 1)
            b = open_tile(TILE_AT[("wtok", 0), 0])
            pe.wait_ge(kif_done, 3)
            for r in range(NB):
                mm = pe.transpose(ps[:, b, 8 * r:8 * r + 8], w_row[32:40, P * r:P * r + P], ident[32:40, 32:40])
            mm.then_inc(lin_full, 1)
            for m in range(4):
                product(("u", m), x_hi, x_lo, FULL)
                if m == 1:
                    pe.wait_ge(cn_done, 1)
                    for j, (t0, tiles, _) in enumerate(XGROUPS):
                        b = open_tile(TILE_AT[("ctok", 0), j])
                        for r in tiles:
                            mm = pe.transpose(ps[0:tile_rows(r), b, P * (r % 4):P * (r % 4) + P], c_sq[:, P * r:P * r + tile_rows(r)], ident[:, :])
                        mm.then_inc(lin_full, 1)
            pe.wait_ge(kilo_done, 1)
            pe.wait_ge(qilo_done, 4)
            for n, (blk, pc, h) in enumerate(UNITS):
                k0, nch, w = pieces(blk)[pc]
                r0 = 32 * (h % 4)
                if n >= 2:
                    pe.wait_ge(relu_done, n - 1)
                for ch in range(nch):
                    for i, (a, kk) in enumerate(((qi_hi, ki_hi), (qi_hi, ki_lo), (qi_lo, ki_hi))):
                        mm = pe.matmul(ps[:, 4 + 2 * (n % 2) + ch, 0:w], a[r0:r0 + 32, h // 4, P * blk:P * blk + P],
                                       kk[r0:r0 + 32, k0 + ch * w:k0 + ch * w + w], start=i == 0, stop=i == 2)
                mm.then_inc(pair_full, 1)
            p = PANEL_AT["poolw", 0]
            pe.wait_ge(wlo_done, p + 1)
            for g in range(4):
                pe.wait_ge(pooled_done, g + 1)
                for j, (t0, w) in enumerate(HALF):
                    b = open_tile(TILE_AT[("poolw", 0), 2 * g + j])
                    for i, (a, r) in enumerate(((w_hi, pool_hi), (w_hi, pool_lo), (w_lo, pool_hi))):
                        mm = pe.matmul(ps[:, b, 0:w], a[:, p % 2, P * g:P * g + P], r[:, g, t0:t0 + w], start=i == 0, stop=i == 2)
                    mm.then_inc(lin_full, 1)
            for m in range(KD):
                product(("q", m), x_hi, x_lo, REAL)
            pe.wait_ge(brlo_done, 8)
            for m in range(KD):
                product(("g0", m), x_hi, x_lo, REAL)
                product(("wa", m), br_hi, br_lo, HALF, 4)
            for m in range(4):
                product(("cc", m), x_hi, x_lo, FULL)
                product(("cu", m), x_hi, x_lo, FULL)
                product(("cb", m), x_hi, x_lo, REAL)
            for m in range(KD):
                product(("g2", m), x_hi, x_lo, REAL)
                if m == 0:
                    pe.wait_ge(brlo_done, 12)
                product(("wc", m), br_hi, br_lo, HALF, 4)
            for m in range(KD):
                product(("g1", m), x_hi, x_lo, REAL)

            pe.wait_ge(g1_done, 2 * KD)

            def logits(g):
                blk, hg = GROUPS[g]
                pe.wait_ge(qlo_done, blk + 1)
                base = LOGITS_TO[g - 1] if g else 0
                for h in range(4):
                    for pc, (k0, nch, w) in enumerate(pieces(blk)):
                        n = base + h * len(pieces(blk)) + pc
                        if n >= 2:
                            pe.wait_ge(masked, n - 1)
                        for ch in range(nch):
                            for i, (a, kk) in enumerate(((q_hi, c_hi), (q_hi, c_lo), (q_lo, c_hi))):
                                mm = pe.matmul(ps[:, 4 + 2 * (n % 2) + ch, 0:w], a[:, blk % 2, 4 * hg + h, :],
                                               kk[:, k0 + ch * w:k0 + ch * w + w], start=i == 0, stop=i == 2)
                        mm.then_inc(pair_full, 1)

            def values(g):
                blk, hg = GROUPS[g]
                base = CHUNKS_TO[g - 1] if g else 0
                nk = blk + 2
                pe.wait_ge(norm_done, 4 * (g + 1))

                def turn(r):
                    n = base + r
                    k = tile_rows(8) if r == nk - 1 else P
                    if n >= 2:
                        pe.wait_ge(ptlo_done, n - 1)
                    for h in range(4):
                        mm = pe.transpose(ps[0:k, n % 2, P * h:P * h + P], logit[:, g % 2, h, P * r:P * r + k], ident[:, :])
                    mm.then_inc(trans_full, 1)

                def weigh(r):
                    n = base + r
                    k = tile_rows(8) if r == nk - 1 else P
                    pe.wait_ge(ptlo_done, n + 1)
                    if r == 0 and g >= 2:
                        pe.wait_ge(olo_done, g - 1)
                    for i, (a, r_) in enumerate(((ck_hi, pt_hi), (ck_hi, pt_lo), (ck_lo, pt_hi))):
                        mm = pe.matmul(ps[:, 2 + g % 2, :], a[0:k, r, :], r_[0:k, n % 2, :],
                                       start=r == 0 and i == 0, stop=r == nk - 1 and i == 2)
                    mm.then_inc(pv_step, 1)

                turn(0)
                for r in range(nk):
                    if r + 1 < nk:
                        turn(r + 1)
                    weigh(r)

            logits(0)
            for g in range(len(GROUPS)):
                if g + 1 < len(GROUPS):
                    logits(g + 1)
                values(g)

            pe.wait_ge(olo_done, 16)
            pe.wait_ge(ptlo_done, CHUNKS_TO[-1])
            for m in range(KD):
                product(("wb", m), x_hi, x_lo, HALF)
            pe.wait_ge(xres_load, 16)
            for m in range(KD):
                def residual(j, b, m=m):
                    for r in range(4):
                        mm = pe.matmul(ps[:, b, P * r:P * r + P], x_res[:, 4 * j + r, P * m:P * m + P], ident[:, :],
                                       start=False, stop=r == 3)
                    return mm
                product(("wo", m), x_hi, x_lo, HALF, extra=residual, ready=mlo_done if m == 0 else None)

            def norm(i):
                pe.wait_ge(acca_done, 7 * i + 7)
                if i:
                    pe.wait_ge(accb_done, 7)
                    pe.wait_ge(upper_free, 8 + 16 * FC)
                for st in range(i + 1):
                    for b in range(NB):
                        mm = pe.matmul(ps[:, 4, 8 * st + b:8 * st + b + 1], n_acc[:, st, P * b:P * b + P], ones[:, 0:1], start=True, stop=True)
                mm.then_inc(stat_full, 1)
                for st in range(i + 1):
                    pe.wait_ge(diag_done, 8 * (i + st + 1))
                    for h, (t0, w) in enumerate(HALF):
                        mm = pe.matmul(ps[:, (4 + 2 * st if i else 6) + h, :], ones[:, :], (n_diag2 if st else n_diag)[:, t0:t0 + w], start=True, stop=True)
                    mm.then_inc(rs_full, 1)

            norm(0)

            def passes(ps_out, w_at, kd, rhs_hi, rhs_lo):
                for k in range(kd):
                    for i, (w, r) in enumerate(((w_hi, rhs_hi), (w_hi, rhs_lo), (w_lo, rhs_hi))):
                        mm = pe.matmul(ps_out, w_at(w, k), r(k), start=k == 0 and i == 0, stop=k == kd - 1 and i == 2)
                return mm

            def gate_and_up(it, par, first=False):
                for half in range(2):
                    off = half if first else 3 * par - 1 + half
                    sl = (PB + off) % 2
                    pe.wait_ge(wlo_done, panel_no(it, off) + 1)
                    for h, (t0, w) in enumerate(HALF):
                        if not first:
                            pe.wait_ge(af_done if half else silu_done, 4 * it + 2 * par + (h - 1))
                        for k in range(KD):
                            if first and half == 0 and h == 0:
                                pe.wait_ge(nlo_done, k + 1)
                            for i, (wt, r) in enumerate(((w_hi, x_hi), (w_hi, x_lo), (w_lo, x_hi))):
                                mm = pe.matmul(ps[:, 2 * half + h, :], wt[:, sl, P * k:P * k + P], r[:, k, t0:t0 + w],
                                               start=k == 0 and i == 0, stop=k == KD - 1 and i == 2)
                        mm.then_inc(lin_full, 1)

            def down(it, par, off):
                sl = (PB + off) % 2
                pe.wait_ge(wlo_done, panel_no(it, off) + 1)
                pe.wait_ge(alo_done, 2 * it + (par + 1))
                for n in range(16):
                    m, (t0, w) = n // 2, HALF[n % 2]
                    pe.wait_ge(upper_free, 32 * it + (16 * par + n + 5))
                    for i, (wt, r) in enumerate(((w_hi, a_hi), (w_hi, a_lo), (w_lo, a_hi))):
                        mm = pe.matmul(ps[:, 4 + n % 4, :], wt[:, sl, P * m:P * m + P], r[:, par, t0:t0 + w], start=i == 0, stop=i == 2)
                    mm.then_inc(lin_full, 1)

            pe.wait_ge(h_done, 2 * KD)
            gate_and_up(0, 0, first=True)
            with pe.Fori(0, (FC - 2) // 2) as it:
                for par in range(2):
                    gate_and_up(it, par + 1)
                    down(it, par, 3 * par + 4)
            it_last = (FC - 2) // 2
            gate_and_up(it_last, 1)
            down(it_last, 0, 4)
            down(it_last, 1, 3 * FC - 1 - 6 * it_last)
            norm(1)

            def upper(key):
                n = UP_AT[key]
                if n >= 4:
                    pe.wait_ge(*up_released(UPPER[n - 4]))
                return 4 + n % 4

            def linear(key, j, rhs_hi, rhs_lo, t0, n):
                p = AT2[key]
                at = LIN_AT[key, j]
                pe.wait_ge(wlo_done, p + 1)
                if at >= 3:
                    pe.wait_ge(*released2(*LINEAR2[at - 3]))
                for k in range(KD):
                    if key == ("av", 0) and j == 0:
                        pe.wait_ge(nlo_done, KD + k + 1)
                    for i, (wt, r) in enumerate(((w_hi, rhs_hi), (w_hi, rhs_lo), (w_lo, rhs_hi))):
                        mm = pe.matmul(ps[:, at % 3, 0:n], wt[:, p % 2, P * k:P * k + P], r[:, k, t0:t0 + n],
                                       start=k == 0 and i == 0, stop=k == KD - 1 and i == 2)
                mm.then_inc(lin_full, 1)

            def panel2(key):
                for j, (t0, w) in enumerate(HALF):
                    linear(key, j, x_hi, x_lo, t0, w)

            pe.wait_ge(x2_done, KD)
            for n in range(16):
                r, h = n // 2, n % 2
                b = upper(("x2", n))
                for c in range(4):
                    mm = pe.transpose(ps[:, b, P * c:P * c + P], mix[:, 4 * h + c, P * r:P * r + P], ident[:, :])
                mm.then_inc(up_full, 1)
            pe.wait_ge(ms_scaled, 2)
            for n in range(4):
                b = upper(("mem", n))
                for c in range(2):
                    for r in range(2):
                        mm = pe.transpose(ps[:, b, MEM * c + P * r:MEM * c + P * r + P], mem_tok[:, r, P * (2 * n + c):P * (2 * n + c) + P], ident[:, :])
                mm.then_inc(up_full, 1)
            b = upper(("wsp", 0))
            pe.wait_ge(wsp_done, 1)
            for g in range(4):
                mm = pe.transpose(ps[:, b, P * g:P * g + P], w_sp[:, g, :], ident[:, :])
            mm.then_inc(up_full, 1)
            b = upper(("rb", 0))
            pe.wait_ge(c2_load, 7 * 16)
            pe.matmul(ps[:, b, 0:SWA_SPAN], relb[0:64, :], onehot[:, :], start=True, stop=True).then_inc(up_full, 1)
            for m in range(4):
                panel2(("av", m))
            def turn_values(blocks):
                for n in blocks:
                    b = upper(("av", n))
                    for c in range(4):
                        mm = pe.transpose(ps[:, b, P * c:P * c + P], av_s[:, c, P * n:P * n + P], ident[:, :])
                    mm.then_inc(up_full, 1)

            panel2(("au", 0))
            pe.wait_ge(av_done, AV_0 + 8)
            turn_values(range(4))
            panel2(("au", 1))
            turn_values(range(4, 6))
            panel2(("au", 2))
            turn_values(range(6, NB))
            panel2(("au", 3))
            pe.wait_ge(rb_load, 16)
            for n in range(2):
                b = upper(("flip", n))
                pe.matmul(ps[:, b, :], anti[:, :], btoe[:, 2 * n:2 * n + 2, :], start=True, stop=True).then_inc(up_full, 1)
            pe.wait_ge(memlo_done, MEMLO_0 + KD)
            for m in range(2):
                linear(("mk", m), 0, memt_hi, memt_lo, 0, MEM)
            for m in range(2):
                linear(("mv", m), 0, memt_hi, memt_lo, 0, MEM)
            b = upper(("mvt", 0))
            pe.wait_ge(mvf_done, MVF_0 + 2)
            for r in range(2):
                for c in range(2):
                    mm = pe.transpose(ps[:, b, MEM * r + P * c:MEM * r + P * c + P], mv_f[:, c, P * r:P * r + P], ident[:, :])
            mm.then_inc(up_full, 1)
            pe.wait_ge(vlnlo_done, VLNLO_0 + NB)
            pe.wait_ge(wtlo_done, WTLO_0 + 1)
            for n in range(8):
                g, h = n // 2, n % 2
                b = upper(("sp", n))
                for c in range(4):
                    blk = 4 * h + c
                    for i, (a, w) in enumerate(((vln_hi, wt_hi), (vln_lo, wt_hi), (vln_hi, wt_lo))):
                        mm = pe.matmul(ps[:, b, P * c:P * c + P], a[:, blk, P * g:P * g + P], w[:, g, :], start=i == 0, stop=i == 2)
                mm.then_inc(up_full, 1)
            panel2(("sk", 0))
            panel2(("sv", 0))
            pe.wait_ge(svf_done, SVF_0 + 2)
            for n in range(2):
                b = upper(("svt", n))
                for c in range(4):
                    mm = pe.transpose(ps[:, b, P * c:P * c + P], sv_f[:, BANK * n + P * c:BANK * n + P * c + P], ident[:, :])
                mm.then_inc(up_full, 1)
            for kind in ("sq", "mq"):
                for m in range(2):
                    panel2((kind, m))
            for m in range(4, 8):
                panel2(("z", m))

            pe.wait_ge(sqlo_done, SQLO_0 + 4)
            pe.wait_ge(mqlo_done, MQLO_0 + 4)
            pe.wait_ge(kdlo_done, KDLO_0 + 1)
            pe.wait_ge(mklo_done, MKLO_0 + 2)
            pe.wait_ge(svlo_done, SVLO_0 + 4)
            pe.wait_ge(sp_sum, SPSUM_0 + 8)
            pe.wait_ge(mvtlo_done, MVTLO_0 + 1)

            def logits2(n):
                blk, kind = UNITS2[n]
                if n >= 1:
                    pe.wait_ge(e2_done, E2_0 + 4 * n)
                q_parts, k_parts = ((mq_hi, mq_lo), (mk_hi, mk_lo)) if kind else ((sq_hi, sq_lo), (kd_hi, kd_lo))
                a, z = (0, MEM) if kind else (P * max(blk - 1, 0), P * blk + P)
                for c, (i, (x, y)), u in [(c, e, u) for c in range(2) for e in enumerate(((0, 0), (0, 1), (1, 0))) for u in range(2)]:
                        r0, h = DH * u, 2 * c + u
                        o = 2 * P * c + 2 * P - (z - a)
                        mm = pe.matmul(ps[:, 4 + h % 2, o:o + z - a], q_parts[x][r0:r0 + DH, c, P * blk:P * blk + P],
                                       k_parts[y][r0:r0 + DH, c, a:z], start=i == 0, stop=i == 2)
                mm.then_inc(lg_full, 1)

            def turn2(n):
                pe.wait_ge(pn_done, PN_0 + 4 * n + 4)
                for kc in key_chunks(n):
                    if n >= 1 and (n - 1, kc) in TURN_AT:
                        pe.wait_ge(p2lo_done, P2LO_0 + TURN_AT[n - 1, kc] + 1)
                    for h in range(4):
                        mm = pe.transpose(ps[:, 6 + kc, P * h:P * h + P], p_s[:, n % 2, 2 * (h % 2) + h // 2, P * kc:P * kc + P], ident[:, :])
                    mm.then_inc(pt_full, 1)

            def values2(n):
                blk, kind = UNITS2[n]
                if n >= 1:
                    pe.wait_ge(pvg_done, 2 * n)
                pe.wait_ge(p2lo_done, P2LO_0 + TURN_AT[n, 1] + 1)
                for c in range(2):
                    chunks = key_chunks(n)
                    for kc in chunks:
                        if kind:
                            v_hi, v_lo = mv_hi[:, kc, P * c:P * c + P], mv_lo[:, kc, P * c:P * c + P]
                        else:
                            v_hi, v_lo = vd_hi[:, blk - 1 + kc, c, :], vd_lo[:, blk - 1 + kc, c, :]
                        for i, (a, r) in enumerate(((v_hi, p2_hi), (v_hi, p2_lo), (v_lo, p2_hi))):
                            mm = pe.matmul(ps[:, 3, 2 * P * c:2 * P * c + 2 * P], a, r[:, kc, 2 * P * c:2 * P * c + 2 * P],
                                           start=kc == chunks[0] and i == 0, stop=kc == chunks[-1] and i == 2)
                mm.then_inc(pv_full, 1)

            logits2(0)
            for n in range(len(UNITS2)):
                if n + 1 < len(UNITS2):
                    logits2(n + 1)
                turn2(n)
                linear(("z", n // 4), n % 4, x_hi, x_lo, 2 * P * (n % 4), 2 * P)
                values2(n)

            for half in range(2):
                for k in range(KD):
                    p = AT2["wout", KD * half + k]
                    pe.wait_ge(wlo_done, p + 1)
                    if half == 0:
                        pe.wait_ge(ylob_done if k % 2 else yloa_done, (YLOB_0 if k % 2 else YLOA_0) + k // 2 + 1)
                    for b in range(NB):
                        if half and k == 0:
                            pe.wait_ge(wy_done, WY_0 + b + 1)
                        for i, (y, w) in enumerate(((x_hi, w_hi), (x_lo, w_hi), (x_hi, w_lo))):
                            mm = pe.matmul(ps[:, b, :], y[:, k, P * b:P * b + P], w[:, p % 2, 0:BANK],
                                           start=k == 0 and i == 0, stop=k == KD - 1 and i == 2)
                        if k == KD - 1 or b == NB - 1:
                            mm.then_inc(lin_full, 1)

        @block.scalar
        def _(act):
            def split(p):
                if p >= PB2 + len(PANELS2):
                    return
                act.wait_ge(raw_load[p % 2], 16 * (p // 2 + 1))
                if p >= 2:
                    act.wait_ge(lin_full, through(p - 2))
                act.copy(w_hi[:, p % 2, 0:width(p)], w_raw[:, p % 2, 0:width(p)]).then_inc(whi_done, 1)

            def split_behind(key):
                split(PANEL_AT[key] + 2)

            def tile(key, j):
                n = TILE_AT[key, j]
                act.wait_ge(lin_full, n + 1)
                return n % 4

            for gi, (t0, tiles, w) in enumerate(XGROUPS):
                for r in tiles:
                    k = tile_rows(r)
                    act.wait_ge(x_load[r], 32 if r == 0 else 16)
                    if r >= 2:
                        act.wait_ge(sq_done, r - 1)
                    act.activation(junk[0:k, r % 2, :], x_tok[0:k, r, :], ACT.Square, accum_out=ss[0:k, r:r + 1]).then_inc(sq_done, 1)
                k = tile_rows(tiles[0])
                act.wait_ge(inv_done, gi + 1)
                act.activation(rstd[0:k, tiles[0]:tiles[-1] + 1], rstd[0:k, tiles[0]:tiles[-1] + 1], ACT.Sqrt).then_inc(rt_done, 1)
            split(0)
            split(1)
            act.wait_ge(vec_full, 1)
            act.copy(vec[:, :], ps[:, 7, 0:rows]).then_inc(vec_ready, 1)
            act.wait_ge(vec_ready, 1)
            n = 0
            for t0, tiles, w in XGROUPS:
                for c in range(KD):
                    act.wait_ge(xt_full, n + 1)
                    act.activation(x_hi[:, c, t0:t0 + w], ps[:, n % 4, 0:w], ACT.Copy, scale=v("norm1_g", c)).then_inc(xhi_done, 1)
                    n += 1

            for j, (t0, w) in enumerate(FULL):
                b = tile(("c", 0), j)
                act.activation(c_sq[:, t0:t0 + w], ps[:, b, 0:w], ACT.Square).then_inc(csq_done, 1)
                act.copy(c_raw[:, t0:t0 + w], ps[:, b, 0:w]).then_inc(craw_done, 1)
            split_behind(("c", 0))
            for j, (t0, w) in enumerate(FULL):
                b = tile(("kw", 0), j)
                real = max(t0, META)
                act.copy(w_row[32:40, real - META:t0 + w - META], ps[32:40, b, real - t0:w])
                act.copy(ki_f[0:32, t0:t0 + w], ps[0:32, b, 0:w]).then_inc(kif_done, 1)
            split_behind(("kw", 0))
            for m in range(2):
                for j, (t0, w) in enumerate(HALF):
                    b = tile(("qi", m), j)
                    act.copy(qi_hi[:, m, t0:t0 + w], ps[:, b, 0:w]).then_inc(qihi_done, 1)
                split_behind(("qi", m))
            act.wait_ge(ki_copies, 48)
            act.copy(ki_hi[:, :], ki_f[:, :]).then_inc(kihi_done, 1)
            b = tile(("wtok", 0), 0)
            act.mul(w_tok[:, :, :], ps[:, b, 0:64].rearrange("p (r h) -> p r h", h=8), IDX_SCALE).then_inc(wtok_done, 1)
            for m in range(4):
                if m >= 2:
                    act.wait_ge(pool_sub, m - 1)
                for j, (t0, w) in enumerate(FULL):
                    b = tile(("u", m), j)
                    act.copy(u_s[:, m % 2, t0:t0 + w], ps[:, b, 0:w]).then_inc(u_done, 1)
                split_behind(("u", m))
                if m == 0:
                    act.wait_ge(cinv_done, 1)
                    act.activation(c_rs[:, :], c_rs[:, :], ACT.Sqrt).then_inc(crt_done, 1)
                    act.wait_ge(cn_done, 1)
                    act.copy(c_hi[:, :], c_sq[:, :]).then_inc(chi_done, 1)
                if m == 1:
                    for j, (t0, tiles, w) in enumerate(XGROUPS):
                        b = tile(("ctok", 0), j)
                        k = tile_rows(tiles[0])
                        act.copy(ck_hi[0:k, tiles[0]:tiles[-1] + 1, :],
                                 ps[0:k, b, 0:P * len(tiles)].rearrange("p (r d) -> p r d", d=P)).then_inc(ckhi_done, 1)
            for n, (blk, pc, h) in enumerate(UNITS):
                k0, nch, w = pieces(blk)[pc]
                act.wait_ge(pair_full, n + 1)
                if n >= 2:
                    act.wait_ge(score_acc, n - 1)
                act.activation(wide(relu_s[:, n % 2, 0:nch * w], nch), pair(n, nch, w), ACT.Relu).then_inc(relu_done, 1)
            act.wait_ge(score_acc, len(UNITS))
            act.wait_ge(pooled_done, 4)
            for g in range(4):
                for j, (t0, w) in enumerate(HALF):
                    n = 2 * g + j
                    b = tile(("poolw", 0), n)
                    if n >= 2:
                        act.wait_ge(brlo_done, n - 1)
                    act.activation(mix_s[:, n % 2, :], ps[:, b, :], ACT.Copy, scale=v("pool_scale", g)).then_inc(mixf_done, 1)
                    act.wait_ge(mixf_done, n + 1)
                    act.copy(br_hi[:, g, t0:t0 + w], mix_s[:, n % 2, :]).then_inc(brhi_done, 1)
            split_behind(("poolw", 0))
            act.wait_ge(brlo_done, 8)

            def store(kind, m, func, done, stores, dram, bias):
                if m >= 2:
                    act.wait_ge(stores[m % 2], 16 * (m // 2))
                for j, (t0, w) in enumerate(HALF):
                    b = tile((kind, m), j)
                    act.activation(stage[:, m % 2, t0:t0 + w], ps[:, b, :], func, bias=bias).then_inc(done, 1)
                split_behind((kind, m))
                act.wait_ge(done, 2 * m + 2)
                act.dma_start(dram[m], stage[:, m % 2, :]).then_inc(stores[m % 2], 16)

            for m in range(KD):
                store("q", m, ACT.Copy, q_copied, q_store, q_scratch, 0.0)
            act.wait_ge(q_store[0], 64)
            act.wait_ge(q_store[1], 64)

            def branch(g, w, i, base):
                for m in range(KD):
                    if base + m >= 2:
                        act.wait_ge(gate_used, base + m - 1)
                    for j, (t0, n) in enumerate(HALF):
                        b = tile((g, m), j)
                        act.activation(stage[:, m % 2, t0:t0 + n], ps[:, b, :], ACT.Sigmoid,
                                       bias=v("b_gate", KD * i + m)).then_inc(gate_done, 1)
                    split_behind((g, m))
                    for j, (t0, n) in enumerate(HALF):
                        b = tile((w, m), j)
                        act.copy(y_s[:, m % 2, t0:t0 + n], ps[:, b, :]).then_inc(y_done, 1)
                    split_behind((w, m))

            branch("g0", "wa", 0, 0)
            act.wait_ge(gate_used, KD)
            for m in range(4):
                if m >= 1:
                    act.wait_ge(brlo_done, 8 + m)
                for slot, kind, chunks in ((0, "cc", FULL), (1, "cu", FULL)):
                    for j, (t0, w) in enumerate(chunks):
                        b = tile((kind, m), j)
                        act.copy(cv[:, slot, t0:t0 + w], ps[:, b, 0:w]).then_inc(cv_in, 1)
                    split_behind((kind, m))
                act.wait_ge(cv_v, m + 1)
                for tap, slot in ((0, 3), (1, 4), (2, 0)):
                    o = META - 2 + tap
                    act.activation(cv[:, slot, 0:S], cv[:, 2, o:o + S], ACT.Copy, scale=v("conv_w", 4 * tap + m)).then_inc(cv_tap, 1)
                for j, (t0, w) in enumerate(HALF):
                    b = tile(("cb", m), j)
                    act.copy(cv[:, 5, t0:t0 + w], ps[:, b, 0:w]).then_inc(cv_in, 1)
                split_behind(("cb", m))
                act.wait_ge(cv_sum, m + 1)
                act.copy(br_hi[:, m, :], cv[:, 1, 0:S]).then_inc(brhi_done, 1)
            act.wait_ge(brlo_done, 12)
            branch("g2", "wc", 2, KD)
            act.wait_ge(gate_used, 2 * KD)
            for m in range(KD):
                store("g1", m, ACT.Sigmoid, g1_done, g1_store, g1_scratch, v("b_gate", KD + m))

            def queries(b):
                act.wait_ge(q_load, 16 * (b + 1))
                if b >= 2:
                    act.wait_ge(pair_full, len(UNITS) + LOGITS_TO[2 * (b - 2) + 1])
                act.copy(q_hi[:, b % 2], q_f[:, :, :]).then_inc(qhi_done, 1)

            def exps(g, heads):
                nk = block_keys(GROUPS[g][0])
                act.wait_ge(nm_done, g + 1)
                for h in heads:
                    act.activation(logit[:, g % 2, h, 0:nk], logit[:, g % 2, h, 0:nk], ACT.Exp, bias=neg_max[:, g % 2, h:h + 1],
                                   scale=ATTN_SCALE, accum_out=row_sum[:, g % 2, h:h + 1]).then_inc(exp_done, 1)

            queries(0)
            queries(1)
            exps(0, range(4))
            for g, (blk, hg) in enumerate(GROUPS):
                for r in range(blk + 2):
                    n = (CHUNKS_TO[g - 1] if g else 0) + r
                    k = META if r == blk + 1 else P
                    act.wait_ge(trans_full, n + 1)
                    if n >= 2:
                        act.wait_ge(pv_step, n - 1)
                    act.copy(pt_hi[0:k, n % 2, :], ps[0:k, n % 2, :]).then_inc(pthi_done, 1)
                    if g + 1 < len(GROUPS) and 1 <= r <= 4:
                        exps(g + 1, [r - 1])
                if g + 1 < len(GROUPS):
                    exps(g + 1, range(blk + 1, 4))
                act.wait_ge(pv_step, CHUNKS_TO[g])
                act.copy(x_hi[:, 4 * hg:4 * hg + 4, P * blk:P * blk + P],
                         ps[:, 2 + g % 2, :].rearrange("p (h t) -> p h t", h=4)).then_inc(ohi_done, 1)
                if hg == 0 and blk + 2 < NB:
                    queries(blk + 2)
            for m in range(KD - 2):
                split_behind(("wb", m))
            for m in range(KD):
                act.wait_ge(m_acc, 2 * (m + 1))
                if m == 0:
                    act.wait_ge(lin_full, TILE_AT[("wb", KD - 1), 1] + 1)
                act.copy(x_hi[:, m, 0:S], mix[:, m, :]).then_inc(mhi_done, 1)
                if m in (1, 2):
                    split(PANEL_AT["wo", m - 1])
            act.wait_ge(mlo_done, KD)
            def squares(i, m):
                if m >= 2:
                    act.wait_ge(acca_done, 7 * i + max(m - 2, 1))
                act.activation(n_sq[:, m % 2, 0, :], mix[:, m, :], ACT.Square).then_inc(sqa_done, 1)
                if i:
                    if m >= 2:
                        act.wait_ge(accb_done, max(m - 2, 1))
                    act.activation(n_sq[:, m % 2, 1, :], mix[:, m, :], ACT.Square, scale=v("final_g", m)).then_inc(sqb_done, 1)

            def norm(i):
                act.wait_ge(nst_step, 5 if i else 2)
                if i:
                    act.activation(nst[:, 4:6, :], nst[:, 1:4:2, :], ACT.Sqrt).then_inc(nrt_done, 1)
                else:
                    act.activation(nst[:, 4, :], nst[:, 1, :], ACT.Sqrt).then_inc(nrt_done, 1)
                for m in range(KD):
                    act.wait_ge(xn_done if i else upper_free, (XN_0 if i else 0) + m + 1)
                    act.copy(x_hi[:, m, 0:S], n_st[:, m % 2, :]).then_inc(nhi_done, 1)

            for m in range(KD):
                for j, (t0, w) in enumerate(HALF):
                    b = tile(("wo", m), j)
                    act.copy(mix[:, m, t0:t0 + w], ps[:, b, :]).then_inc(h_done, 1)
                split_behind(("wo", m))
                act.wait_ge(h_done, 2 * m + 2)
                squares(0, m)
            norm(0)

            def split_mlp(it, off, ticks):
                sl = (PB + off) % 2
                act.wait_ge(raw_load[sl], 16 * loads_of(it, off))
                act.wait_ge(lin_full, ticks)
                act.copy(w_hi[:, sl, :], w_raw[:, sl, :]).then_inc(whi_done, 1)

            def activations(it, par, first=False):
                at = L0 if first else gu_at(it, par)
                off = 0 if first else 3 * par - 1
                for h, (t0, w) in enumerate(HALF):
                    act.wait_ge(lin_full, at + (h + 1))
                    if not first:
                        act.wait_ge(af_done, 4 * it + 2 * par + (h - 1))
                    act.activation(silu_s[:, t0:t0 + w], ps[:, h, :], ACT.Silu).then_inc(silu_done, 1)
                split_mlp(it, off + 2, at + 2)
                split_mlp(it, off + 3, at + 4)
                act.wait_ge(af_done, 4 * it + (2 * par + 2))
                act.copy(a_hi[:, par % 2, :], a_f[:, :]).then_inc(ahi_done, 1)

            activations(0, 0, first=True)
            with act.Fori(0, (FC - 2) // 2) as it:
                for par in range(2):
                    activations(it, par + 1)
                    split_mlp(it, 3 * par + 6, gu_at(it, par + 1) + 20)
            it_last = (FC - 2) // 2
            activations(it_last, 1)
            act.wait_ge(mem_load, 16)
            for r in range(2):
                act.activation(silu_s[:, :], mem_tok[:, r, :], ACT.Square, accum_out=mem_ss[:, r:r + 1]).then_inc(msq_done, 1)
                act.wait_ge(msq_done, r + 1)
            split_mlp(it_last, 6, L2 - 16)
            act.wait_ge(mst_step, 2)
            act.activation(mem_ss[:, :], mem_ss[:, :], ACT.Sqrt).then_inc(mrt_done, 1)
            for m in range(KD):
                act.wait_ge(upper_free, 8 + 16 * (FC - 1) + 2 * m + 2)
                squares(1, m)
            split_mlp(it_last, 7, L2)
            norm(1)

            def tile2(key, j):
                act.wait_ge(lin_full, TICK2[key, j] + 1)
                return LIN_AT[key, j] % 3

            def up(key):
                n = UP_AT[key]
                act.wait_ge(up_full, UP_0 + n + 1)
                return 4 + n % 4

            def behind2(key):
                split(AT2[key] + 2)

            for n in range(16):
                r, h = n // 2, n % 2
                b = up(("x2", n))
                if r >= 2 and h == 0:
                    act.wait_ge(x2_store[r % 2], 16 * (r // 2))
                act.copy(x2_s[:, r % 2, BANK * h:BANK * h + BANK], ps[:, b, :]).then_inc(x2_copied, 1)
                if h:
                    act.wait_ge(x2_copied, X2_0 + n + 1)
                    act.dma_start(x2_scratch[P * r:P * r + P, :], x2_s[:, r % 2, :]).then_inc(x2_store[r % 2], 16)
            for n in range(4):
                b = up(("mem", n))
                for c in range(2):
                    act.activation(memt_hi[:, 2 * n + c, :], ps[:, b, MEM * c:MEM * c + MEM], ACT.Copy, scale=v("mem_norm_g_2", 2 * n + c)).then_inc(memhi_done, 1)
            b = up(("wsp", 0))
            act.wait_ge(nlo_done, 2 * KD)
            act.copy(wt_hi[:, :, :], ps[:, b, :].rearrange("p (g t) -> p g t", g=4)).then_inc(wthi_done, 1)
            b = up(("rb", 0))
            act.copy(rb_s[:, :], ps[0:4, b, 0:SWA_SPAN]).then_inc(rb_done, 1)
            act.wait_ge(rb_done, RB_0 + 1)
            act.dma_start(rb_scratch, rb_s[:, :]).then_inc(rb_store, 16)
            for m in range(4):
                for j, (t0, w) in enumerate(HALF):
                    b = tile2(("av", m), j)
                    act.activation(av_s[:, m, t0:t0 + w], ps[:, b, :], ACT.Gelu_apprx_tanh).then_inc(av_done, 1)
                behind2(("av", m))
            act.wait_ge(c2_load, 7 * 16)
            act.copy(sink[:, :].rearrange("p (u c) -> p u c", u=2), sink_n[:, :].rearrange("p (c u) -> p u c", u=2)).then_inc(sink_done, 1)
            act.wait_ge(rb_store, 16)
            act.dma_start(btoe[:, :, :], bass.AP(tensor=rb_scratch.tensor, offset=0, ap=[[1, P], [SWA_SPAN, 4], [1, 2 * P]])).then_inc(rb_load, 16)

            def ln_root(n):
                act.wait_ge(ln_step, 6 * n + 6)
                act.activation(vrs[:, n % 2, :], vrs[:, n % 2, :], ACT.Sqrt).then_inc(lnrt_done, 1)

            act.wait_ge(x2_store[0], 64)
            act.wait_ge(x2_store[1], 64)
            def u_panel(m):
                for j, (t0, w) in enumerate(HALF):
                    b = tile2(("au", m), j)
                    act.activation(yz[:, m, t0:t0 + w], ps[:, b, :], ACT.Gelu_apprx_tanh).then_inc(au_done, 1)
                behind2(("au", m))

            u_panel(0)
            ln_root(0)
            for n in range(NB):
                if n in (3, 5, 7):
                    u_panel((n - 1) // 2)
                if n + 1 < NB:
                    ln_root(n + 1)
                act.wait_ge(vn_done, VN_0 + 2 * n + 2)
                act.copy(vln_hi[:, n, :], vn_s[:, n % 2, :]).then_inc(vlnhi_done, 1)
            for n in range(2):
                b = up(("flip", n))
                act.copy(bias[:, n:n + 3:2, :], ps[:, b, :].rearrange("p (h k) -> p h k", h=2)).then_inc(bias_done, 1)
            for m in range(2):
                b = tile2(("mk", m), 0)
                act.copy(mk_hi[:, m, :], ps[:, b, 0:MEM]).then_inc(mkhi_done, 1)
                behind2(("mk", m))
            for m in range(2):
                b = tile2(("mv", m), 0)
                act.copy(mv_f[:, m, :], ps[:, b, 0:MEM]).then_inc(mvf_done, 1)
                behind2(("mv", m))
            b = up(("mvt", 0))
            act.copy(mv_hi[:, :, :], ps[:, b, :].rearrange("p (r d) -> p r d", r=2)).then_inc(mvthi_done, 1)
            act.wait_ge(sp_done, SP_0 + 8)
            for j, (t0, w) in enumerate(HALF):
                b = tile2(("sk", 0), j)
                for c in range(2):
                    act.copy(kd_f[DH * c:DH * c + DH, c, t0:t0 + w], ps[DH * c:DH * c + DH, b, :]).then_inc(skf_done, 1)
            behind2(("sk", 0))
            for j, (t0, w) in enumerate(HALF):
                b = tile2(("sv", 0), j)
                act.copy(sv_f[:, t0:t0 + w], ps[:, b, :]).then_inc(svf_done, 1)
            behind2(("sv", 0))
            for n in range(2):
                b = up(("svt", n))
                for u in range(2):
                    act.copy(vd_hi[:, 4 * n:4 * n + 4, :, DH * u:DH * u + DH],
                             ps[:, b, :].rearrange("p (b c d) -> p b c d", b=4, c=2)).then_inc(svhi_done, 1)
            for kind, hi, done in (("sq", sq_hi, sqhi_done), ("mq", mq_hi, mqhi_done)):
                for m in range(2):
                    for j, (t0, w) in enumerate(HALF):
                        b = tile2((kind, m), j)
                        act.copy(hi[:, m, t0:t0 + w], ps[:, b, :]).then_inc(done, 1)
                    behind2((kind, m))
            act.wait_ge(kd_copies, 32)
            act.copy(kd_hi[:, :, :], kd_f[:, :, :]).then_inc(kdhi_done, 1)
            act.wait_ge(kdlo_done, KDLO_0 + 1)
            act.wait_ge(svlo_done, SVLO_0 + 4)
            for m in range(4, 8):
                for j, (t0, w) in enumerate(HALF):
                    b = tile2(("z", m), j)
                    act.activation(yz[:, m, t0:t0 + w], ps[:, b, :], ACT.Silu).then_inc(zs_done, 1)
                behind2(("z", m))

            def exps2(n):
                blk, kind = UNITS2[n]
                k0 = P if n == 0 else 0
                act.wait_ge(nm2_done, NM2_0 + n + 1)
                if n >= 2 and kind:
                    act.wait_ge(pt_full, TURN_AT[n - 2, 1] + 1)
                for h in range(4):
                    src = ps[:, 4 + h // 2, 2 * P * (h % 2):2 * P * (h % 2) + 2 * P] if kind else p_s[:, n % 2, h, k0:2 * P]
                    act.activation(p_s[:, n % 2, h, k0:2 * P], src, ACT.Exp, bias=nm2[:, n % 2, h:h + 1], scale=DH ** -0.5 if kind else 1.0,
                                   accum_out=rs2[:, n % 2, h:h + 1]).then_inc(e2_done, 1)
                if not kind:
                    act.activation(se2[:, n % 2, :], se2[:, n % 2, :], ACT.Exp).then_inc(b_done, 1)

            exps2(0)
            for n in range(len(UNITS2)):
                for kc in key_chunks(n):
                    act.wait_ge(pt_full, TURN_AT[n, kc] + 1)
                    if n >= 1:
                        act.wait_ge(pv_full, PV_0 + n)
                    act.copy(p2_hi[:, kc, :], ps[:, 6 + kc, :]).then_inc(p2hi_done, 1)
                if n + 1 < len(UNITS2):
                    exps2(n + 1)
                m, j = n // 4, n % 4
                b = tile2(("z", m), j)
                if n >= 2:
                    act.wait_ge(zt_done, n - 1)
                act.activation(z_s[:, 2 * P * (n % 2):2 * P * (n % 2) + 2 * P], ps[:, b, 0:2 * P], ACT.Silu).then_inc(zsilu_done, 1)
                if j == 3:
                    behind2(("z", m))
            act.wait_ge(zt_done, len(UNITS2))
            for m in range(KD):
                if m == 4:
                    act.wait_ge(pvg_done, 2 * len(UNITS2))
                act.copy(x_hi[:, m, 0:S], yz[:, m, :]).then_inc(yhi_done, 1)
            for n in range(KD):
                behind2(("wout", n))
            for b in range(NB):
                act.wait_ge(lin_full, TICK2[("wout", KD - 1), b] + 1)
                act.copy(wy[:, b, :], ps[:, b, :]).then_inc(wy_done, 1)
                act.wait_ge(wy_done, WY_0 + b + 1)
                if b >= 2:
                    act.wait_ge(wysq_done, WYSQ_0 + b - 1)
                act.activation(sq_junk[:, b % 2, :], wy[:, b, :], ACT.Square, accum_out=osum[:, 0, b:b + 1]).then_inc(wysq_done, 1)
            for n in range(KD, 2 * KD):
                behind2(("wout", n))
            for b in range(NB):
                act.wait_ge(lin_full, TICK2[("wout", 2 * KD - 1), b] + 1)
                if b < 2:
                    act.wait_ge(wysq_done, WYSQ_0 + NB - 1 + b)
                else:
                    act.wait_ge(ysq_done, YSQ_0 + b - 1)
                act.activation(sq_junk[:, b % 2, :], ps[:, b, :], ACT.Square, accum_out=osum[:, 1, b:b + 1]).then_inc(ysq_done, 1)
                if b % 4 == 3:
                    act.wait_ge(os_step, 3 * (b // 4) + 3)
                    act.activation(osum[:, 2, b - 3:b + 1], osum[:, 2, b - 3:b + 1], ACT.Sqrt).then_inc(osrt_done, 1)

        @block.vector
        def _(dve):
            def bank(key, j):
                return TILE_AT[key, j] % 4

            dve.wait_ge(rb_const, 2)
            dve.memset(relb[32:33, :], NEG).then_inc(rb_const, 1)
            for gi, (t0, tiles, w) in enumerate(XGROUPS):
                k = tile_rows(tiles[0])
                a, z = tiles[0], tiles[-1] + 1
                dve.wait_ge(sq_done, z)
                dve.tensor_scalar(ss[0:k, a:z], ss[0:k, a:z], 1.0 / D, EPS, ALU.mult, ALU.add).then_inc(ms_done, 1)
                dve.wait_ge(ms_done, gi + 1)
                dve.reciprocal(rstd[0:k, a:z], ss[0:k, a:z]).then_inc(inv_done, 1)
                dve.wait_ge(rt_done, gi + 1)
                for r in tiles:
                    dve.tensor_scalar(x_tok[0:k, r, :], x_tok[0:k, r, :], rstd[0:k, r:r + 1], None, ALU.mult).then_inc(xs_done, 1)
            n = 0
            dve.wait_ge(vec_ready, 1)
            for t0, tiles, w in XGROUPS:
                for c in range(KD):
                    dve.wait_ge(xhi_done, n + 1)
                    dve.scalar_tensor_tensor(out=x_lo[:, c, t0:t0 + w], in0=ps[:, n % 4, 0:w], scalar=v("norm1_g", c),
                                             in1=x_hi[:, c, t0:t0 + w], op0=ALU.mult, op1=ALU.subtract).then_inc(xlo_done, 1)
                    n += 1
            for m in range(2):
                for j, (t0, w) in enumerate(HALF):
                    dve.wait_ge(qihi_done, 2 * m + j + 1)
                    dve.tensor_tensor(qi_lo[:, m, t0:t0 + w], ps[:, bank(("qi", m), j), :], qi_hi[:, m, t0:t0 + w],
                                      ALU.subtract).then_inc(qilo_done, 1)
            dve.wait_ge(kihi_done, 1)
            dve.tensor_tensor(ki_lo[:, :], ki_f[:, :], ki_hi[:, :], ALU.subtract).then_inc(kilo_done, 1)
            for j, (t0, w) in enumerate(FULL):
                dve.wait_ge(lin_full, TILE_AT[("csum", 0), j] + 1)
                dve.tensor_scalar(c_rs[:, t0:t0 + w], ps[:, bank(("csum", 0), j), 0:w], 1.0 / P, EPS, ALU.mult, ALU.add).then_inc(cms_done, 1)
            dve.wait_ge(cms_done, 3)
            dve.reciprocal(c_rs[:, :], c_rs[:, :]).then_inc(cinv_done, 1)
            dve.wait_ge(crt_done, 1)
            dve.wait_ge(craw_done, 3)
            dve.scalar_tensor_tensor(out=c_sq[:, :], in0=c_raw[:, :], scalar=v("kv_norm_g", 0), in1=c_rs[:, :],
                                     op0=ALU.mult, op1=ALU.mult).then_inc(cn_done, 1)
            dve.wait_ge(chi_done, 1)
            dve.tensor_tensor(c_lo[:, :], c_sq[:, :], c_hi[:, :], ALU.subtract).then_inc(clo_done, 1)
            for j, (t0, tiles, w) in enumerate(XGROUPS):
                k = tile_rows(tiles[0])
                dve.wait_ge(ckhi_done, j + 1)
                dve.tensor_tensor(ck_lo[0:k, tiles[0]:tiles[-1] + 1, :],
                                  ps[0:k, bank(("ctok", 0), j), 0:P * len(tiles)].rearrange("p (r d) -> p r d", d=P),
                                  ck_hi[0:k, tiles[0]:tiles[-1] + 1, :], ALU.subtract).then_inc(cklo_done, 1)
            dve.wait_ge(wtok_done, 1)
            for n, (blk, pc, h) in enumerate(UNITS):
                k0, nch, w = pieces(blk)[pc]
                a = SC_AT[blk] + k0
                dve.wait_ge(relu_done, n + 1)
                if h == 0:
                    dve.tensor_scalar(score[:, a:a + nch * w], relu_s[:, n % 2, 0:nch * w], w_tok[:, blk, h:h + 1], None,
                                      ALU.mult).then_inc(score_acc, 1)
                else:
                    dve.wait_ge(score_acc, n)
                    dve.scalar_tensor_tensor(out=score[:, a:a + nch * w], in0=relu_s[:, n % 2, 0:nch * w], scalar=w_tok[:, blk, h:h + 1],
                                             in1=score[:, a:a + nch * w], op0=ALU.mult, op1=ALU.add).then_inc(score_acc, 1)

            def keys(blk):
                return score[:, SC_AT[blk]:SC_AT[blk + 1]]

            def last(blk):
                return score[:, SC_AT[blk + 1] - P:SC_AT[blk + 1]]

            dve.wait_ge(score_acc, len(UNITS))
            dve.wait_ge(const_ready, 5)
            dve.memset(keys(0), 0.0).then_inc(topk_step, 1)
            dve.wait_ge(topk_step, 1)
            dve.tensor_tensor(last(0), last(0), causal[:, :], ALU.min).then_inc(mask_ready, 1)
            steps = 1
            for blocks in TOPK_PAIRS:
                nb = len(blocks)
                for blk in blocks:
                    dve.tensor_tensor(last(blk), last(blk), causal[:, :], ALU.add).then_inc(topk_step, 1)
                steps += nb
                with dve.Fori(0, TOP_K // 32) as i:
                    for r in range(4):
                        done = steps + 2 * nb * (4 * i + r)
                        for a, blk in enumerate(blocks):
                            dve.wait_ge(topk_step, done - nb + a + 1)
                            dve.memset(turn[:, a:a + 1], 0.0)
                            dve.max(out=best[:, a, :], in_=keys(blk)).then_inc(topk_step, 1)
                        for a, blk in enumerate(blocks):
                            dve.wait_ge(topk_step, done + a + 1)
                            dve.memset(turn[:, 2 + a:3 + a], 0.0)
                            dve.match_replace(out=keys(blk), in_to_replace=best[:, a, :], in_values=keys(blk), imm_value=SENT).then_inc(topk_step, 1)
                steps += 2 * nb * (TOP_K // 8)
                for a, blk in enumerate(blocks):
                    dve.wait_ge(topk_step, steps)
                    dve.tensor_scalar(keys(blk), keys(blk), SENT, FILL, ALU.not_equal, ALU.mult).then_inc(topk_step, 1)
                    steps += 1
                    dve.wait_ge(topk_step, steps)
                    dve.tensor_tensor(last(blk), last(blk), causal[:, :], ALU.min).then_inc(mask_ready, 1)

            def mask(g):
                blk, hg = GROUPS[g]
                ncp = len(pieces(blk))
                base = LOGITS_TO[g - 1] if g else 0
                if g >= 2:
                    dve.wait_ge(trans_full, CHUNKS_TO[g - 2])
                dve.wait_ge(mask_ready, MASK_AT[blk] + 1)
                for h in range(4):
                    for pc, (k0, nch, w) in enumerate(pieces(blk)):
                        n = base + h * ncp + pc
                        a = SC_AT[blk] + k0
                        dve.wait_ge(pair_full, len(UNITS) + n + 1)
                        if pc:
                            dve.wait_ge(masked, n)
                        dve.tensor_tensor_reduce(wide(logit[:, g % 2, h, k0:k0 + nch * w], nch), pair(n, nch, w),
                                                 wide(score[:, a:a + nch * w], nch), 1.0, row_max[:, g % 2, 4 + h:5 + h] if pc else SENT,
                                                 ALU.add, ALU.max, row_max[:, g % 2, h:h + 1] if pc == ncp - 1 else row_max[:, g % 2, 4 + h:5 + h]).then_inc(masked, 1)
                dve.wait_ge(masked, LOGITS_TO[g])
                dve.tensor_scalar(neg_max[:, g % 2, :], row_max[:, g % 2, 0:4], -ATTN_SCALE, None, ALU.mult).then_inc(nm_done, 1)

            def probabilities(g):
                nk = block_keys(GROUPS[g][0])
                dve.wait_ge(exp_done, 4 * (g + 1))
                dve.reciprocal(inv_sum[:, g % 2, :], row_sum[:, g % 2, :]).then_inc(inv_step, 1)
                dve.wait_ge(inv_step, g + 1)
                for h in range(4):
                    dve.tensor_scalar(logit[:, g % 2, h, 0:nk], logit[:, g % 2, h, 0:nk], inv_sum[:, g % 2, h:h + 1], None, ALU.mult).then_inc(norm_done, 1)

            mask(0)
            probabilities(0)
            for g, (blk, hg) in enumerate(GROUPS):
                if g + 1 < len(GROUPS):
                    mask(g + 1)
                for r in range(blk + 2):
                    n = (CHUNKS_TO[g - 1] if g else 0) + r
                    k = META if r == blk + 1 else P
                    dve.wait_ge(pthi_done, n + 1)
                    dve.tensor_tensor(pt_lo[0:k, n % 2, :], ps[0:k, n % 2, :], pt_hi[0:k, n % 2, :], ALU.subtract).then_inc(ptlo_done, 1)
                dve.wait_ge(ohi_done, g + 1)
                dve.tensor_tensor(x_lo[:, 4 * hg:4 * hg + 4, P * blk:P * blk + P],
                                  ps[:, 2 + g % 2, :].rearrange("p (h t) -> p h t", h=4),
                                  x_hi[:, 4 * hg:4 * hg + 4, P * blk:P * blk + P], ALU.subtract).then_inc(olo_done, 1)
                if g + 1 < len(GROUPS):
                    probabilities(g + 1)
            dve.wait_ge(gate_used, 2 * KD)
            for m in range(KD):
                dve.wait_ge(g1_load[m % 2], 16 * (m // 2 + 1))
                for j, (t0, w) in enumerate(HALF):
                    n = 2 * m + j
                    dve.wait_ge(lin_full, TILE_AT[("wb", m), j] + 1)
                    if n >= 2:
                        dve.wait_ge(m_acc, n - 1)
                    dve.tensor_tensor(gy_s[:, n % 2, :], ps[:, bank(("wb", m), j), :], g1_s[:, m % 2, t0:t0 + w], ALU.mult).then_inc(gy_done, 1)
                    dve.wait_ge(gy_done, n + 1)
                    dve.tensor_tensor(mix[:, m, t0:t0 + w], mix[:, m, t0:t0 + w], gy_s[:, n % 2, :], ALU.add).then_inc(m_acc, 1)
            for m in range(KD):
                dve.wait_ge(mhi_done, m + 1)
                dve.tensor_tensor(x_lo[:, m, 0:S], mix[:, m, :], x_hi[:, m, 0:S], ALU.subtract).then_inc(mlo_done, 1)

            def wide_rs(first):
                return ps[:, first:first + 2, :]

            def two(ap):
                return ap.rearrange("p (n w) -> p n w", n=2)

            def diagonal(which, out_, done):
                for b in range(NB):
                    dve.tensor_scalar(out_[:, P * b:P * b + P], ident[:, :], nst[:, which, b:b + 1], None, ALU.mult).then_inc(diag_done, 1)

            dve.wait_ge(stat_full, 1)
            dve.tensor_scalar(nst[:, 0, :], ps[:, 4, 0:8], 1.0 / D, EPS, ALU.mult, ALU.add).then_inc(nst_step, 1)
            dve.wait_ge(nst_step, 1)
            dve.reciprocal(nst[:, 1, :], nst[:, 0, :]).then_inc(nst_step, 1)
            dve.wait_ge(nrt_done, 1)
            diagonal(4, n_diag, 0)
            dve.wait_ge(rs_full, 1)
            for m in range(KD):
                if m >= 2:
                    dve.wait_ge(nlo_done, m - 1)
                dve.scalar_tensor_tensor(out=two(n_st[:, m % 2, :]), in0=two(mix[:, m, :]), scalar=v("norm2_g", m), in1=wide_rs(6),
                                         op0=ALU.mult, op1=ALU.mult).then_inc(upper_free, 1)

            def gated_chunk(it, par, first=False):
                at = L0 if first else gu_at(it, par)
                for h, (t0, w) in enumerate(HALF):
                    dve.wait_ge(lin_full, at + (h + 3))
                    dve.wait_ge(silu_done, 4 * it + (2 * par + h + 1))
                    if not first:
                        dve.wait_ge(alo_done, 2 * it + par)
                    dve.tensor_tensor(a_f[:, t0:t0 + w], silu_s[:, t0:t0 + w], ps[:, 2 + h, :], ALU.mult).then_inc(af_done, 1)

            def sums(it, par, at, behind=None):
                for n in range(16):
                    m, (t0, w) = n // 2, HALF[n % 2]
                    dve.wait_ge(lin_full, at + (n + 1))
                    dve.wait_ge(upper_free, 32 * it + (16 * par + n + 1))
                    dve.tensor_tensor(mix[:, m, t0:t0 + w], mix[:, m, t0:t0 + w], ps[:, 4 + n % 4, :], ALU.add).then_inc(upper_free, 1)
                    if behind is not None and n % 2:
                        behind(m - 1)

            def add_squares(m):
                if m < 1:
                    return
                dve.wait_ge(sqa_done, KD + m + 1)
                if m >= 2:
                    dve.wait_ge(acca_done, 7 + m - 1)
                dve.tensor_tensor(n_acc[:, 0, :], n_sq[:, 0, 0, :] if m == 1 else n_acc[:, 0, :], n_sq[:, m % 2, 0, :], ALU.add).then_inc(acca_done, 1)

            gated_chunk(0, 0, first=True)
            with dve.Fori(0, (FC - 2) // 2) as it:
                for par in range(2):
                    gated_chunk(it, par + 1)
                    sums(it, par, gu_at(it, par + 1) + 4)
            it_last = (FC - 2) // 2
            gated_chunk(it_last, 1)
            dve.wait_ge(msq_done, 2)
            dve.tensor_scalar(mem_ss[:, :], mem_ss[:, :], 1.0 / D, EPS, ALU.mult, ALU.add).then_inc(mst_step, 1)
            dve.wait_ge(mst_step, 1)
            dve.reciprocal(mem_ss[:, :], mem_ss[:, :]).then_inc(mst_step, 1)
            sums(it_last, 0, L2 - 32)
            dve.wait_ge(mrt_done, 1)
            for r in range(2):
                dve.tensor_scalar(mem_tok[:, r, :], mem_tok[:, r, :], mem_ss[:, r:r + 1], None, ALU.mult).then_inc(ms_scaled, 1)
            dve.tensor_tensor(gfg[:, :], vec[:, VEC["final_g"]:VEC["final_g"] + KD], vec[:, VEC["pre_norm_g_2"]:VEC["pre_norm_g_2"] + KD], ALU.mult).then_inc(mst_step, 1)
            sums(it_last, 1, L2 - 16, add_squares)
            add_squares(KD - 1)

            dve.wait_ge(stat_full, 2)
            dve.tensor_scalar(nst[:, 0, :], ps[:, 4, 0:8], 1.0 / D, EPS, ALU.mult, ALU.add).then_inc(nst_step, 1)
            dve.wait_ge(nst_step, 3)
            dve.reciprocal(nst[:, 1, :], nst[:, 0, :]).then_inc(nst_step, 1)
            dve.wait_ge(nst_step, 4)
            dve.scalar_tensor_tensor(out=nst[:, 2, :], in0=ps[:, 4, 8:16], scalar=1.0 / D, in1=nst[:, 1, :], op0=ALU.mult, op1=ALU.mult).then_inc(mst_step, 1)
            dve.wait_ge(mst_step, 4)
            dve.tensor_scalar(nst[:, 2, :], nst[:, 2, :], EPS, None, ALU.add).then_inc(mst_step, 1)
            dve.wait_ge(mst_step, 5)
            dve.reciprocal(nst[:, 3, :], nst[:, 2, :]).then_inc(nst_step, 1)
            dve.wait_ge(nrt_done, 2)
            diagonal(4, n_diag, 8)
            dve.tensor_tensor(nst[:, 5, :], nst[:, 4, :], nst[:, 5, :], ALU.mult).then_inc(mst_step, 1)
            dve.wait_ge(mst_step, 6)
            diagonal(5, n_diag2, 16)
            dve.wait_ge(rs_full, 3)
            for m in range(KD):
                if m >= 2:
                    dve.wait_ge(nlo_done, KD + m - 1)
                dve.scalar_tensor_tensor(out=two(n_st[:, m % 2, :]), in0=two(mix[:, m, :]), scalar=gfg[:, m:m + 1], in1=wide_rs(6),
                                         op0=ALU.mult, op1=ALU.mult).then_inc(xn_done, 1)
                dve.wait_ge(xn_done, XN_0 + m + 1)
                dve.scalar_tensor_tensor(out=two(mix[:, m, :]), in0=two(mix[:, m, :]), scalar=v("final_g", m), in1=wide_rs(4),
                                         op0=ALU.mult, op1=ALU.mult).then_inc(x2_done, 1)

            def ub(key):
                return 4 + UP_AT[key] % 4

            def lb(key, j):
                return LIN_AT[key, j] % 3

            for n in range(4):
                for c in range(2):
                    dve.wait_ge(memhi_done, MEMHI_0 + 2 * n + 2)
                    dve.scalar_tensor_tensor(out=memt_lo[:, 2 * n + c, :], in0=ps[:, ub(("mem", n)), MEM * c:MEM * c + MEM], scalar=v("mem_norm_g_2", 2 * n + c),
                                             in1=memt_hi[:, 2 * n + c, :], op0=ALU.mult, op1=ALU.subtract).then_inc(memlo_done, 1)
            dve.wait_ge(wthi_done, WTHI_0 + 1)
            dve.tensor_tensor(wt_lo[:, :, :], ps[:, ub(("wsp", 0)), :].rearrange("p (g t) -> p g t", g=4), wt_hi[:, :, :], ALU.subtract).then_inc(wtlo_done, 1)

            def ln_stats(n):
                b = ub(("av", n))
                dve.wait_ge(up_full, UP_0 + UP_AT["av", n] + 1)
                if n >= 2:
                    dve.wait_ge(vn_sub, VSUB_0 + 4 * (n - 1))
                for g in range(4):
                    dve.bn_stats(bst[:, n % 2, g, :], ps[:, b, P * g:P * g + P]).then_inc(ln_step, 1)
                for g in range(4):
                    dve.wait_ge(ln_step, 6 * n + g + 1)
                    dve.bn_aggr(bag[:, n % 2, g, :], bst[:, n % 2, g, :]).then_inc(mx_step if g < 3 else vn_ready, 1)
                dve.wait_ge(vn_ready, n + 1)
                dve.tensor_scalar(vrs[:, n % 2, :], bag[:, n % 2, :, 1], EPS, None, ALU.add).then_inc(ln_step, 1)
                dve.wait_ge(ln_step, 6 * n + 5)
                dve.reciprocal(vrs[:, n % 2, :], vrs[:, n % 2, :]).then_inc(ln_step, 1)

            def ln_apply(n):
                b = ub(("av", n))
                dve.wait_ge(lnrt_done, LNRT_0 + n + 1)
                if n >= 2:
                    dve.wait_ge(vlnlo_done, VLNLO_0 + n - 1)
                for g in range(4):
                    dve.tensor_scalar(vn_s[:, n % 2, P * g:P * g + P], ps[:, b, P * g:P * g + P], bag[:, n % 2, g, 0:1], vrs[:, n % 2, g:g + 1],
                                      ALU.subtract, ALU.mult).then_inc(vn_sub, 1)
                dve.wait_ge(vn_sub, VSUB_0 + 4 * n + 4)
                dve.tensor_tensor(vn_s[:, n % 2, :], vn_s[:, n % 2, :], vgb[:, :], ALU.mult).then_inc(vn_done, 1)
                dve.wait_ge(vn_done, VN_0 + 2 * n + 1)
                dve.tensor_tensor(vn_s[:, n % 2, :], vn_s[:, n % 2, :], vbb[:, :], ALU.add).then_inc(vn_done, 1)

            dve.wait_ge(c2_load, 7 * 16)
            dve.wait_ge(nlo_done, 2 * KD)
            ln_stats(0)
            for n in range(NB):
                if n + 1 < NB:
                    ln_stats(n + 1)
                ln_apply(n)
            for m in range(2):
                dve.wait_ge(mkhi_done, MKHI_0 + m + 1)
                dve.tensor_tensor(mk_lo[:, m, :], ps[:, lb(("mk", m), 0), 0:MEM], mk_hi[:, m, :], ALU.subtract).then_inc(mklo_done, 1)
            dve.wait_ge(mvthi_done, MVTHI_0 + 1)
            dve.tensor_tensor(mv_lo[:, :, :], ps[:, ub(("mvt", 0)), :].rearrange("p (r d) -> p r d", r=2), mv_hi[:, :, :], ALU.subtract).then_inc(mvtlo_done, 1)
            dve.wait_ge(au_done, AU_0 + 8)
            dve.wait_ge(vlnlo_done, VLNLO_0 + NB)
            for n in range(8):
                g, h = n // 2, n % 2
                dve.wait_ge(up_full, UP_0 + UP_AT["sp", n] + 1)
                if n >= 2:
                    dve.wait_ge(sp_done, SP_0 + n - 1)
                t = vn_s[:, n % 2, :].rearrange("p (b t) -> p b t", b=4)
                dve.tensor_tensor(t, ps[:, ub(("sp", n)), :].rearrange("p (b t) -> p b t", b=4),
                                  bsp[:, g, :].unsqueeze(1).broadcast_to([P, 4, P]), ALU.add).then_inc(sp_sum, 1)
                dve.wait_ge(sp_sum, SPSUM_0 + n + 1)
                dve.tensor_tensor(yz[:, g, BANK * h:BANK * h + BANK], yz[:, g, BANK * h:BANK * h + BANK], vn_s[:, n % 2, :], ALU.mult).then_inc(sp_done, 1)
            for n in range(2):
                for u in range(2):
                    dve.wait_ge(svhi_done, SVHI_0 + 2 * n + 2)
                    o = vd_hi[:, 4 * n:4 * n + 4, :, DH * u:DH * u + DH]
                    dve.tensor_tensor(vd_lo[:, 4 * n:4 * n + 4, :, DH * u:DH * u + DH],
                                      ps[:, ub(("svt", n)), :].rearrange("p (b c d) -> p b c d", b=4, c=2), o, ALU.subtract).then_inc(svlo_done, 1)
            for kind, hi, lo, hi_done, before, lo_done in (("sq", sq_hi, sq_lo, sqhi_done, SQHI_0, sqlo_done), ("mq", mq_hi, mq_lo, mqhi_done, MQHI_0, mqlo_done)):
                for m in range(2):
                    for j, (t0, w) in enumerate(HALF):
                        dve.wait_ge(hi_done, before + 2 * m + j + 1)
                        dve.tensor_tensor(lo[:, m, t0:t0 + w], ps[:, lb((kind, m), j), :], hi[:, m, t0:t0 + w], ALU.subtract).then_inc(lo_done, 1)

            dve.wait_ge(bias_done, BIAS_0 + 2)
            dve.wait_ge(sink_done, 1)
            MX = 3 * NB

            def maxima(n):
                blk, kind = UNITS2[n]
                s_ = n % 2
                k0 = P if n == 0 else 0
                first = MX + 4 * (n // 2) + (3 if kind else 0)
                dve.wait_ge(lg_full, LG_0 + n + 1)
                lg = ps[:, 4:6, :].rearrange("p u (c k) -> p (u c) k", c=2)
                if kind:
                    dve.tensor_reduce(mx2[:, s_, :], lg, mybir.AxisListType.X, ALU.max).then_inc(mx_step, 1)
                    dve.wait_ge(mx_step, first + 1)
                    dve.tensor_scalar(nm2[:, s_, :], mx2[:, s_, :], -(DH ** -0.5), None, ALU.mult).then_inc(nm2_done, 1)
                    return
                if n >= 2:
                    dve.wait_ge(pt_full, TURN_AT[n - 2, 1] + 1)
                dve.scalar_tensor_tensor(out=p_s[:, s_, :, k0:2 * P], in0=lg[:, :, k0:2 * P], scalar=DH ** -0.5, in1=bias[:, :, k0:2 * P],
                                         op0=ALU.mult, op1=ALU.add).then_inc(mx_step, 1)
                dve.wait_ge(mx_step, first + 1)
                dve.tensor_reduce(mx2[:, s_, :], p_s[:, s_, :, k0:2 * P], mybir.AxisListType.X, ALU.max).then_inc(mx_step, 1)
                dve.wait_ge(mx_step, first + 2)
                dve.tensor_tensor(mx2[:, s_, :], mx2[:, s_, :], sink[:, :], ALU.max).then_inc(mx_step, 1)
                dve.wait_ge(mx_step, first + 3)
                dve.tensor_tensor(se2[:, s_, :], sink[:, :], mx2[:, s_, :], ALU.subtract).then_inc(mx_step2, 1)
                dve.tensor_scalar(nm2[:, s_, :], mx2[:, s_, :], -1.0, None, ALU.mult).then_inc(nm2_done, 1)

            def normed(n):
                blk, kind = UNITS2[n]
                s_ = n % 2
                k0 = P if n == 0 else 0
                dve.wait_ge(e2_done, E2_0 + 4 * n + 4)
                if not kind:
                    dve.wait_ge(b_done, blk + 1)
                    dve.tensor_tensor(rs2[:, s_, :], rs2[:, s_, :], se2[:, s_, :], ALU.add).then_inc(pn_step, 1)
                    dve.wait_ge(pn_step, 3 * blk + 1)
                dve.reciprocal(rs2[:, s_, :], rs2[:, s_, :]).then_inc(pn_step, 1)
                dve.wait_ge(pn_step, 3 * blk + 2 + kind)
                for h in range(4):
                    dve.tensor_scalar(p_s[:, s_, h, k0:2 * P], p_s[:, s_, h, k0:2 * P], rs2[:, s_, h:h + 1], None, ALU.mult).then_inc(pn_done, 1)

            maxima(0)
            normed(0)
            dve.wait_ge(zs_done, ZS_0 + 8)
            for n, (blk, kind) in enumerate(UNITS2):
                if n + 1 < len(UNITS2):
                    maxima(n + 1)
                for kc in key_chunks(n):
                    t = TURN_AT[n, kc]
                    dve.wait_ge(p2hi_done, P2HI_0 + t + 1)
                    if n >= 1:
                        dve.wait_ge(pv_full, PV_0 + n)
                    dve.tensor_tensor(p2_lo[:, kc, :], ps[:, 6 + kc, :], p2_hi[:, kc, :], ALU.subtract).then_inc(p2lo_done, 1)
                if n + 1 < len(UNITS2):
                    normed(n + 1)
                m, t0 = n // 4, 2 * P * (n % 4)
                dve.wait_ge(zsilu_done, ZSILU_0 + n + 1)
                dve.tensor_tensor(yz[:, m, t0:t0 + 2 * P], yz[:, m, t0:t0 + 2 * P], z_s[:, 2 * P * (n % 2):2 * P * (n % 2) + 2 * P], ALU.mult).then_inc(zt_done, 1)
                dve.wait_ge(pv_full, PV_0 + n + 1)
                o = ps[:, 3, :].rearrange("p (c u t) -> p c u t", c=2, u=2)
                for u in range(2):
                    y = yz[DH * u:DH * u + DH, 4 + 2 * kind:6 + 2 * kind, P * blk:P * blk + P]
                    dve.tensor_tensor(y, y, o[DH * u:DH * u + DH, :, u, :], ALU.mult).then_inc(pvg_done, 1)
            for m in range(0, KD, 2):
                dve.wait_ge(yhi_done, YHI_0 + m + 1)
                dve.tensor_tensor(x_lo[:, m, 0:S], yz[:, m, :], x_hi[:, m, 0:S], ALU.subtract).then_inc(yloa_done, 1)
            dve.wait_ge(pg_load, 16)
            dve.wait_ge(x2_load, 16)
            for q in range(2):
                a, z = 4 * q, 4 * q + 4
                dve.wait_ge(ysq_done, YSQ_0 + z)
                dve.wait_ge(wysq_done, WYSQ_0 + z)
                dve.tensor_tensor(osum[:, 2, a:z], osum[:, 0, a:z], osum[:, 1, a:z], ALU.add).then_inc(os_step, 1)
                dve.wait_ge(os_step, 3 * q + 1)
                dve.tensor_scalar(osum[:, 2, a:z], osum[:, 2, a:z], 1.0 / D, EPS, ALU.mult, ALU.add).then_inc(os_step, 1)
                dve.wait_ge(os_step, 3 * q + 2)
                dve.reciprocal(osum[:, 2, a:z], osum[:, 2, a:z]).then_inc(os_step, 1)
                dve.wait_ge(osrt_done, q + 1)
                dve.wait_ge(ylob_done, YLOB_0 + 4)
                for b in range(a, z):
                    if b >= 4:
                        dve.wait_ge(o_store[b % 4], 16)
                    dve.scalar_tensor_tensor(out=o_s[:, b % 4, 0:BANK], in0=wy[:, b, :], scalar=osum[:, 2, b:b + 1], in1=pg[:, 0:BANK],
                                             op0=ALU.mult, op1=ALU.mult).then_inc(on_done, 1)
                    dve.scalar_tensor_tensor(out=o_s[:, b % 4, BANK:D], in0=ps[:, b, :], scalar=osum[:, 2, b:b + 1], in1=pg[:, BANK:D],
                                             op0=ALU.mult, op1=ALU.mult).then_inc(on_done, 1)
                    dve.wait_ge(on_done, 2 * b + 2)
                    dve.tensor_tensor(o_s[:, b % 4, BANK:D], o_s[:, b % 4, BANK:D], x2_tok[:, b, BANK:D], ALU.add).then_inc(oa_done, 1)

        @block.gpsimd
        def _(pool):
            pool.memset(ident[:, :], 0.0).then_inc(const_ready, 1)
            pool.memset(ones[:, :], 1.0).then_inc(const_ready, 1)
            pool.memset(causal[:, :], 0.0).then_inc(const_ready, 1)
            pool.memset(anti[:, :], 0.0).then_inc(rb_const, 1)
            pool.memset(relb[:, :], 0.0).then_inc(rb_const, 1)
            pool.wait_ge(const_ready, 3)
            pool.affine_select(out=ident[:, :], in_=ident[:, :], compare_op=ALU.not_equal, fill=1.0, base=0,
                               pattern=[[-1, P]], channel_multiplier=1).then_inc(const_ready, 1)
            pool.affine_select(out=causal[:, :], in_=causal[:, :], compare_op=ALU.is_ge, fill=FILL, base=0,
                               pattern=[[-1, P]], channel_multiplier=1).then_inc(const_ready, 1)

            pool.wait_ge(rb_const, 2)
            pool.affine_select(out=anti[:, :], in_=anti[:, :], compare_op=ALU.not_equal, fill=1.0, base=1 - P,
                               pattern=[[1, P]], channel_multiplier=1).then_inc(rb_const, 1)

            def split(p):
                if p >= PB2 + len(PANELS2):
                    return
                pool.wait_ge(whi_done, p + 1)
                n = width(p)
                pool.tensor_tensor(w_lo[:, p % 2, 0:n], w_raw[:, p % 2, 0:n], w_hi[:, p % 2, 0:n], ALU.subtract).then_inc(wlo_done, 1)

            def split_behind(key):
                split(PANEL_AT[key] + 2)

            split(0)
            split(1)
            split_behind(("c", 0))
            split_behind(("kw", 0))
            split_behind(("qi", 0))
            split_behind(("qi", 1))
            steps = 0
            for g in range(4):
                split_behind(("u", g))
                pool.wait_ge(u_done, 3 * (g + 1))
                if g == 0:
                    pool.wait_ge(cklo_done, 3)
                if g >= 1:
                    pool.wait_ge(pooled_done, g)
                src, shift = u_s[:, g % 2], 1
                for i in range(g + 1):
                    dst, lead = sum_s[:, i % 2], 2 * shift - 1
                    if i:
                        pool.wait_ge(pool_step, steps)
                    pool.tensor_tensor(dst[:, lead:T], src[:, lead:T], src[:, lead - shift:T - shift], ALU.add).then_inc(pool_step, 1)
                    steps += 1
                    src, shift = dst, 2 * shift
                mean, less = sum_s[:, (g + 1) % 2, 0:S], sum_s[:, g % 2, META:T]
                pool.wait_ge(pool_step, steps)
                pool.tensor_scalar(mean, less, 1.0 / shift, None, ALU.mult).then_inc(pool_step, 1)
                steps += 1
                pool.wait_ge(pool_step, steps)
                pool.tensor_tensor(mean, mean, u_s[:, g % 2, META:T], ALU.subtract).then_inc(pool_sub, 1)
                pool.wait_ge(pool_sub, g + 1)
                pool.tensor_copy(pool_hi[:, g, :], mean).then_inc(pool_step, 1)
                steps += 1
                pool.wait_ge(pool_step, steps)
                pool.tensor_tensor(pool_lo[:, g, :], mean, pool_hi[:, g, :], ALU.subtract).then_inc(pooled_done, 1)
            for g in range(4):
                for j, (t0, w) in enumerate(HALF):
                    n = 2 * g + j
                    pool.wait_ge(brhi_done, n + 1)
                    pool.tensor_tensor(br_lo[:, g, t0:t0 + w], mix_s[:, n % 2, :], br_hi[:, g, t0:t0 + w], ALU.subtract).then_inc(brlo_done, 1)
            split_behind(("poolw", 0))
            for m in range(KD):
                split_behind(("q", m))

            def branch(g, w, base):
                for m in range(KD):
                    split_behind((g, m))
                    split_behind((w, m))
                    pool.wait_ge(gate_done, 2 * (base + m + 1))
                    pool.wait_ge(y_done, 2 * (base + m + 1))
                    if base == 0:
                        pool.tensor_tensor(mix[:, m, :], stage[:, m % 2, :], y_s[:, m % 2, :], ALU.mult).then_inc(gate_used, 1)
                        continue
                    pool.tensor_tensor(y_s[:, m % 2, :], stage[:, m % 2, :], y_s[:, m % 2, :], ALU.mult).then_inc(gated, 1)
                    pool.wait_ge(gated, m + 1)
                    pool.tensor_tensor(mix[:, m, :], mix[:, m, :], y_s[:, m % 2, :], ALU.add).then_inc(gate_used, 1)

            branch("g0", "wa", 0)
            for m in range(4):
                split_behind(("cc", m))
                split_behind(("cu", m))
                pool.wait_ge(cv_in, 8 * m + 6)
                pool.tensor_tensor(cv[:, 2, :], cv[:, 0, :], cv[:, 1, :], ALU.mult).then_inc(cv_v, 1)
                pool.wait_ge(cv_tap, 3 * m + 3)
                pool.tensor_tensor(cv[:, 3, 0:S], cv[:, 3, 0:S], cv[:, 4, 0:S], ALU.add).then_inc(cv_step, 1)
                pool.wait_ge(cv_step, 2 * m + 1)
                pool.tensor_tensor(cv[:, 3, 0:S], cv[:, 3, 0:S], cv[:, 0, 0:S], ALU.add).then_inc(cv_step, 1)
                split_behind(("cb", m))
                pool.wait_ge(cv_step, 2 * m + 2)
                pool.wait_ge(cv_in, 8 * m + 8)
                pool.tensor_tensor(cv[:, 1, 0:S], cv[:, 3, 0:S], cv[:, 5, 0:S], ALU.mult).then_inc(cv_sum, 1)
                pool.wait_ge(brhi_done, 8 + m + 1)
                pool.tensor_tensor(br_lo[:, m, :], cv[:, 1, 0:S], br_hi[:, m, :], ALU.subtract).then_inc(brlo_done, 1)
            branch("g2", "wc", KD)
            for m in range(KD):
                split_behind(("g1", m))
            for b in range(NB):
                pool.wait_ge(qhi_done, b + 1)
                pool.tensor_tensor(q_lo[:, b % 2], q_f[:, :, :], q_hi[:, b % 2], ALU.subtract).then_inc(qlo_done, 1)
            for m in range(KD):
                split_behind(("wb", m))
            def low_parts(i):
                for m in range(KD):
                    pool.wait_ge(nhi_done, KD * i + m + 1)
                    pool.tensor_tensor(x_lo[:, m, 0:S], n_st[:, m % 2, :], x_hi[:, m, 0:S], ALU.subtract).then_inc(nlo_done, 1)

            for m in range(KD):
                split_behind(("wo", m))
                if m >= 1:
                    pool.wait_ge(sqa_done, m + 1)
                    if m >= 2:
                        pool.wait_ge(acca_done, m - 1)
                    pool.tensor_tensor(n_acc[:, 0, :], n_sq[:, 0, 0, :] if m == 1 else n_acc[:, 0, :], n_sq[:, m % 2, 0, :], ALU.add).then_inc(acca_done, 1)
            low_parts(0)

            def split_mlp(it, off):
                sl = (PB + off) % 2
                pool.wait_ge(whi_done, panel_no(it, off) + 1)
                pool.tensor_tensor(w_lo[:, sl, :], w_raw[:, sl, :], w_hi[:, sl, :], ALU.subtract).then_inc(wlo_done, 1)

            def activations(it, par, first=False):
                off = 0 if first else 3 * par - 1
                split_mlp(it, off + 2)
                split_mlp(it, off + 3)
                pool.wait_ge(ahi_done, 2 * it + (par + 1))
                pool.tensor_tensor(a_lo[:, par % 2, :], a_f[:, :], a_hi[:, par % 2, :], ALU.subtract).then_inc(alo_done, 1)

            activations(0, 0, first=True)
            with pool.Fori(0, (FC - 2) // 2) as it:
                for par in range(2):
                    activations(it, par + 1)
                    split_mlp(it, 3 * par + 6)
            it_last = (FC - 2) // 2
            activations(it_last, 1)
            pool.wait_ge(c2_load, 7 * 16)
            pool.affine_select(out=w_sp[:, :, :], in_=w_sp[:, :, :], compare_op=ALU.is_ge, fill=0.0, base=0,
                               pattern=[[0, 4], [-1, P]], channel_multiplier=1).then_inc(wsp_done, 1)
            split_mlp(it_last, 6)
            for m in range(1, KD):
                pool.wait_ge(sqb_done, m + 1)
                if m >= 2:
                    pool.wait_ge(accb_done, m - 1)
                pool.tensor_tensor(n_acc[:, 1, :], n_sq[:, 0, 1, :] if m == 1 else n_acc[:, 1, :], n_sq[:, m % 2, 1, :], ALU.add).then_inc(accb_done, 1)
            split_mlp(it_last, 7)
            low_parts(1)

            def behind2(key):
                split(AT2[key] + 2)

            for m in range(4):
                behind2(("av", m))
            pool.wait_ge(x2_store[0], 64)
            pool.wait_ge(x2_store[1], 64)
            behind2(("au", 0))
            for n in range(NB):
                if n in (3, 5, 7):
                    behind2(("au", (n - 1) // 2))
                pool.wait_ge(vlnhi_done, VLNHI_0 + n + 1)
                pool.tensor_tensor(vln_lo[:, n, :], vn_s[:, n % 2, :], vln_hi[:, n, :], ALU.subtract).then_inc(vlnlo_done, 1)
            for kind in ("mk", "mv"):
                for m in range(2):
                    behind2((kind, m))
            behind2(("sk", 0))
            behind2(("sv", 0))
            for kind in ("sq", "mq"):
                for m in range(2):
                    behind2((kind, m))
            pool.wait_ge(kdhi_done, KDHI_0 + 1)
            pool.tensor_tensor(kd_lo[:, :, :], kd_f[:, :, :], kd_hi[:, :, :], ALU.subtract).then_inc(kdlo_done, 1)
            for m in (4, 5, 6, 7, 0, 1, 2, 3):
                behind2(("z", m))
            for m in range(1, KD, 2):
                pool.wait_ge(yhi_done, YHI_0 + m + 1)
                pool.tensor_tensor(x_lo[:, m, 0:S], yz[:, m, :], x_hi[:, m, 0:S], ALU.subtract).then_inc(ylob_done, 1)
            for n in range(2 * KD):
                behind2(("wout", n))
            for b in range(NB):
                pool.wait_ge(x2_load, 16)
                pool.wait_ge(on_done, 2 * b + 1)
                pool.tensor_tensor(o_s[:, b % 4, 0:BANK], o_s[:, b % 4, 0:BANK], x2_tok[:, b, 0:BANK], ALU.add).then_inc(ob_done, 1)


_INS = ["x", "meta", "norm1_g", "w_in", "b_gate", "pool_w", "pool_scale", "w_a", "kv_norm_g", "w_b", "conv_w", "w_c", "w_o",
        "norm2_g", "w_gate_up", "w_down", "final_g", "mem_2", "pre_norm_g_2", "post_norm_g_2", "mem_norm_g_2",
        "w_in_2", "w_mem_kv_2", "v_norm_g_2", "v_norm_b_2", "w_spatial_2", "b_spatial_2", "attn_sinks_2", "rel_bias_2", "w_out_2"]


def kernel(**inputs):
    import concourse.bacc as bacc
    from concourse.bass_utils import run_bass_kernel_spmd

    nc = bacc.Bacc("TRN2", target_bir_lowering=False, num_devices=1, dynamic_dma_scratch_size=1024)
    arrays, I = {}, {}
    for name in _INS:
        a = np.ascontiguousarray(inputs[name])
        arrays[f"in_{name}"] = a
        I[name] = nc.dram_tensor(f"in_{name}", a.shape, mybir.dt.from_np(a.dtype), kind="ExternalInput").ap()
    arrays["in_bucket_table"] = bucket_table()
    I["bucket_table"] = nc.dram_tensor("in_bucket_table", (64, SWA_SPAN), F32, kind="ExternalInput").ap()
    out = nc.dram_tensor("out_0", (1, S, D), F32, kind="ExternalOutput").ap()
    scratch = {name: nc.dram_tensor(f"{name}_scratch", (KD, P, S), F32, kind="Internal").ap() for name in ("q", "g1")}
    scratch["x2"] = nc.dram_tensor("x2_scratch", (S, D), F32, kind="Internal").ap()
    scratch["rb"] = nc.dram_tensor("rb_scratch", (4, SWA_SPAN), F32, kind="Internal").ap()
    build(nc, I, out, scratch)
    return run_bass_kernel_spmd(nc, [arrays], core_ids=[0]).results[0]["out_0"]
```

```python
from contextlib import ExitStack

import numpy as np
import concourse.bass as bass
from concourse import mybir

ALU = mybir.AluOpType
ACT = mybir.ActivationFunctionType
F32 = mybir.dt.float32
F32R = mybir.dt.float32r

P = 128
D = 1024
KD = D // P
S = 1024
META = 16
T = S + META
EPS = 1e-6
HEADS = 8
TOP_K = 256
IDX_SCALE = (8 ** -0.5) * (32 ** -0.5)
ATTN_SCALE = P ** -0.5
D_FF = 2816
FC = D_FF // P
BANK = 512
NB = S // P
MEM = 256
DH = 64
NEG = -1e30
SWA_SPAN = 3 * P
SENT = -3.4e38
FILL = -3.0e38

FULL = [(0, 352), (352, 352), (704, 336)]
REAL = [(META, BANK), (META + BANK, BANK)]
HALF = [(0, BANK), (BANK, BANK)]

U0, Q0, C0, QI0, KI0, CB0, CC0, CU0, G0 = 0, 512, 1536, 1664, 1920, 1960, 2472, 2984, 3496


AU2, AV2, SQ2, SK2, SV2, MQ2, Z2 = 0, 512, 1024, 1280, 1408, 1536, 1792


def block_keys(b):
    return META + P * (b + 1)


def pieces(b):
    n = block_keys(b)
    if n <= BANK:
        return [(0, 1, n)]
    if n <= 2 * BANK:
        return [(0, 2, n // 2)]
    return [(0, 2, 352), (704, 1, n - 704)]


def linear_plan():
    panels, tiles = [], []

    def panel(key, n_tiles):
        panels.append(key)
        tiles.extend((key, j) for j in range(n_tiles))

    panel(("c", 0), 3)
    panel(("kw", 0), 3)
    for m in range(2):
        panel(("qi", m), 2)
    tiles.extend((("csum", 0), j) for j in range(3))
    tiles.append((("wtok", 0), 0))
    for m in range(4):
        panel(("u", m), 3)
        if m == 2:
            tiles.extend((("ctok", 0), j) for j in range(3))
    for m in range(KD):
        panel(("q", m), 2)
    panel(("poolw", 0), 8)
    for m in range(KD):
        panel(("g0", m), 2)
        panel(("wa", m), 2)
    for m in range(4):
        panel(("cc", m), 3)
        panel(("cu", m), 3)
        panel(("cb", m), 2)
    for m in range(KD):
        panel(("g2", m), 2)
        panel(("wc", m), 2)
    for m in range(KD):
        panel(("g1", m), 2)
    for m in range(KD):
        panel(("wb", m), 2)
    for m in range(KD):
        panel(("wo", m), 2)
    return panels, tiles


def second_plan():
    panels, ticks = [], []

    def panel(key, n):
        panels.append(key)
        ticks.extend((key, j) for j in range(n))

    for m in range(2):
        panel(("mk", m), 1)
    for m in range(2):
        panel(("mv", m), 1)
    for m in range(2):
        panel(("au", m), 2)
    for m in range(4):
        panel(("av", m), 2)
    for m in range(2, 4):
        panel(("au", m), 2)
    panel(("sk", 0), 2)
    panel(("sv", 0), 2)
    for m in range(2):
        panel(("sq", m), 2)
    for m in range(2):
        panel(("mq", m), 2)
    for m in (4, 5, 6, 7, 0, 1, 2, 3):
        panel(("z", m), 2 if m >= 4 else 4)
    for n in range(2 * KD):
        panel(("wout", n), NB if n % KD == KD - 1 else int(n < 2 * KD - 2))
    upper = [("mem", n) for n in range(4)] + [("x2", n) for n in range(16)] + [("wsp", 0), ("rb", 0), ("mvt", 0)]
    upper += [("av", n) for n in range(NB)] + [("flip", 0), ("flip", 1)]
    upper += [("sp", n) for n in range(8)] + [("svt", 0), ("svt", 1)]
    return panels, ticks, upper


def bucket_table():
    table = np.zeros((64, SWA_SPAN), np.float32)
    for i in range(SWA_SPAN):
        dist = 2 * P - 1 - i
        if not 0 <= dist < P:
            table[32, i] = 1.0
            continue
        large = 16 + int(np.log(max(dist, 1) / 16) / np.log(128 / 16) * 16)
        table[dist if dist < 16 else min(large, 31), i] = 1.0
    return table


def build(nc, I, out, scratch):
    PANELS, TILES = linear_plan()
    PANEL_AT = {key: p for p, key in enumerate(PANELS)}
    TILE_AT = {key: n for n, key in enumerate(TILES)}
    THROUGH = {p: max(n for (key, _), n in TILE_AT.items() if key == PANELS[p]) + 1 for p in range(len(PANELS))}
    WIDTH = {"wa": 512, "wc": 512, "poolw": 512}

    PB, L0 = len(PANELS), len(TILES)
    PANELS2, TICKS2, UPPER = second_plan()
    PB2, L2 = PB + 3 * FC, L0 + 20 * FC - 16
    AT2 = {key: PB2 + n for n, key in enumerate(PANELS2)}
    TICK2 = {key: L2 + n for n, key in enumerate(TICKS2)}
    THROUGH2 = {key: max(n for (k_, _), n in TICK2.items() if k_ == key) + 1 for key in PANELS2 if (key, 0) in TICK2}
    UP_AT = {key: n for n, key in enumerate(UPPER)}

    def width(p):
        if PB <= p < PB2:
            return KD * P
        if p >= PB2:
            return BANK if PANELS2[p - PB2][0] == "wout" else KD * P
        return WIDTH.get(PANELS[p][0], KD * P)

    def through(p):
        if p < PB:
            return THROUGH[p]
        if p < PB2:
            off = p - PB
            return {0: L0 + 2, 1: L0 + 4, 3 * FC - 1: L2, 3 * FC - 2: L2}[off]
        return THROUGH2[PANELS2[p - PB2]]

    def gu_at(it, par):
        return 40 * it + (L0 + 20 * par - 16)

    def panel_no(it, off):
        return 6 * it + (PB + off)

    def loads_of(it, off):
        return 3 * it + ((PB + off) // 2 + 1)

    q_scratch, g1_scratch, x2_scratch, rb_scratch = scratch["q"], scratch["g1"], scratch["x2"], scratch["rb"]
    w_in2 = I["w_in_2"][0]

    def second_source(key):
        kind, m = key
        if kind == "wout":
            return I["w_out_2"][0][P * (m % KD):P * (m % KD) + P, BANK * (m // KD):BANK * (m // KD) + BANK]
        if kind in ("mk", "mv"):
            w, c = I["w_mem_kv_2"][0], P * m + (MEM if kind == "mv" else 0)
        else:
            w, c = w_in2, {"av": AV2, "au": AU2, "sk": SK2, "sv": SV2, "sq": SQ2, "mq": MQ2, "z": Z2}[kind] + P * m
        return w[:, c:c + P].rearrange("(k p) c -> p k c", p=P)
    w_in = I["w_in"][0]

    def panel_source(key):
        kind, m = key
        cols = {"c": C0, "kw": KI0, "qi": QI0 + P * m, "u": U0 + P * m, "q": Q0 + P * m, "cb": CB0 + P * m,
                "cc": CC0 + P * m, "cu": CU0 + P * m, "g0": G0 + P * m, "g1": G0 + D + P * m, "g2": G0 + 2 * D + P * m}
        if kind in cols:
            w, c = w_in, cols[kind]
        elif kind == "poolw":
            return I["pool_w"][0].rearrange("g c d -> c g d")
        else:
            w, c = I[{"wa": "w_a", "wb": "w_b", "wc": "w_c", "wo": "w_o"}[kind]][0], P * m
        return w[:, c:c + P].rearrange("(k p) c -> p k c", p=P)

    with ExitStack() as ctx:
        at = [1152]

        def place(name, shape, dt, offset=None):
            if offset is None:
                offset = at[0]
                at[0] += -(-int(np.prod(shape[1:])) * 4 // 32) * 32
            return nc.alloc_sbuf_tensor_at(name, shape, dt, offset=offset)

        def sem(name):
            return ctx.enter_context(nc.semaphore(name))

        x_hi = place("x_hi", [P, KD, T], F32R)
        x_lo = place("x_lo", [P, KD, T], F32R)
        W_RAW = at[0]
        w_raw = place("w_raw", [P, 2, KD * P], F32)
        w_hi = place("w_hi", [P, 2, KD * P], F32R)
        w_lo = place("w_lo", [P, 2, KD * P], F32R)
        SC_AT = [sum(block_keys(a) for a in range(b)) for b in range(NB + 1)]
        score = place("score", [P, SC_AT[NB]], F32)
        c_hi = place("c_hi", [P, T], F32R)
        c_lo = place("c_lo", [P, T], F32R)
        ck_hi = place("ck_hi", [P, 9, P], F32R)
        ck_lo = place("ck_lo", [P, 9, P], F32R)
        RA = at[0]
        at[0] += 4 * 2 * T * 4
        RB = at[0]
        at[0] += KD * S * 4
        ident = place("ident", [P, P], F32)
        ones = place("ones", [P, P], F32)
        vec = place("vec", [P, 89], F32)
        w_tok = place("w_tok", [P, NB, 8], F32)
        ss = place("ss", [P, 9], F32)
        rstd = place("rstd", [P, 9], F32)
        best = place("best", [P, 2, 8], F32)
        causal = place("causal", [P, P], F32)
        row_max = place("row_max", [P, 2, 8], F32)
        neg_max = place("neg_max", [P, 2, 4], F32)
        row_sum = place("row_sum", [P, 2, 4], F32)
        inv_sum = place("inv_sum", [P, 2, 4], F32)
        anti = place("anti", [P, P], F32)
        relb = place("relb", [64, P], F32)
        nst = place("nst", [P, 6, 8], F32)
        gfg = place("gfg", [P, KD], F32)
        sink_n = place("sink_n", [P, 4], F32)
        sink = place("sink", [P, 4], F32)
        bst = place("bst", [P, 2, 4, 6], F32)
        bag = place("bag", [P, 2, 4, 2], F32)
        vrs = place("vrs", [P, 2, 4], F32)
        mem_ss = place("mem_ss", [P, 2], F32)
        mx2 = place("mx2", [P, 2, 4], F32)
        nm2 = place("nm2", [P, 2, 4], F32)
        se2 = place("se2", [P, 2, 4], F32)
        rs2 = place("rs2", [P, 2, 4], F32)
        osum = place("osum", [P, 3, NB], F32)
        turn = place("turn", [P, 4], F32)
        ST = at[0]
        VEC = {}
        rows = 0
        for name in ("norm1_g", "norm2_g", "final_g", "pre_norm_g_2", "post_norm_g_2", "mem_norm_g_2", "b_gate",
                     "pool_scale", "conv_w", "kv_norm_g"):
            VEC[name] = rows
            rows += int(np.prod(I[name].shape)) // P

        def v(name, n):
            return vec[:, VEC[name] + n:VEC[name] + n + 1]

        x_tok = place("x_tok", [P, 9, D], F32, RA)
        qi_hi = place("qi_hi", [P, 2, S], F32R, RA)
        qi_lo = place("qi_lo", [P, 2, S], F32R, RA + 8 * S)
        ki_hi = place("ki_hi", [P, T], F32R, RA + 16 * S)
        ki_lo = place("ki_lo", [P, T], F32R, RA + 16 * S + 4 * T)
        ki_f = place("ki_f", [P, T], F32, RA + 16 * S + 8 * T)
        pool_hi = place("pool_hi", [P, 4, S], F32R, RB)
        pool_lo = place("pool_lo", [P, 4, S], F32R, RB + 16 * S)
        br_hi = place("br_hi", [P, 4, S], F32R, RA)
        br_lo = place("br_lo", [P, 4, S], F32R, RA + 16 * S)
        mix = place("mix", [P, KD, S], F32, RB)
        logit = place("logit", [P, 2, 4, T], F32, RA)
        x_res = place("x_res", [P, KD, D], F32, RA)
        vec_rows = place("vec_rows", [P, P], F32, ST)
        junk = place("junk", [P, 2, D], F32, ST + 512)
        relu_s = place("relu_s", [P, 4, BANK], F32, RA + 16 * S + 8 * T)
        u_s = place("u_s", [P, 2, T], F32, ST + 8 * T)
        sum_s = place("sum_s", [P, 2, T], F32, ST + 16 * T)
        w_row = place("w_row", [P, S], F32, ST + 24 * T)
        c_raw = place("c_raw", [P, T], F32, RA + 16 * S + 12 * T)
        c_rs = place("c_rs", [P, T], F32, RB + 20 * S)
        c_sq = place("c_sq", [P, T], F32, RB + 32 * S - 4 * T)
        stage = place("stage", [P, 2, S], F32, ST)
        y_s = place("y_s", [P, 2, S], F32, ST + 8 * S)
        mix_s = place("mix_s", [P, 2, BANK], F32, ST + 16 * S)
        cv = place("cv", [P, 6, T], F32, ST)
        q_f = place("q_f", [P, HEADS, P], F32, ST)
        q_hi = place("q_hi", [P, 2, HEADS, P], F32R, ST + 4 * S)
        q_lo = place("q_lo", [P, 2, HEADS, P], F32R, ST + 12 * S)
        pt_hi = place("pt_hi", [P, 3, BANK], F32R, W_RAW)
        pt_lo = place("pt_lo", [P, 3, BANK], F32R, ST + 20 * S)
        g1_ring = place("g1_ring", [P, 2, S], F32, ST + 20 * S)
        g1_s = place("g1_s", [P, 2, S], F32, ST)
        gy_s = place("gy_s", [P, 2, BANK], F32, ST + 8 * S)

        n_acc = place("n_acc", [P, 2, S], F32, ST)
        n_sq = place("n_sq", [P, 2, 2, S], F32, ST + 8 * S)
        n_diag2 = place("n_diag2", [P, S], F32, ST + 8 * S)
        n_st = place("n_st", [P, 4, BANK], F32, ST + 16 * S)
        n_diag = place("n_diag", [P, S], F32, ST + 24 * S)
        silu_s = place("silu_s", [P, S], F32, RA)
        a_f = place("a_f", [P, S], F32, RA + 4 * S)
        a_hi = place("a_hi", [P, 2, S], F32R, RA + 8 * S)
        a_lo = place("a_lo", [P, 2, S], F32R, RA + 16 * S)
        RS = 1152 + 2 * KD * T * 4 + 6 * KD * P * 4
        x2_s = place("x2_s", [P, 4, S], F32, RA + 16 * S)
        memt_hi = place("memt_hi", [P, KD, MEM], F32R, RS)
        memt_lo = place("memt_lo", [P, KD, MEM], F32R, RS + 8 * S)
        vln_lo = place("vln_lo", [P, NB, BANK], F32R, RA + 16 * S)
        vd_hi = place("vd_hi", [P, NB, 2, P], F32R, RA)
        vd_lo = place("vd_lo", [P, NB, 2, P], F32R, RA + 8 * S)
        kd_hi = place("kd_hi", [P, 2, S], F32R, RA + 16 * S)
        kd_lo = place("kd_lo", [P, 2, S], F32R, RA + 24 * S)
        wy = place("wy", [P, NB, BANK], F32, RA)
        mem_junk = place("mem_junk", [P, 2, D], F32, RA + 24 * S)
        av_s = place("av_s", [P, 4, S], F32, RB)
        vln_hi = place("vln_hi", [P, NB, BANK], F32R, RB + 16 * S)
        mq_hi = place("mq_hi", [P, 2, S], F32R, RB)
        mq_lo = place("mq_lo", [P, 2, S], F32R, RB + 8 * S)
        sq_hi = place("sq_hi", [P, 2, S], F32R, RB + 16 * S)
        sq_lo = place("sq_lo", [P, 2, S], F32R, RB + 24 * S)
        x2_tok = place("x2_tok", [P, NB, D], F32, RB)
        yz = place("yz", [P, KD, S], F32, RS)
        mem_tok = place("mem_tok", [P, 2, D], F32, RS + 16 * S)
        kd_f = place("kd_f", [P, 2, S], F32, RS + 16 * S)
        vgb = place("vgb", [P, BANK], F32, RS + 24 * S)
        vbb = place("vbb", [P, BANK], F32, RS + 26 * S)
        bsp = place("bsp", [P, 4, P], F32, RS + 28 * S)
        sv_f = place("sv_f", [P, S], F32, RS + 24 * S)
        w_sp = place("w_sp", [P, 4, P], F32, RS + 32 * S)
        onehot = place("onehot", [64, SWA_SPAN], F32, RS + 34 * S)
        o_s = place("o_s", [P, 4, D], F32, RS)
        mk_hi = place("mk_hi", [P, 2, MEM], F32R, ST)
        mk_lo = place("mk_lo", [P, 2, MEM], F32R, ST + 2 * S)
        mv_hi = place("mv_hi", [P, 2, MEM], F32R, ST + 4 * S)
        mv_lo = place("mv_lo", [P, 2, MEM], F32R, ST + 6 * S)
        bias = place("bias", [P, 4, 2 * P], F32, ST + 8 * S)
        wt_hi = place("wt_hi", [P, 4, P], F32R, ST + 12 * S)
        wt_lo = place("wt_lo", [P, 4, P], F32R, ST + 14 * S)
        vn_s = place("vn_s", [P, 2, BANK], F32, ST + 16 * S)
        mv_f = place("mv_f", [P, 2, MEM], F32, RA + 8 * S)
        rb_s = place("rb_s", [4, SWA_SPAN], F32, ST + 22 * S)
        btoe = place("btoe", [P, 4, 2 * P], F32, ST + 24 * S)
        p_s = place("p_s", [P, 2, 4, 2 * P], F32, ST + 12 * S)
        p2_hi = place("p2_hi", [P, 2, BANK], F32R, ST + 20 * S)
        p2_lo = place("p2_lo", [P, 2, BANK], F32R, ST + 24 * S)
        z_s = place("z_s", [P, BANK], F32, RS + 32 * S)
        assert ST + 28 * S <= 229344
        pg = place("pg", [P, D], F32, ST + 12 * S)
        sq_junk = place("sq_junk", [P, 2, BANK], F32, ST + 16 * S)

        ps = ctx.enter_context(nc.psum_tensor("ps", [P, 8, BANK], F32))

        x_load = [sem(f"x_load{r}") for r in range(9)]
        vec_load, const_ready, vec_full, vec_ready = sem("vec_load"), sem("const_ready"), sem("vec_full"), sem("vec_ready")
        raw_load = [sem("raw_load0"), sem("raw_load1")]
        whi_done, wlo_done, lin_full, pair_full = sem("whi_done"), sem("wlo_done"), sem("lin_full"), sem("pair_full")
        sq_done, ms_done, inv_done, rt_done, xs_done = sem("sq_done"), sem("ms_done"), sem("inv_done"), sem("rt_done"), sem("xs_done")
        xt_full, xhi_done, xlo_done = sem("xt_full"), sem("xhi_done"), sem("xlo_done")
        csq_done, craw_done, cms_done, cinv_done = sem("csq_done"), sem("craw_done"), sem("cms_done"), sem("cinv_done")
        crt_done, cn_done, chi_done, clo_done = sem("crt_done"), sem("cn_done"), sem("chi_done"), sem("clo_done")
        ckhi_done, cklo_done, wtok_done = sem("ckhi_done"), sem("cklo_done"), sem("wtok_done")
        kif_done, kihi_done, kilo_done, ki_copies = sem("kif_done"), sem("kihi_done"), sem("kilo_done"), sem("ki_copies")
        qihi_done, qilo_done = sem("qihi_done"), sem("qilo_done")
        relu_done, score_acc, topk_step, mask_ready = sem("relu_done"), sem("score_acc"), sem("topk_step"), sem("mask_ready")
        u_done, pool_step, pool_sub, pooled_done = sem("u_done"), sem("pool_step"), sem("pool_sub"), sem("pooled_done")
        mixf_done, brhi_done, brlo_done = sem("mixf_done"), sem("brhi_done"), sem("brlo_done")
        q_copied, q_store = sem("q_copied"), [sem("q_store0"), sem("q_store1")]
        gate_done, y_done, gated, gate_used = sem("gate_done"), sem("y_done"), sem("gated"), sem("gate_used")
        cv_in, cv_v, cv_tap, cv_step, cv_sum = sem("cv_in"), sem("cv_v"), sem("cv_tap"), sem("cv_step"), sem("cv_sum")
        g1_done, g1_store = sem("g1_done"), [sem("g1_store0"), sem("g1_store1")]
        q_load, qhi_done, qlo_done = sem("q_load"), sem("qhi_done"), sem("qlo_done")
        masked, nm_done, exp_done, inv_step, norm_done = sem("masked"), sem("nm_done"), sem("exp_done"), sem("inv_step"), sem("norm_done")
        trans_full, pthi_done, ptlo_done, pv_step = sem("trans_full"), sem("pthi_done"), sem("ptlo_done"), sem("pv_step")
        ohi_done, olo_done = sem("ohi_done"), sem("olo_done")
        g1_load, gy_done, m_acc = [sem("g1_load0"), sem("g1_load1")], sem("gy_done"), sem("m_acc")
        mhi_done, mlo_done, xres_load, h_done = sem("mhi_done"), sem("mlo_done"), sem("xres_load"), sem("h_done")

        sqa_done, sqb_done, acca_done, accb_done, stat_full, nst_step = sem("sqa_done"), sem("sqb_done"), sem("acca_done"), sem("accb_done"), sem("stat_full"), sem("nst_step")
        nrt_done, diag_done, rs_full, upper_free, nhi_done, nlo_even = sem("nrt_done"), sem("diag_done"), sem("rs_full"), sem("upper_free"), sem("nhi_done"), sem("nlo_even")
        x2_done, silu_done, af_done, ahi_done, alo_done = sem("x2_done"), sem("silu_done"), sem("af_done"), sem("ahi_done"), sem("alo_done")
        c2_load, mem_load, msq_done, mst_step, mrt_done, ms_scaled = sem("c2_load"), sem("mem_load"), sem("msq_done"), sem("mst_step"), sem("mrt_done"), sem("ms_scaled")
        wsp_done = sem("wsp_done")
        rb_store, rb_load = sem("rb_store"), sem("rb_load")
        ln_step = sem("ln_step")

        kd_copies = sem("kd_copies")

        zt_done, b_done = sem("zt_done"), sem("b_done")
        mx_step, pn_step, pt_full = sem("mx_step"), sem("pn_step"), sem("pt_full")
        pvg_done = sem("pvg_done")
        os_step, osrt_done = sem("os_step"), sem("osrt_done")
        oa_done, ob_done, pg_load, rb_const = sem("oa_done"), sem("ob_done"), sem("pg_load"), sem("rb_const")
        zg_done, nlo_odd, vn_ready, mx_step2, on_done, sink_done = sem("zg_done"), sem("nlo_odd"), sem("vn_ready"), sem("mx_step2"), sem("on_done"), sem("sink_done")
        x2_store, x2_load, o_store = [sem(f"x2_store{n}") for n in range(4)], sem("x2_load"), [sem(f"o_store{n}") for n in range(4)]

        XGROUPS = [(0, [0, 1, 2, 3], BANK), (BANK, [4, 5, 6, 7], BANK), (2 * BANK, [8], META)]

        def tile_rows(r):
            return P if r < 8 else META

        SCORES = [(b, k0 + ch * w, w, hg) for b in range(NB) for k0, nch, w in pieces(b) for ch in range(nch) for hg in range(2)]
        SCORE_SLOTS = [(key, half) for key in [("u", 3, j) for j in range(3)] + [("q", m, j) for m in range(KD) for j in range(2)]
                       for half in range(2)]

        def scores_behind(kind, m, j, half):
            if ((kind, m, j), half) not in SCORE_SLOTS:
                return range(0)
            i, n = SCORE_SLOTS.index(((kind, m, j), half)), len(SCORE_SLOTS)
            return range(i * len(SCORES) // n, (i + 1) * len(SCORES) // n)

        TOPK_PAIRS = [(1,), (2, 3), (4, 5), (6, 7)]
        MASK_AT = {b: n for n, b in enumerate([0] + [b for pair in TOPK_PAIRS for b in pair])}
        GROUPS = [(b, g) for b in range(NB) for g in range(2)]
        LOGITS = [(b, g, h, pc) for b, g in GROUPS for h in range(4) for pc in range(len(pieces(b)))]
        LOGITS_TO = [sum(4 * len(pieces(b)) for b, _ in GROUPS[:n + 1]) for n in range(len(GROUPS))]
        CHUNKS_TO = [sum(b + 2 for b, _ in GROUPS[:n + 1]) for n in range(len(GROUPS))]

        x2_copied, X2_0 = craw_done, 3
        memhi_done, MEMHI_0 = csq_done, 3
        wthi_done, WTHI_0 = chi_done, 1
        rb_done, RB_0 = crt_done, 1
        av_done, AV_0 = u_done, 3 * 4
        lnrt_done, LNRT_0 = rt_done, 3
        vlnhi_done, VLNHI_0 = xhi_done, 3 * KD
        bias_done, BIAS_0 = wtok_done, 1
        au_done, AU_0 = mixf_done, 8
        mkhi_done, MKHI_0 = kihi_done, 1
        mvf_done, MVF_0 = kif_done, 3
        mvthi_done, MVTHI_0 = ckhi_done, 3
        skf_done, SKF_0 = q_copied, 2 * KD
        svf_done, SVF_0 = g1_done, 2 * KD
        svhi_done, SVHI_0 = brhi_done, 12
        sqhi_done, SQHI_0 = qihi_done, 4
        mqhi_done, MQHI_0 = qhi_done, NB
        zs_done, ZS_0 = gate_done, 4 * KD
        zcopy_done, ZCOPY_0 = y_done, 4 * KD
        e2_done, E2_0 = exp_done, 4 * len(GROUPS)
        p2hi_done, P2HI_0 = pthi_done, CHUNKS_TO[-1]
        yhi_done, YHI_0 = mhi_done, 2 * KD
        wy_done, WY_0 = cv_in, 32
        wysq_done, WYSQ_0 = sq_done, 9
        ysq_done, YSQ_0 = cv_tap, 12
        kdhi_done, KDHI_0 = ohi_done, len(GROUPS)
        memlo_done, MEMLO_0 = ms_done, 3
        wtlo_done, WTLO_0 = clo_done, 1
        mklo_done, MKLO_0 = kilo_done, 1
        mvtlo_done, MVTLO_0 = cklo_done, 3
        sp_sum, SPSUM_0 = masked, LOGITS_TO[-1]
        sp_done, SP_0 = m_acc, 2 * KD
        svlo_done, SVLO_0 = olo_done, len(GROUPS)
        sqlo_done, SQLO_0 = qilo_done, 4
        mqlo_done, MQLO_0 = norm_done, 3 * len(GROUPS)
        pnorm_done, PNORM_0 = pool_sub, 4
        vn_sub, VSUB_0 = xs_done, 9
        vn_done, VN_0 = gy_done, 2 * KD
        xn_done, XN_0 = cn_done, 1
        nm2_done, NM2_0 = nm_done, 4 * len(GROUPS)
        pn_done, PN_0 = score_acc, 4 * len(SCORES)
        p2lo_done, P2LO_0 = ptlo_done, CHUNKS_TO[-1]
        yloa_done, YLOA_0 = mlo_done, 2 * KD
        vlnlo_done, VLNLO_0 = pooled_done, 4
        kdlo_done, KDLO_0 = brlo_done, 12
        ylob_done, YLOB_0 = qlo_done, NB
        pv_full, PV_0 = pv_step, CHUNKS_TO[-1]
        up_full, UP_0 = xt_full, 24
        lg_full, LG_0 = pair_full, len(SCORES) + LOGITS_TO[-1]

        def released2(key, j):
            kind, m = key
            if kind == "z":
                return (zs_done, ZS_0 + 2 * (m - 4) + j + 1) if m >= 4 else (zcopy_done, ZCOPY_0 + 4 * m + j + 1)
            s, before, per = {"av": (av_done, AV_0, 2), "au": (au_done, AU_0, 2), "mk": (mklo_done, MKLO_0, 1), "mv": (mvf_done, MVF_0, 1),
                              "sk": (skf_done, SKF_0, 4), "sv": (svf_done, SVF_0, 2), "sq": (sqlo_done, SQLO_0, 2),
                              "mq": (mqlo_done, MQLO_0, 2)}[kind]
            return s, before + per * m + (2 * j + 2 if kind == "sk" else j + 1)

        LINEAR2 = [key for key in TICKS2 if key[0][0] != "wout"]
        LIN_AT = {key: n for n, key in enumerate(LINEAR2)}

        def up_released(key):
            kind, n = key
            return {"x2": (x2_copied, X2_0 + n + 1), "mem": (memlo_done, MEMLO_0 + 2 * n + 2), "wsp": (wtlo_done, WTLO_0 + 1),
                    "rb": (rb_done, RB_0 + 1), "av": (vn_sub, VSUB_0 + 4 * n + 4), "flip": (bias_done, BIAS_0 + n + 1),
                    "mvt": (mvtlo_done, MVTLO_0 + 1), "sp": (sp_sum, SPSUM_0 + n + 1), "svt": (svlo_done, SVLO_0 + 2 * n + 2)}[kind]

        UNITS2 = [(b, kind) for b in range(NB) for kind in range(2)]

        def key_chunks(n):
            return [1] if n == 0 else [0, 1]

        TURN_AT = {t: i for i, t in enumerate((n, kc) for n in range(len(UNITS2)) for kc in key_chunks(n))}

        def released(key, j):
            kind, m = key
            if kind in ("g0", "g2"):
                return gate_done, 2 * (m + (KD if kind == "g2" else 0)) + j + 1
            if kind in ("wa", "wc"):
                return y_done, 2 * (m + (KD if kind == "wc" else 0)) + j + 1
            if kind in ("cc", "cu", "cb"):
                return cv_in, 8 * m + {"cc": 0, "cu": 3, "cb": 6}[kind] + j + 1
            s, per = {"c": (craw_done, 3), "kw": (kif_done, 3), "qi": (qilo_done, 2), "csum": (cms_done, 3),
                      "ctok": (cklo_done, 3), "wtok": (wtok_done, 1), "u": (u_done, 3), "poolw": (mixf_done, 8),
                      "q": (q_copied, 2), "g1": (g1_done, 2), "wb": (gy_done, 2), "wo": (h_done, 2)}[kind]
            return s, per * m + j + 1

        def heads_at(g, r):
            if not 0 <= g < len(GROUPS):
                return []
            if g == 0:
                return []
            nk = GROUPS[g - 1][0] + 2
            return [h for h in range(4) if (h if nk >= 4 else h * nk // 4) == r]

        def pair(n, nch, w):
            a = 4 + 2 * (n % 2)
            return ps[:, a:a + nch, 0:w]

        def wide(ap, nch):
            return ap.rearrange("p (n w) -> p n w", n=nch)

        block = ctx.enter_context(nc.Block())

        @block.sync
        def _(sp):
            meta, x = I["meta"], I["x"][0]
            sp.dma_start(x_tok[0:META, 0, :], meta).then_inc(x_load[0], 16)
            sp.dma_start(x_tok[META:P, 0, :], x[0:P - META, :]).then_inc(x_load[0], 16)
            for r in range(1, 9):
                sp.dma_start(x_tok[0:tile_rows(r), r, :], x[P * r - META:P * r - META + tile_rows(r), :]).then_inc(x_load[r], 16)
            for name, row in VEC.items():
                n = int(np.prod(I[name].shape)) // P
                a = I[name]
                a = a.rearrange("(n p) -> n p", p=P) if len(a.shape) == 1 else (
                    a[0].rearrange("(n p) -> n p", p=P) if len(a.shape) == 2 else a[0].rearrange("t (n p) -> (t n) p", p=P))
                sp.dma_start(vec_rows[row:row + n, :], a).then_inc(vec_load, 16)

            def load(p, src):
                if p >= 2:
                    sp.wait_ge(wlo_done, p - 1)
                dst = w_raw[:, p % 2, 0:width(p)]
                sp.dma_start(dst.rearrange("p (k c) -> p k c", c=P) if len(src.shape) == 3 else dst, src).then_inc(raw_load[p % 2], 16)

            for p, key in enumerate(PANELS):
                load(p, panel_source(key))
                if key == ("qi", 1):
                    sp.wait_ge(kif_done, 3)
                    for j in range(1, 4):
                        sp.dma_start(ki_f[32 * j:32 * j + 32, :], ki_f[0:32, :]).then_inc(ki_copies, 16)
                if key == ("g1", 4):
                    sp.wait_ge(q_store[0], 64)
                    sp.wait_ge(q_store[1], 64)
                    sp.wait_ge(gate_used, 2 * KD)
                    sp.dma_start(q_f[:, :, :], q_scratch[:, :, 0:P].rearrange("h d t -> d h t")).then_inc(q_load, 16)
                if key == ("g1", 6):
                    sp.wait_ge(qlo_done, 1)
                    sp.dma_start(q_f[:, :, :], q_scratch[:, :, P:2 * P].rearrange("h d t -> d h t")).then_inc(q_load, 16)
                if key == ("wb", 1):
                    sp.wait_ge(g1_store[0], 64)
                    sp.wait_ge(g1_store[1], 64)
                    for b in range(2, NB):
                        sp.wait_ge(qlo_done, b)
                        sp.dma_start(q_f[:, :, :], q_scratch[:, :, P * b:P * b + P].rearrange("h d t -> d h t")).then_inc(q_load, 16)
                    sp.wait_ge(olo_done, 16)
                    for m in range(2):
                        sp.dma_start(g1_s[:, m, :], g1_scratch[m]).then_inc(g1_load[m], 16)
                    sp.dma_start(x_res[:, :, :], x.rearrange("(r p) d -> p r d", p=P)).then_inc(xres_load, 16)
                if key[0] == "wb" and key[1] >= 2:
                    sp.wait_ge(m_acc, 2 * (key[1] - 1))
                    sp.dma_start(g1_s[:, key[1] % 2, :], g1_scratch[key[1]]).then_inc(g1_load[key[1] % 2], 16)
            sp.wait_ge(rb_const, 4)
            sp.dma_start(relb[0:32, 0:4], I["rel_bias_2"]).then_inc(c2_load, 16)
            sp.dma_start(onehot[:, :], I["bucket_table"]).then_inc(c2_load, 16)
            sp.dma_start(w_sp[:, :, :], I["w_spatial_2"][0].rearrange("g t s -> t g s")).then_inc(c2_load, 16)
            sp.dma_start(vgb[:, :], I["v_norm_g_2"][0].partition_broadcast(P)).then_inc(c2_load, 16)
            sp.dma_start(vbb[:, :], I["v_norm_b_2"][0].partition_broadcast(P)).then_inc(c2_load, 16)
            sp.dma_start(bsp[:, :, :], I["b_spatial_2"][0].partition_broadcast(P)).then_inc(c2_load, 16)
            sp.dma_start(sink_n[:, :], I["attn_sinks_2"][0].partition_broadcast(P)).then_inc(c2_load, 16)
            sp.dma_start(mem_tok[:, :, :], I["mem_2"][0].rearrange("(r p) d -> p r d", p=P)).then_inc(mem_load, 16)

            w_gu, w_dn = I["w_gate_up"][0], I["w_down"][0]

            def load_mlp(it, off, src):
                sp.wait_ge(wlo_done, panel_no(it, off) - 1)
                sl = (PB + off) % 2
                dst = w_raw[:, sl, :]
                sp.dma_start(dst.rearrange("p (k c) -> p k c", c=P) if len(src.shape) == 3 else dst, src).then_inc(raw_load[sl], 16)

            def gate_up(c, half):
                return w_gu[:, bass.ds(c * P + half * D_FF, P)].rearrange("(k p) c -> p k c", p=P)

            def mlp_chunk(it, par):
                c = 2 * it + par
                load_mlp(it, 3 * par + 2, gate_up(c + 1, 0))
                load_mlp(it, 3 * par + 3, gate_up(c + 1, 1))
                load_mlp(it, 3 * par + 4, w_dn[bass.ds(c * P, P), :])

            load_mlp(0, 0, gate_up(0, 0))
            load_mlp(0, 1, gate_up(0, 1))
            with sp.Fori(0, (FC - 2) // 2) as it:
                for par in range(2):
                    mlp_chunk(it, par)
            mlp_chunk((FC - 2) // 2, 0)
            load_mlp(0, 3 * FC - 1, w_dn[P * (FC - 1):P * FC, :])

            for key in PANELS2:
                load(AT2[key], second_source(key))
                if key == ("sq", 0):
                    sp.wait_ge(skf_done, SKF_0 + 4)
                    sp.dma_start(kd_f[DH:P, 0, :], kd_f[0:DH, 0, :]).then_inc(kd_copies, 16)
                    sp.dma_start(kd_f[0:DH, 1, :], kd_f[DH:P, 1, :]).then_inc(kd_copies, 16)
                if key == ("wout", 2):
                    for n in range(4):
                        sp.wait_ge(x2_store[n], 32)
                    sp.wait_ge(lg_full, LG_0 + len(UNITS2))
                    sp.dma_start(x2_tok[:, :, :], x2_scratch.rearrange("(r p) d -> p r d", p=P)).then_inc(x2_load, 16)
                    sp.wait_ge(pt_full, len(TURN_AT))
                    sp.dma_start(pg[:, :], I["post_norm_g_2"][0].partition_broadcast(P)).then_inc(pg_load, 16)
            for b in range(NB):
                sp.wait_ge(oa_done, b + 1)
                sp.wait_ge(ob_done, b + 1)
                sp.dma_start(out[0, P * b:P * b + P, :], o_s[:, b % 4, :]).then_inc(o_store[b % 4], 16)
            for n in range(4):
                sp.wait_ge(o_store[n], 32)

        @block.tensor
        def _(pe):
            def open_tile(n):
                if n >= 4:
                    pe.wait_ge(*released(*TILES[n - 4]))
                return n % 4

            def product(key, rhs_hi, rhs_lo, chunks, kd=KD, extra=None, ready=None, behind=None):
                p = PANEL_AT[key]
                s = p % 2
                pe.wait_ge(wlo_done, p + 1)
                for j, (t0, n) in enumerate(chunks):
                    b = open_tile(TILE_AT[key, j])
                    for k in range(kd):
                        if ready is not None:
                            pe.wait_ge(ready, KD * j + k + 1)
                        for i, (w, r) in enumerate(((w_hi, rhs_hi), (w_hi, rhs_lo), (w_lo, rhs_hi))):
                            mm = pe.matmul(ps[:, b, 0:n], w[:, s, P * k:P * k + P], r[:, k, t0:t0 + n],
                                           start=k == 0 and i == 0, stop=k == kd - 1 and i == 2 and extra is None)
                        if behind is not None and k == kd // 2 - 1:
                            behind(j, 0)
                    if extra is not None:
                        mm = extra(j, b)
                    mm.then_inc(lin_full, 1)
                    if behind is not None:
                        behind(j, 1)

            pe.wait_ge(const_ready, 5)
            pe.wait_ge(vec_load, 16 * 10)
            pe.transpose(ps[:, 7, 0:rows], vec_rows[0:rows, :], ident[0:rows, 0:rows]).then_inc(vec_full, 1)
            n = 0
            for t0, tiles, w in XGROUPS:
                pe.wait_ge(xs_done, tiles[-1] + 1)
                for c in range(KD):
                    if n >= 4:
                        pe.wait_ge(xlo_done, n - 3)
                    for r in tiles:
                        k = tile_rows(r)
                        mm = pe.transpose(ps[:, n % 4, P * (r % 4):P * (r % 4) + k], x_tok[0:k, r, P * c:P * c + P], ident[0:k, 0:k])
                    mm.then_inc(xt_full, 1)
                    n += 1
            pe.wait_ge(xlo_done, 24)
            product(("c", 0), x_hi, x_lo, FULL)
            product(("kw", 0), x_hi, x_lo, FULL)
            for m in range(2):
                product(("qi", m), x_hi, x_lo, REAL)
            for j, (t0, w) in enumerate(FULL):
                b = open_tile(TILE_AT[("csum", 0), j])
                pe.wait_ge(csq_done, j + 1)
                pe.matmul(ps[:, b, 0:w], ones[:, :], c_sq[:, t0:t0 + w], start=True, stop=True).then_inc(lin_full, 1)
            b = open_tile(TILE_AT[("wtok", 0), 0])
            pe.wait_ge(kif_done, 3)
            for r in range(NB):
                mm = pe.transpose(ps[:, b, 8 * r:8 * r + 8], w_row[32:40, P * r:P * r + P], ident[32:40, 32:40])
            mm.then_inc(lin_full, 1)
            def scores(n):
                blk, k0, w, hg = SCORES[n]
                if n == 0:
                    pe.wait_ge(kilo_done, 1)
                    pe.wait_ge(qilo_done, 4)
                else:
                    pe.wait_ge(relu_done, 4 * n)
                for i, (a, kk) in enumerate(((qi_hi, ki_hi), (qi_hi, ki_lo), (qi_lo, ki_hi))):
                    for r in range(4):
                        mm = pe.matmul(ps[:, 4 + r, 0:w], a[32 * r:32 * r + 32, hg, P * blk:P * blk + P],
                                       kk[32 * r:32 * r + 32, k0:k0 + w], start=i == 0, stop=i == 2)
                mm.then_inc(pair_full, 1)

            def scored_product(kind, m, chunks):
                def behind(j, half):
                    for n in scores_behind(kind, m, j, half):
                        scores(n)
                product((kind, m), x_hi, x_lo, chunks, behind=behind)

            for m in range(4):
                scored_product("u", m, FULL)
                if m == 2:
                    pe.wait_ge(cn_done, 1)
                    for j, (t0, tiles, _) in enumerate(XGROUPS):
                        b = open_tile(TILE_AT[("ctok", 0), j])
                        for r in tiles:
                            mm = pe.transpose(ps[0:tile_rows(r), b, P * (r % 4):P * (r % 4) + P], c_sq[:, P * r:P * r + tile_rows(r)], ident[:, :])
                        mm.then_inc(lin_full, 1)
            for m in range(KD):
                scored_product("q", m, REAL)
            p = PANEL_AT["poolw", 0]
            pe.wait_ge(wlo_done, p + 1)
            for g in range(4):
                pe.wait_ge(pooled_done, g + 1)
                for j, (t0, w) in enumerate(HALF):
                    b = open_tile(TILE_AT[("poolw", 0), 2 * g + j])
                    for i, (a, r) in enumerate(((w_hi, pool_hi), (w_hi, pool_lo), (w_lo, pool_hi))):
                        mm = pe.matmul(ps[:, b, 0:w], a[:, p % 2, P * g:P * g + P], r[:, g, t0:t0 + w], start=i == 0, stop=i == 2)
                    mm.then_inc(lin_full, 1)
            for m in range(KD):
                product(("g0", m), x_hi, x_lo, REAL)
                if m == 0:
                    pe.wait_ge(brlo_done, 8)
                product(("wa", m), br_hi, br_lo, HALF, 4)
            for m in range(4):
                product(("cc", m), x_hi, x_lo, FULL)
                product(("cu", m), x_hi, x_lo, FULL)
                product(("cb", m), x_hi, x_lo, REAL)
            for m in range(KD):
                product(("g2", m), x_hi, x_lo, REAL)
                if m == 0:
                    pe.wait_ge(brlo_done, 12)
                product(("wc", m), br_hi, br_lo, HALF, 4)
            def logits(g, h):
                blk, hg = GROUPS[g]
                pe.wait_ge(qlo_done, blk + 1)
                for pc, (k0, nch, w) in enumerate(pieces(blk)):
                    n = (LOGITS_TO[g - 1] if g else 0) + h * len(pieces(blk)) + pc
                    if n >= 2:
                        pe.wait_ge(masked, n - 1)
                    for ch in range(nch):
                        for i, (a, kk) in enumerate(((q_hi, c_hi), (q_hi, c_lo), (q_lo, c_hi))):
                            mm = pe.matmul(ps[:, 4 + 2 * (n % 2) + ch, 0:w], a[:, blk % 2, 4 * hg + h, :],
                                           kk[:, k0 + ch * w:k0 + ch * w + w], start=i == 0, stop=i == 2)
                    mm.then_inc(pair_full, 1)

            for m in range(KD):
                if m == KD - 1:
                    for h in range(4):
                        logits(0, h)
                product(("g1", m), x_hi, x_lo, REAL)

            pe.wait_ge(g1_done, 2 * KD)

            def turn(g, r):
                blk = GROUPS[g][0]
                n = (CHUNKS_TO[g - 1] if g else 0) + r
                k = META if r == blk + 1 else P
                if n >= 3:
                    pe.wait_ge(ptlo_done, n - 2)
                for h in range(4):
                    mm = pe.transpose(ps[0:k, n % 3, P * h:P * h + P], logit[:, g % 2, h, P * r:P * r + k], ident[:, :])
                mm.then_inc(trans_full, 1)

            def weigh(g, r):
                blk = GROUPS[g][0]
                n = (CHUNKS_TO[g - 1] if g else 0) + r
                k = META if r == blk + 1 else P
                pe.wait_ge(ptlo_done, n + 1)
                if r == 0 and g >= 1:
                    pe.wait_ge(olo_done, g)
                for i, (a, r_) in enumerate(((ck_hi, pt_hi), (ck_hi, pt_lo), (ck_lo, pt_hi))):
                    mm = pe.matmul(ps[:, 3, :], a[0:k, r, :], r_[0:k, n % 3, :],
                                   start=r == 0 and i == 0, stop=r == blk + 1 and i == 2)
                mm.then_inc(pv_step, 1)

            for g, (blk, hg) in enumerate(GROUPS):
                pe.wait_ge(norm_done, 3 * (g + 1))
                pe.wait_ge(pnorm_done, PNORM_0 + g + 1)
                turn(g, 0)
                turn(g, 1)
                for r in range(blk + 2):
                    if r + 2 < blk + 2:
                        turn(g, r + 2)
                    for h in heads_at(g + 1, r):
                        logits(g + 1, h)
                    weigh(g, r)

            pe.wait_ge(olo_done, 16)
            pe.wait_ge(ptlo_done, CHUNKS_TO[-1])
            for m in range(KD):
                product(("wb", m), x_hi, x_lo, HALF)
            pe.wait_ge(xres_load, 16)
            for m in range(KD):
                def residual(j, b, m=m):
                    for r in range(4):
                        mm = pe.matmul(ps[:, b, P * r:P * r + P], x_res[:, 4 * j + r, P * m:P * m + P], ident[:, :],
                                       start=False, stop=r == 3)
                    return mm
                product(("wo", m), x_hi, x_lo, HALF, extra=residual, ready=mlo_done if m == 0 else None)

            def norm_sums(i):
                pe.wait_ge(acca_done, 7 * i + 7)
                if i:
                    pe.wait_ge(accb_done, 7)
                    pe.wait_ge(upper_free, 2 * KD + 16 * (FC - 1))
                for st in range(i + 1):
                    for b in range(NB):
                        mm = pe.matmul(ps[:, 4, 8 * st + b:8 * st + b + 1], n_acc[:, st, P * b:P * b + P], ones[:, 0:1], start=True, stop=True)
                mm.then_inc(stat_full, 1)

            def norm_spread(i):
                for st in range(i + 1):
                    for h, (t0, w) in enumerate(HALF):
                        pe.wait_ge(diag_done, 8 * (i + st) + 4 * h + 4)
                        pe.matmul(ps[:, 6 - 2 * st + h, :], ones[:, :], (n_diag2 if st else n_diag)[:, t0:t0 + w], start=True, stop=True).then_inc(rs_full, 1)

            norm_sums(0)
            norm_spread(0)

            def gate_and_up(it, par, first=False, between=None):
                for half in range(2):
                    if half and between is not None:
                        between()
                    off = half if first else 3 * par - 1 + half
                    sl = (PB + off) % 2
                    pe.wait_ge(wlo_done, panel_no(it, off) + 1)
                    for h, (t0, w) in enumerate(HALF):
                        if not first:
                            pe.wait_ge(af_done if half else silu_done, 4 * it + 2 * par + (h - 1))
                        for k in range(KD):
                            if first and half == 0:
                                pe.wait_ge(nlo_odd if k % 2 else nlo_even, 4 * h + k // 2 + 1)
                            for i, (wt, r) in enumerate(((w_hi, x_hi), (w_hi, x_lo), (w_lo, x_hi))):
                                mm = pe.matmul(ps[:, 2 * half + h, :], wt[:, sl, P * k:P * k + P], r[:, k, t0:t0 + w],
                                               start=k == 0 and i == 0, stop=k == KD - 1 and i == 2)
                        mm.then_inc(lin_full, 1)

            def down(it, par, off, chunks=1):
                for n0 in range(0, 16, 4):
                    for c in range(chunks):
                        sl = (PB + off + c) % 2
                        if n0 == 0:
                            pe.wait_ge(wlo_done, panel_no(it, off) + (c + 1))
                            pe.wait_ge(alo_done, 2 * it + (par + c + 1))
                        for n in range(n0, n0 + 4):
                            m, (t0, w) = n // 2, HALF[n % 2]
                            if c == 0:
                                pe.wait_ge(upper_free, 32 * it + (16 * par + n + 2 * KD - 3))
                            for i, (wt, r) in enumerate(((w_hi, a_hi), (w_hi, a_lo), (w_lo, a_hi))):
                                mm = pe.matmul(ps[:, 4 + n % 4, :], wt[:, sl, P * m:P * m + P], r[:, par + c, t0:t0 + w],
                                               start=c == 0 and i == 0, stop=c == chunks - 1 and i == 2)
                            if c == chunks - 1:
                                mm.then_inc(lin_full, 1)

            def upper(key):
                n = UP_AT[key]
                if n >= 4:
                    pe.wait_ge(*up_released(UPPER[n - 4]))
                return 4 + n % 4

            def memory_turned():
                pe.wait_ge(upper_free, 2 * KD + 16 * (FC - 2))
                pe.wait_ge(ms_scaled, 2)
                for n in range(4):
                    b = upper(("mem", n))
                    for c in range(2):
                        for r in range(2):
                            mm = pe.transpose(ps[:, b, MEM * c + P * r:MEM * c + P * r + P], mem_tok[:, r, P * (2 * n + c):P * (2 * n + c) + P], ident[:, :])
                    mm.then_inc(up_full, 1)

            pe.wait_ge(h_done, 2 * KD)
            gate_and_up(0, 0, first=True)
            with pe.Fori(0, (FC - 2) // 2) as it:
                for par in range(2):
                    gate_and_up(it, par + 1)
                    down(it, par, 3 * par + 4)
            it_last = (FC - 2) // 2
            gate_and_up(it_last, 1, between=memory_turned)
            pe.wait_ge(memlo_done, MEMLO_0 + KD)
            down(it_last, 0, 4, chunks=2)

            def linear(key, j, rhs_hi, rhs_lo, t0, n):
                p = AT2[key]
                at = LIN_AT[key, j]
                pe.wait_ge(wlo_done, p + 1)
                if at >= 3:
                    pe.wait_ge(*released2(*LINEAR2[at - 3]))
                for k in range(KD):
                    if key == ("au", 0):
                        pe.wait_ge(nlo_odd if k % 2 else nlo_even, KD + 4 * j + k // 2 + 1)
                    for i, (wt, r) in enumerate(((w_hi, rhs_hi), (w_hi, rhs_lo), (w_lo, rhs_hi))):
                        mm = pe.matmul(ps[:, at % 3, 0:n], wt[:, p % 2, P * k:P * k + P], r[:, k, t0:t0 + n],
                                       start=k == 0 and i == 0, stop=k == KD - 1 and i == 2)
                mm.then_inc(lin_full, 1)

            def panel2(key):
                for j, (t0, w) in enumerate(HALF):
                    linear(key, j, x_hi, x_lo, t0, w)

            norm_sums(1)
            norm_spread(1)
            for m in range(2):
                linear(("mk", m), 0, memt_hi, memt_lo, 0, MEM)
            for m in range(2):
                linear(("mv", m), 0, memt_hi, memt_lo, 0, MEM)
            for m in range(2):
                panel2(("au", m))
            pe.wait_ge(x2_done, KD)
            for n in range(16):
                r, h = n // 2, n % 2
                b = upper(("x2", n))
                for c in range(4):
                    mm = pe.transpose(ps[:, b, P * c:P * c + P], mix[:, 4 * h + c, P * r:P * r + P], ident[:, :])
                mm.then_inc(up_full, 1)
            b = upper(("wsp", 0))
            pe.wait_ge(wsp_done, 1)
            for g in range(4):
                mm = pe.transpose(ps[:, b, P * g:P * g + P], w_sp[:, g, :], ident[:, :])
            mm.then_inc(up_full, 1)
            b = upper(("rb", 0))
            pe.wait_ge(c2_load, 7 * 16)
            pe.matmul(ps[:, b, 0:SWA_SPAN], relb[0:64, :], onehot[:, :], start=True, stop=True).then_inc(up_full, 1)
            b = upper(("mvt", 0))
            pe.wait_ge(mvf_done, MVF_0 + 2)
            for r in range(2):
                for c in range(2):
                    mm = pe.transpose(ps[:, b, MEM * r + P * c:MEM * r + P * c + P], mv_f[:, c, P * r:P * r + P], ident[:, :])
            mm.then_inc(up_full, 1)
            for m in range(4):
                panel2(("av", m))
            def turn_values(blocks):
                for n in blocks:
                    b = upper(("av", n))
                    for c in range(4):
                        mm = pe.transpose(ps[:, b, P * c:P * c + P], av_s[:, c, P * n:P * n + P], ident[:, :])
                    mm.then_inc(up_full, 1)

            pe.wait_ge(av_done, AV_0 + 8)
            turn_values(range(4))
            panel2(("au", 2))
            turn_values(range(4, 6))
            panel2(("au", 3))
            turn_values(range(6, NB))
            pe.wait_ge(rb_load, 16)
            for n in range(2):
                b = upper(("flip", n))
                pe.matmul(ps[:, b, :], anti[:, :], btoe[:, 2 * n:2 * n + 2, :], start=True, stop=True).then_inc(up_full, 1)
            panel2(("sk", 0))
            pe.wait_ge(vlnlo_done, VLNLO_0 + NB)
            pe.wait_ge(wtlo_done, WTLO_0 + 1)
            for n in range(8):
                g, h = n // 2, n % 2
                b = upper(("sp", n))
                for c in range(4):
                    blk = 4 * h + c
                    for i, (a, w) in enumerate(((vln_hi, wt_hi), (vln_lo, wt_hi), (vln_hi, wt_lo))):
                        mm = pe.matmul(ps[:, b, P * c:P * c + P], a[:, blk, P * g:P * g + P], w[:, g, :], start=i == 0, stop=i == 2)
                mm.then_inc(up_full, 1)
            panel2(("sv", 0))
            pe.wait_ge(svf_done, SVF_0 + 2)
            for n in range(2):
                b = upper(("svt", n))
                for c in range(4):
                    mm = pe.transpose(ps[:, b, P * c:P * c + P], sv_f[:, BANK * n + P * c:BANK * n + P * c + P], ident[:, :])
                mm.then_inc(up_full, 1)
            for kind in ("sq", "mq"):
                for m in range(2):
                    panel2((kind, m))
            for m in range(4, 8):
                panel2(("z", m))

            pe.wait_ge(sqlo_done, SQLO_0 + 4)
            pe.wait_ge(mqlo_done, MQLO_0 + 4)
            pe.wait_ge(kdlo_done, KDLO_0 + 1)
            pe.wait_ge(mklo_done, MKLO_0 + 2)
            pe.wait_ge(svlo_done, SVLO_0 + 4)
            pe.wait_ge(sp_sum, SPSUM_0 + 8)
            pe.wait_ge(mvtlo_done, MVTLO_0 + 1)

            def logits2(n):
                blk, kind = UNITS2[n]
                if n >= 1:
                    pe.wait_ge(e2_done, E2_0 + 4 * n)
                q_parts, k_parts = ((mq_hi, mq_lo), (mk_hi, mk_lo)) if kind else ((sq_hi, sq_lo), (kd_hi, kd_lo))
                a, z = (0, MEM) if kind else (P * max(blk - 1, 0), P * blk + P)
                for c, (i, (x, y)), u in [(c, e, u) for c in range(2) for e in enumerate(((0, 0), (0, 1), (1, 0))) for u in range(2)]:
                        r0, h = DH * u, 2 * c + u
                        o = 2 * P * c + 2 * P - (z - a)
                        mm = pe.matmul(ps[:, 4 + h % 2, o:o + z - a], q_parts[x][r0:r0 + DH, c, P * blk:P * blk + P],
                                       k_parts[y][r0:r0 + DH, c, a:z], start=i == 0, stop=i == 2)
                mm.then_inc(lg_full, 1)

            def turn2(n):
                pe.wait_ge(pn_done, PN_0 + 4 * n + 4)
                for kc in key_chunks(n):
                    if n >= 1 and (n - 1, kc) in TURN_AT:
                        pe.wait_ge(p2lo_done, P2LO_0 + TURN_AT[n - 1, kc] + 1)
                    for h in range(4):
                        mm = pe.transpose(ps[:, 6 + kc, P * h:P * h + P], p_s[:, n % 2, 2 * (h % 2) + h // 2, P * kc:P * kc + P], ident[:, :])
                    mm.then_inc(pt_full, 1)

            def values2(n):
                blk, kind = UNITS2[n]
                if n >= 1:
                    pe.wait_ge(pvg_done, 2 * n)
                pe.wait_ge(p2lo_done, P2LO_0 + TURN_AT[n, 1] + 1)
                for c in range(2):
                    chunks = key_chunks(n)
                    for kc in chunks:
                        if kind:
                            v_hi, v_lo = mv_hi[:, kc, P * c:P * c + P], mv_lo[:, kc, P * c:P * c + P]
                        else:
                            v_hi, v_lo = vd_hi[:, blk - 1 + kc, c, :], vd_lo[:, blk - 1 + kc, c, :]
                        for i, (a, r) in enumerate(((v_hi, p2_hi), (v_hi, p2_lo), (v_lo, p2_hi))):
                            mm = pe.matmul(ps[:, 3, 2 * P * c:2 * P * c + 2 * P], a, r[:, kc, 2 * P * c:2 * P * c + 2 * P],
                                           start=kc == chunks[0] and i == 0, stop=kc == chunks[-1] and i == 2)
                mm.then_inc(pv_full, 1)

            logits2(0)
            for n in range(len(UNITS2)):
                if n + 1 < len(UNITS2):
                    logits2(n + 1)
                turn2(n)
                linear(("z", n // 4), n % 4, x_hi, x_lo, 2 * P * (n % 4), 2 * P)
                values2(n)

            def out_step(half, k, b):
                p = AT2["wout", KD * half + k]
                for i, (y, w) in enumerate(((x_hi, w_hi), (x_lo, w_hi), (x_hi, w_lo))):
                    mm = pe.matmul(ps[:, b, :], y[:, k, P * b:P * b + P], w[:, p % 2, 0:BANK],
                                   start=k == 0 and i == 0, stop=k == KD - 1 and i == 2)
                return mm

            for half in range(2):
                for k in range(KD - 2 * half):
                    pe.wait_ge(wlo_done, AT2["wout", KD * half + k] + 1)
                    if half == 0:
                        pe.wait_ge(ylob_done if k % 2 else yloa_done, (YLOB_0 if k % 2 else YLOA_0) + k // 2 + 1)
                    for b in range(NB):
                        if half and k == 0:
                            pe.wait_ge(wy_done, WY_0 + b + 1)
                        mm = out_step(half, k, b)
                        if k == KD - 1 or b == NB - 1:
                            mm.then_inc(lin_full, 1)
            pe.wait_ge(wlo_done, PB2 + len(PANELS2))
            for b in range(NB):
                for k in (KD - 2, KD - 1):
                    mm = out_step(1, k, b)
                mm.then_inc(lin_full, 1)

        @block.scalar
        def _(act):
            def split(p):
                if p >= PB2 + len(PANELS2):
                    return
                act.wait_ge(raw_load[p % 2], 16 * (p // 2 + 1))
                if p >= 2:
                    act.wait_ge(lin_full, through(p - 2))
                act.copy(w_hi[:, p % 2, 0:width(p)], w_raw[:, p % 2, 0:width(p)]).then_inc(whi_done, 1)

            def split_behind(key):
                split(PANEL_AT[key] + 2)

            def tile(key, j):
                n = TILE_AT[key, j]
                act.wait_ge(lin_full, n + 1)
                return n % 4

            for gi, (t0, tiles, w) in enumerate(XGROUPS):
                for r in tiles:
                    k = tile_rows(r)
                    act.wait_ge(x_load[r], 32 if r == 0 else 16)
                    if r >= 2:
                        act.wait_ge(sq_done, r - 1)
                    act.activation(junk[0:k, r % 2, :], x_tok[0:k, r, :], ACT.Square, accum_out=ss[0:k, r:r + 1]).then_inc(sq_done, 1)
                k = tile_rows(tiles[0])
                act.wait_ge(inv_done, gi + 1)
                act.activation(rstd[0:k, tiles[0]:tiles[-1] + 1], rstd[0:k, tiles[0]:tiles[-1] + 1], ACT.Sqrt).then_inc(rt_done, 1)
            split(0)
            split(1)
            act.wait_ge(vec_full, 1)
            act.copy(vec[:, :], ps[:, 7, 0:rows]).then_inc(vec_ready, 1)
            act.wait_ge(vec_ready, 1)
            n = 0
            for t0, tiles, w in XGROUPS:
                for c in range(KD):
                    act.wait_ge(xt_full, n + 1)
                    act.activation(x_hi[:, c, t0:t0 + w], ps[:, n % 4, 0:w], ACT.Copy, scale=v("norm1_g", c)).then_inc(xhi_done, 1)
                    n += 1

            for j, (t0, w) in enumerate(FULL):
                b = tile(("c", 0), j)
                act.activation(c_sq[:, t0:t0 + w], ps[:, b, 0:w], ACT.Square).then_inc(csq_done, 1)
                act.copy(c_raw[:, t0:t0 + w], ps[:, b, 0:w]).then_inc(craw_done, 1)
            split_behind(("c", 0))
            for j, (t0, w) in enumerate(FULL):
                b = tile(("kw", 0), j)
                real = max(t0, META)
                act.copy(w_row[32:40, real - META:t0 + w - META], ps[32:40, b, real - t0:w])
                act.copy(ki_f[0:32, t0:t0 + w], ps[0:32, b, 0:w]).then_inc(kif_done, 1)
            split_behind(("kw", 0))
            for m in range(2):
                for j, (t0, w) in enumerate(HALF):
                    b = tile(("qi", m), j)
                    act.copy(qi_hi[:, m, t0:t0 + w], ps[:, b, 0:w]).then_inc(qihi_done, 1)
                split_behind(("qi", m))
            act.wait_ge(ki_copies, 48)
            act.copy(ki_hi[:, :], ki_f[:, :]).then_inc(kihi_done, 1)
            b = tile(("wtok", 0), 0)
            act.mul(w_tok[:, :, :], ps[:, b, 0:64].rearrange("p (r h) -> p r h", h=8), IDX_SCALE).then_inc(wtok_done, 1)
            def rectified(kind, m, j, half):
                for n in scores_behind(kind, m, j, half):
                    w = SCORES[n][2]
                    for r in range(4):
                        act.wait_ge(pair_full, n + 1)
                        if n:
                            act.wait_ge(score_acc, 4 * n + r - 3)
                        act.activation(relu_s[:, r, 0:w], ps[:, 4 + r, 0:w], ACT.Relu).then_inc(relu_done, 1)

            for m in range(4):
                if m >= 2:
                    act.wait_ge(pool_sub, m - 1)
                for j, (t0, w) in enumerate(FULL):
                    rectified("u", m, j, 0)
                    b = tile(("u", m), j)
                    act.copy(u_s[:, m % 2, t0:t0 + w], ps[:, b, 0:w]).then_inc(u_done, 1)
                    rectified("u", m, j, 1)
                split_behind(("u", m))
                if m == 1:
                    act.wait_ge(cinv_done, 1)
                    act.activation(c_rs[:, :], c_rs[:, :], ACT.Sqrt).then_inc(crt_done, 1)
                    act.wait_ge(cn_done, 1)
                    act.copy(c_hi[:, :], c_sq[:, :]).then_inc(chi_done, 1)
                if m == 2:
                    for j, (t0, tiles, w) in enumerate(XGROUPS):
                        b = tile(("ctok", 0), j)
                        k = tile_rows(tiles[0])
                        act.copy(ck_hi[0:k, tiles[0]:tiles[-1] + 1, :],
                                 ps[0:k, b, 0:P * len(tiles)].rearrange("p (r d) -> p r d", d=P)).then_inc(ckhi_done, 1)
            def store(kind, m, func, done, stores, dram, bias):
                ring = g1_ring if kind == "g1" else stage
                if m >= 2:
                    act.wait_ge(stores[m % 2], 16 * (m // 2))
                for j, (t0, w) in enumerate(HALF):
                    rectified(kind, m, j, 0)
                    b = tile((kind, m), j)
                    act.activation(ring[:, m % 2, t0:t0 + w], ps[:, b, :], func, bias=bias).then_inc(done, 1)
                    if j == 0:
                        rectified(kind, m, j, 1)
                split_behind((kind, m))
                act.wait_ge(done, 2 * m + 2)
                act.dma_start(dram[m], ring[:, m % 2, :]).then_inc(stores[m % 2], 16)
                rectified(kind, m, 1, 1)

            for m in range(KD):
                store("q", m, ACT.Copy, q_copied, q_store, q_scratch, 0.0)
            act.wait_ge(q_store[0], 64)
            act.wait_ge(q_store[1], 64)
            act.wait_ge(score_acc, 4 * len(SCORES))
            act.wait_ge(pooled_done, 4)
            for g in range(4):
                for j, (t0, w) in enumerate(HALF):
                    n = 2 * g + j
                    b = tile(("poolw", 0), n)
                    if n >= 2:
                        act.wait_ge(brlo_done, n - 1)
                    act.activation(mix_s[:, n % 2, :], ps[:, b, :], ACT.Copy, scale=v("pool_scale", g)).then_inc(mixf_done, 1)
                    act.wait_ge(mixf_done, n + 1)
                    act.copy(br_hi[:, g, t0:t0 + w], mix_s[:, n % 2, :]).then_inc(brhi_done, 1)
            split_behind(("poolw", 0))
            act.wait_ge(brlo_done, 8)

            def branch(g, w, i, base):
                for m in range(KD):
                    if base + m >= 2:
                        act.wait_ge(gate_used, base + m - 1)
                    for j, (t0, n) in enumerate(HALF):
                        b = tile((g, m), j)
                        act.activation(stage[:, m % 2, t0:t0 + n], ps[:, b, :], ACT.Sigmoid,
                                       bias=v("b_gate", KD * i + m)).then_inc(gate_done, 1)
                    split_behind((g, m))
                    for j, (t0, n) in enumerate(HALF):
                        b = tile((w, m), j)
                        act.copy(y_s[:, m % 2, t0:t0 + n], ps[:, b, :]).then_inc(y_done, 1)
                    split_behind((w, m))

            branch("g0", "wa", 0, 0)
            act.wait_ge(gate_used, KD)
            for m in range(4):
                if m >= 1:
                    act.wait_ge(brlo_done, 8 + m)
                for slot, kind, chunks in ((0, "cc", FULL), (1, "cu", FULL)):
                    for j, (t0, w) in enumerate(chunks):
                        b = tile((kind, m), j)
                        act.copy(cv[:, slot, t0:t0 + w], ps[:, b, 0:w]).then_inc(cv_in, 1)
                    split_behind((kind, m))
                act.wait_ge(cv_v, m + 1)
                for tap, slot in ((0, 3), (1, 4), (2, 0)):
                    o = META - 2 + tap
                    act.activation(cv[:, slot, 0:S], cv[:, 2, o:o + S], ACT.Copy, scale=v("conv_w", 4 * tap + m)).then_inc(cv_tap, 1)
                for j, (t0, w) in enumerate(HALF):
                    b = tile(("cb", m), j)
                    act.copy(cv[:, 5, t0:t0 + w], ps[:, b, 0:w]).then_inc(cv_in, 1)
                split_behind(("cb", m))
                act.wait_ge(cv_sum, m + 1)
                act.copy(br_hi[:, m, :], cv[:, 1, 0:S]).then_inc(brhi_done, 1)
            act.wait_ge(brlo_done, 12)
            branch("g2", "wc", 2, KD)
            act.wait_ge(gate_used, 2 * KD)
            def queries(b):
                act.wait_ge(q_load, 16 * (b + 1))
                if b >= 2:
                    act.wait_ge(pair_full, len(SCORES) + LOGITS_TO[2 * (b - 2) + 1])
                act.copy(q_hi[:, b % 2], q_f[:, :, :]).then_inc(qhi_done, 1)

            def exp(g, h):
                nk = block_keys(GROUPS[g][0])
                act.wait_ge(nm_done, 4 * g + h + 1)
                act.activation(logit[:, g % 2, h, 0:nk], logit[:, g % 2, h, 0:nk], ACT.Exp, bias=neg_max[:, g % 2, h:h + 1],
                               scale=ATTN_SCALE, accum_out=row_sum[:, g % 2, h:h + 1]).then_inc(exp_done, 1)

            for m in range(KD):
                store("g1", m, ACT.Sigmoid, g1_done, g1_store, g1_scratch, v("b_gate", KD + m))
                if m in (4, 6):
                    queries((m - 4) // 2)
                if m == 6:
                    for h in range(4):
                        exp(0, h)
            act.wait_ge(g1_store[0], 64)
            act.wait_ge(g1_store[1], 64)

            act.wait_ge(wlo_done, PANEL_AT["wb", 1] + 1)
            def high_part(g, r):
                n = (CHUNKS_TO[g - 1] if g else 0) + r
                k = META if r == GROUPS[g][0] + 1 else P
                act.wait_ge(trans_full, n + 1)
                if n >= 3:
                    act.wait_ge(pv_step, n - 2)
                act.copy(pt_hi[0:k, n % 3, :], ps[0:k, n % 3, :]).then_inc(pthi_done, 1)

            for g, (blk, hg) in enumerate(GROUPS):
                high_part(g, 0)
                high_part(g, 1)
                for r in range(blk + 2):
                    if r + 2 < blk + 2:
                        high_part(g, r + 2)
                    for h in heads_at(g + 1, r - 1):
                        exp(g + 1, h)
                for h in heads_at(g + 1, blk + 1):
                    exp(g + 1, h)
                act.wait_ge(pv_step, CHUNKS_TO[g])
                act.copy(x_hi[:, 4 * hg:4 * hg + 4, P * blk:P * blk + P],
                         ps[:, 3, :].rearrange("p (h t) -> p h t", h=4)).then_inc(ohi_done, 1)
                if hg == 0 and blk + 2 < NB:
                    queries(blk + 2)
            for m in range(KD - 1):
                split_behind(("wb", m))
            act.wait_ge(lin_full, TILE_AT[("wb", KD - 1), 1] + 1)
            for j, (t0, w) in enumerate(HALF):
                for m in range(KD):
                    act.wait_ge(m_acc, 2 * m + j + 1)
                    act.copy(x_hi[:, m, t0:t0 + w], mix[:, m, t0:t0 + w]).then_inc(mhi_done, 1)
                if j == 0:
                    split_behind(("wb", KD - 1))
            act.wait_ge(mlo_done, 2 * KD)

            def squares(i, m):
                if m >= 2:
                    act.wait_ge(acca_done, 7 * i + max(m - 2, 1))
                act.activation(n_sq[:, m % 2, 0, :], mix[:, m, :], ACT.Square).then_inc(sqa_done, 1)
                if i:
                    if m >= 2:
                        act.wait_ge(accb_done, max(m - 2, 1))
                    act.activation(n_sq[:, m % 2, 1, :], mix[:, m, :], ACT.Square, scale=v("final_g", m)).then_inc(sqb_done, 1)

            def tile2(key, j):
                act.wait_ge(lin_full, TICK2[key, j] + 1)
                return LIN_AT[key, j] % 3

            def up(key):
                n = UP_AT[key]
                act.wait_ge(up_full, UP_0 + n + 1)
                return 4 + n % 4

            def behind2(key):
                split(AT2[key] + 2)

            def memory_high_parts():
                for n in range(4):
                    b = up(("mem", n))
                    for c in range(2):
                        act.activation(memt_hi[:, 2 * n + c, :], ps[:, b, MEM * c:MEM * c + MEM], ACT.Copy, scale=v("mem_norm_g_2", 2 * n + c)).then_inc(memhi_done, 1)

            def memory_panel(n):
                kind, m = (("mk", 0), ("mk", 1), ("mv", 0), ("mv", 1))[n]
                b = tile2((kind, m), 0)
                if kind == "mk":
                    act.copy(mk_hi[:, m, :], ps[:, b, 0:MEM]).then_inc(mkhi_done, 1)
                else:
                    act.copy(mv_f[:, m, :], ps[:, b, 0:MEM]).then_inc(mvf_done, 1)
                behind2((kind, m))

            def norm(i):
                act.wait_ge(nst_step, 5 if i else 2)
                if i:
                    act.activation(nst[:, 4:6, :], nst[:, 1:4:2, :], ACT.Sqrt).then_inc(nrt_done, 1)
                else:
                    act.activation(nst[:, 4, :], nst[:, 1, :], ACT.Sqrt).then_inc(nrt_done, 1)
                for q in range(2 * KD):
                    if i and q in (1, 2, 4, 6):
                        memory_panel((1, 2, 4, 6).index(q))
                    m, (t0, w) = q % KD, HALF[q // KD]
                    act.wait_ge(xn_done if i else upper_free, (XN_0 if i else 0) + q + 1)
                    act.copy(x_hi[:, m, t0:t0 + w], n_st[:, q % 4, :]).then_inc(nhi_done, 1)

            for m in range(KD):
                for j, (t0, w) in enumerate(HALF):
                    b = tile(("wo", m), j)
                    act.copy(mix[:, m, t0:t0 + w], ps[:, b, :]).then_inc(h_done, 1)
                if m < KD - 1:
                    split_behind(("wo", m))
                act.wait_ge(h_done, 2 * m + 2)
                squares(0, m)
            split_behind(("wo", KD - 1))
            norm(0)

            def split_mlp(it, off, ticks):
                sl = (PB + off) % 2
                act.wait_ge(raw_load[sl], 16 * loads_of(it, off))
                act.wait_ge(lin_full, ticks)
                act.copy(w_hi[:, sl, :], w_raw[:, sl, :]).then_inc(whi_done, 1)

            def activations(it, par, first=False, between=None):
                at = L0 if first else gu_at(it, par)
                off = 0 if first else 3 * par - 1
                for h, (t0, w) in enumerate(HALF):
                    act.wait_ge(lin_full, at + (h + 1))
                    if not first:
                        act.wait_ge(af_done, 4 * it + 2 * par + (h - 1))
                    act.activation(silu_s[:, t0:t0 + w], ps[:, h, :], ACT.Silu).then_inc(silu_done, 1)
                split_mlp(it, off + 2, at + 2)
                if between is not None:
                    between()
                split_mlp(it, off + 3, at + 4)
                act.wait_ge(af_done, 4 * it + (2 * par + 2))
                act.copy(a_hi[:, par % 2, :], a_f[:, :]).then_inc(ahi_done, 1)

            activations(0, 0, first=True)
            act.wait_ge(mem_load, 16)
            for r in range(2):
                act.activation(mem_junk[:, r, :], mem_tok[:, r, :], ACT.Square, accum_out=mem_ss[:, r:r + 1]).then_inc(msq_done, 1)
            act.wait_ge(mst_step, 2)
            act.activation(mem_ss[:, :], mem_ss[:, :], ACT.Sqrt).then_inc(mrt_done, 1)
            with act.Fori(0, (FC - 2) // 2) as it:
                for par in range(2):
                    activations(it, par + 1)
                    split_mlp(it, 3 * par + 6, gu_at(it, par + 1) + 20)
            it_last = (FC - 2) // 2
            activations(it_last, 1, between=memory_high_parts)
            for m in range(KD):
                act.wait_ge(upper_free, 2 * KD + 16 * (FC - 2) + 2 * m + 2)
                squares(1, m)
            split_mlp(it_last, 6, L2)
            split_mlp(it_last, 7, L2)

            norm(1)

            def v_panel(m):
                for j, (t0, w) in enumerate(HALF):
                    b = tile2(("av", m), j)
                    act.activation(av_s[:, m, t0:t0 + w], ps[:, b, :], ACT.Gelu_apprx_tanh).then_inc(av_done, 1)
                behind2(("av", m))

            def u_panel(m):
                for j, (t0, w) in enumerate(HALF):
                    b = tile2(("au", m), j)
                    act.activation(yz[:, m, t0:t0 + w], ps[:, b, :], ACT.Gelu_apprx_tanh).then_inc(au_done, 1)
                behind2(("au", m))

            for m in range(2):
                u_panel(m)
            for n in range(16):
                r, h = n // 2, n % 2
                b = up(("x2", n))
                if r >= 4 and h == 0:
                    act.wait_ge(x2_store[r % 4], 16 * (r // 4))
                act.copy(x2_s[:, r % 4, BANK * h:BANK * h + BANK], ps[:, b, :]).then_inc(x2_copied, 1)
                if h:
                    act.wait_ge(x2_copied, X2_0 + n + 1)
                    act.dma_start(x2_scratch[P * r:P * r + P, :], x2_s[:, r % 4, :]).then_inc(x2_store[r % 4], 16)
            b = up(("wsp", 0))
            act.wait_ge(nlo_even, 2 * KD)
            act.wait_ge(nlo_odd, 2 * KD)
            act.copy(wt_hi[:, :, :], ps[:, b, :].rearrange("p (g t) -> p g t", g=4)).then_inc(wthi_done, 1)
            b = up(("rb", 0))
            act.copy(rb_s[:, :], ps[0:4, b, 0:SWA_SPAN]).then_inc(rb_done, 1)
            act.wait_ge(rb_done, RB_0 + 1)
            act.dma_start(rb_scratch, rb_s[:, :]).then_inc(rb_store, 16)
            b = up(("mvt", 0))
            act.copy(mv_hi[:, :, :], ps[:, b, :].rearrange("p (r d) -> p r d", r=2)).then_inc(mvthi_done, 1)
            for m in range(4):
                v_panel(m)
            act.wait_ge(c2_load, 7 * 16)
            act.copy(sink[:, :].rearrange("p (u c) -> p u c", u=2), sink_n[:, :].rearrange("p (c u) -> p u c", u=2)).then_inc(sink_done, 1)
            act.wait_ge(rb_store, 16)
            act.dma_start(btoe[:, :, :], bass.AP(tensor=rb_scratch.tensor, offset=0, ap=[[1, P], [SWA_SPAN, 4], [1, 2 * P]])).then_inc(rb_load, 16)

            def ln_root(n):
                act.wait_ge(ln_step, 6 * n + 6)
                act.activation(vrs[:, n % 2, :], vrs[:, n % 2, :], ACT.Sqrt).then_inc(lnrt_done, 1)

            for n in range(4):
                act.wait_ge(x2_store[n], 32)
            ln_root(0)
            for n in range(NB):
                if n in (3, 5):
                    u_panel((n + 1) // 2)
                if n + 1 < NB:
                    ln_root(n + 1)
                act.wait_ge(vn_done, VN_0 + 2 * n + 2)
                act.copy(vln_hi[:, n, :], vn_s[:, n % 2, :]).then_inc(vlnhi_done, 1)
            for n in range(2):
                b = up(("flip", n))
                act.copy(bias[:, n:n + 3:2, :], ps[:, b, :].rearrange("p (h k) -> p h k", h=2)).then_inc(bias_done, 1)
            for j, (t0, w) in enumerate(HALF):
                b = tile2(("sk", 0), j)
                for c in range(2):
                    act.copy(kd_f[DH * c:DH * c + DH, c, t0:t0 + w], ps[DH * c:DH * c + DH, b, :]).then_inc(skf_done, 1)
            behind2(("sk", 0))
            act.wait_ge(sp_done, SP_0 + 8)
            for j, (t0, w) in enumerate(HALF):
                b = tile2(("sv", 0), j)
                act.copy(sv_f[:, t0:t0 + w], ps[:, b, :]).then_inc(svf_done, 1)
            behind2(("sv", 0))
            for n in range(2):
                b = up(("svt", n))
                for u in range(2):
                    act.copy(vd_hi[:, 4 * n:4 * n + 4, :, DH * u:DH * u + DH],
                             ps[:, b, :].rearrange("p (b c d) -> p b c d", b=4, c=2)).then_inc(svhi_done, 1)
            for kind, hi, done in (("sq", sq_hi, sqhi_done), ("mq", mq_hi, mqhi_done)):
                for m in range(2):
                    for j, (t0, w) in enumerate(HALF):
                        b = tile2((kind, m), j)
                        act.copy(hi[:, m, t0:t0 + w], ps[:, b, :]).then_inc(done, 1)
                    behind2((kind, m))
            act.wait_ge(kd_copies, 32)
            act.copy(kd_hi[:, :, :], kd_f[:, :, :]).then_inc(kdhi_done, 1)
            act.wait_ge(kdlo_done, KDLO_0 + 1)
            act.wait_ge(svlo_done, SVLO_0 + 4)
            for m in range(4, 8):
                for j, (t0, w) in enumerate(HALF):
                    b = tile2(("z", m), j)
                    act.activation(yz[:, m, t0:t0 + w], ps[:, b, :], ACT.Silu).then_inc(zs_done, 1)
                behind2(("z", m))

            def exps2(n):
                blk, kind = UNITS2[n]
                k0 = P if n == 0 else 0
                act.wait_ge(nm2_done, NM2_0 + n + 1)
                if n >= 2 and kind:
                    act.wait_ge(pt_full, TURN_AT[n - 2, 1] + 1)
                for h in range(4):
                    src = ps[:, 4 + h // 2, 2 * P * (h % 2):2 * P * (h % 2) + 2 * P] if kind else p_s[:, n % 2, h, k0:2 * P]
                    act.activation(p_s[:, n % 2, h, k0:2 * P], src, ACT.Exp, bias=nm2[:, n % 2, h:h + 1], scale=DH ** -0.5 if kind else 1.0,
                                   accum_out=rs2[:, n % 2, h:h + 1]).then_inc(e2_done, 1)
                if not kind:
                    act.activation(se2[:, n % 2, :], se2[:, n % 2, :], ACT.Exp).then_inc(b_done, 1)

            exps2(0)
            for n in range(len(UNITS2)):
                for kc in key_chunks(n):
                    act.wait_ge(pt_full, TURN_AT[n, kc] + 1)
                    if n >= 1:
                        act.wait_ge(pv_full, PV_0 + n)
                    act.copy(p2_hi[:, kc, :], ps[:, 6 + kc, :]).then_inc(p2hi_done, 1)
                if n + 1 < len(UNITS2):
                    exps2(n + 1)
                m, j = n // 4, n % 4
                b = tile2(("z", m), j)
                if n >= 2 and n % 2 == 0:
                    act.wait_ge(zt_done, n // 2)
                act.copy(z_s[:, 2 * P * (n % 2):2 * P * (n % 2) + 2 * P], ps[:, b, 0:2 * P]).then_inc(zcopy_done, 1)
                if n % 2:
                    act.wait_ge(zcopy_done, ZCOPY_0 + n + 1)
                    act.activation(z_s[:, :], z_s[:, :], ACT.Silu).then_inc(zg_done, 1)
                if j == 3:
                    behind2(("z", m))
            act.wait_ge(zt_done, NB)
            for m in range(KD):
                if m == 4:
                    act.wait_ge(pvg_done, 2 * len(UNITS2))
                act.copy(x_hi[:, m, 0:S], yz[:, m, :]).then_inc(yhi_done, 1)
            for n in range(KD):
                behind2(("wout", n))
            for b in range(NB):
                act.wait_ge(lin_full, TICK2[("wout", KD - 1), b] + 1)
                act.copy(wy[:, b, :], ps[:, b, :]).then_inc(wy_done, 1)
            for b in range(NB):
                behind2(("wout", KD + b))
                act.wait_ge(wy_done, WY_0 + b + 1)
                if b >= 2:
                    act.wait_ge(wysq_done, WYSQ_0 + b - 1)
                act.activation(sq_junk[:, b % 2, :], wy[:, b, :], ACT.Square, accum_out=osum[:, 0, b:b + 1]).then_inc(wysq_done, 1)
            for b in range(NB):
                act.wait_ge(lin_full, TICK2[("wout", 2 * KD - 1), b] + 1)
                if b < 2:
                    act.wait_ge(wysq_done, WYSQ_0 + NB - 1 + b)
                else:
                    act.wait_ge(ysq_done, YSQ_0 + b - 1)
                act.activation(sq_junk[:, b % 2, :], ps[:, b, :], ACT.Square, accum_out=osum[:, 1, b:b + 1]).then_inc(ysq_done, 1)
                if b % 2:
                    act.wait_ge(os_step, 3 * (b // 2) + 3)
                    act.activation(osum[:, 2, b - 1:b + 1], osum[:, 2, b - 1:b + 1], ACT.Sqrt).then_inc(osrt_done, 1)

        @block.vector
        def _(dve):
            def bank(key, j):
                return TILE_AT[key, j] % 4

            dve.wait_ge(rb_const, 2)
            dve.memset(relb[32:33, :], NEG).then_inc(rb_const, 1)
            for gi, (t0, tiles, w) in enumerate(XGROUPS):
                k = tile_rows(tiles[0])
                a, z = tiles[0], tiles[-1] + 1
                dve.wait_ge(sq_done, z)
                dve.tensor_scalar(ss[0:k, a:z], ss[0:k, a:z], 1.0 / D, EPS, ALU.mult, ALU.add).then_inc(ms_done, 1)
                dve.wait_ge(ms_done, gi + 1)
                dve.reciprocal(rstd[0:k, a:z], ss[0:k, a:z]).then_inc(inv_done, 1)
                dve.wait_ge(rt_done, gi + 1)
                for r in tiles:
                    dve.tensor_scalar(x_tok[0:k, r, :], x_tok[0:k, r, :], rstd[0:k, r:r + 1], None, ALU.mult).then_inc(xs_done, 1)
            n = 0
            dve.wait_ge(vec_ready, 1)
            for t0, tiles, w in XGROUPS:
                for c in range(KD):
                    dve.wait_ge(xhi_done, n + 1)
                    dve.scalar_tensor_tensor(out=x_lo[:, c, t0:t0 + w], in0=ps[:, n % 4, 0:w], scalar=v("norm1_g", c),
                                             in1=x_hi[:, c, t0:t0 + w], op0=ALU.mult, op1=ALU.subtract).then_inc(xlo_done, 1)
                    n += 1
            for m in range(2):
                for j, (t0, w) in enumerate(HALF):
                    dve.wait_ge(qihi_done, 2 * m + j + 1)
                    dve.tensor_tensor(qi_lo[:, m, t0:t0 + w], ps[:, bank(("qi", m), j), :], qi_hi[:, m, t0:t0 + w],
                                      ALU.subtract).then_inc(qilo_done, 1)
            dve.wait_ge(kihi_done, 1)
            dve.tensor_tensor(ki_lo[:, :], ki_f[:, :], ki_hi[:, :], ALU.subtract).then_inc(kilo_done, 1)
            for j, (t0, w) in enumerate(FULL):
                dve.wait_ge(lin_full, TILE_AT[("csum", 0), j] + 1)
                dve.tensor_scalar(c_rs[:, t0:t0 + w], ps[:, bank(("csum", 0), j), 0:w], 1.0 / P, EPS, ALU.mult, ALU.add).then_inc(cms_done, 1)
            dve.wait_ge(cms_done, 3)
            dve.reciprocal(c_rs[:, :], c_rs[:, :]).then_inc(cinv_done, 1)
            dve.wait_ge(crt_done, 1)
            dve.wait_ge(craw_done, 3)
            dve.scalar_tensor_tensor(out=c_sq[:, :], in0=c_raw[:, :], scalar=v("kv_norm_g", 0), in1=c_rs[:, :],
                                     op0=ALU.mult, op1=ALU.mult).then_inc(cn_done, 1)
            dve.wait_ge(chi_done, 1)
            dve.tensor_tensor(c_lo[:, :], c_sq[:, :], c_hi[:, :], ALU.subtract).then_inc(clo_done, 1)
            for j, (t0, tiles, w) in enumerate(XGROUPS):
                k = tile_rows(tiles[0])
                dve.wait_ge(ckhi_done, j + 1)
                dve.tensor_tensor(ck_lo[0:k, tiles[0]:tiles[-1] + 1, :],
                                  ps[0:k, bank(("ctok", 0), j), 0:P * len(tiles)].rearrange("p (r d) -> p r d", d=P),
                                  ck_hi[0:k, tiles[0]:tiles[-1] + 1, :], ALU.subtract).then_inc(cklo_done, 1)
            dve.wait_ge(wtok_done, 1)
            for n, (blk, k0, w, hg) in enumerate(SCORES):
                a = SC_AT[blk] + k0
                for r in range(4):
                    h = 4 * hg + r
                    dve.wait_ge(relu_done, 4 * n + r + 1)
                    if h == 0:
                        dve.tensor_scalar(score[:, a:a + w], relu_s[:, r, 0:w], w_tok[:, blk, h:h + 1], None, ALU.mult).then_inc(score_acc, 1)
                    else:
                        dve.wait_ge(score_acc, 4 * n + r)
                        dve.scalar_tensor_tensor(out=score[:, a:a + w], in0=relu_s[:, r, 0:w], scalar=w_tok[:, blk, h:h + 1],
                                                 in1=score[:, a:a + w], op0=ALU.mult, op1=ALU.add).then_inc(score_acc, 1)

            def keys(blk):
                return score[:, SC_AT[blk]:SC_AT[blk + 1]]

            def last(blk):
                return score[:, SC_AT[blk + 1] - P:SC_AT[blk + 1]]

            dve.wait_ge(score_acc, 4 * len(SCORES))
            dve.wait_ge(const_ready, 5)
            dve.memset(keys(0), 0.0).then_inc(topk_step, 1)
            dve.wait_ge(topk_step, 1)
            dve.tensor_tensor(last(0), last(0), causal[:, :], ALU.min).then_inc(mask_ready, 1)
            steps = 1
            for blocks in TOPK_PAIRS:
                nb = len(blocks)
                for blk in blocks:
                    dve.tensor_tensor(last(blk), last(blk), causal[:, :], ALU.add).then_inc(topk_step, 1)
                steps += nb
                with dve.Fori(0, TOP_K // 32) as i:
                    for r in range(4):
                        done = steps + 2 * nb * (4 * i + r)
                        for a, blk in enumerate(blocks):
                            dve.wait_ge(topk_step, done - nb + a + 1)
                            dve.memset(turn[:, a:a + 1], 0.0)
                            dve.max(out=best[:, a, :], in_=keys(blk)).then_inc(topk_step, 1)
                        for a, blk in enumerate(blocks):
                            dve.wait_ge(topk_step, done + a + 1)
                            dve.memset(turn[:, 2 + a:3 + a], 0.0)
                            dve.match_replace(out=keys(blk), in_to_replace=best[:, a, :], in_values=keys(blk), imm_value=SENT).then_inc(topk_step, 1)
                steps += 2 * nb * (TOP_K // 8)
                for a, blk in enumerate(blocks):
                    dve.wait_ge(topk_step, steps)
                    dve.tensor_scalar(keys(blk), keys(blk), SENT, FILL, ALU.not_equal, ALU.mult).then_inc(topk_step, 1)
                    steps += 1
                    dve.wait_ge(topk_step, steps)
                    dve.tensor_tensor(last(blk), last(blk), causal[:, :], ALU.min).then_inc(mask_ready, 1)

            def mask(g, h):
                blk, hg = GROUPS[g]
                ncp = len(pieces(blk))
                base = LOGITS_TO[g - 1] if g else 0
                if g >= 2:
                    dve.wait_ge(trans_full, CHUNKS_TO[g - 2])
                dve.wait_ge(mask_ready, MASK_AT[blk] + 1)
                for pc, (k0, nch, w) in enumerate(pieces(blk)):
                    n = base + h * ncp + pc
                    a = SC_AT[blk] + k0
                    dve.wait_ge(pair_full, len(SCORES) + n + 1)
                    if pc:
                        dve.wait_ge(masked, n)
                    dve.tensor_tensor_reduce(wide(logit[:, g % 2, h, k0:k0 + nch * w], nch), pair(n, nch, w),
                                             wide(score[:, a:a + nch * w], nch), 1.0, row_max[:, g % 2, 4 + h:5 + h] if pc else SENT,
                                             ALU.add, ALU.max, row_max[:, g % 2, h:h + 1] if pc == ncp - 1 else row_max[:, g % 2, 4 + h:5 + h]).then_inc(masked, 1)
                dve.wait_ge(masked, base + (h + 1) * ncp)
                dve.tensor_scalar(neg_max[:, g % 2, h:h + 1], row_max[:, g % 2, h:h + 1], -ATTN_SCALE, None, ALU.mult).then_inc(nm_done, 1)

            def probabilities(g, h):
                nk = block_keys(GROUPS[g][0])
                dve.wait_ge(exp_done, 4 * g + h + 1)
                dve.reciprocal(inv_sum[:, g % 2, h:h + 1], row_sum[:, g % 2, h:h + 1]).then_inc(inv_step, 1)
                if h:
                    dve.wait_ge(inv_step, 4 * g + h + 1)
                    dve.tensor_scalar(logit[:, g % 2, h, 0:nk], logit[:, g % 2, h, 0:nk], inv_sum[:, g % 2, h:h + 1], None, ALU.mult).then_inc(norm_done, 1)

            def low_part(g, r):
                n = (CHUNKS_TO[g - 1] if g else 0) + r
                k = META if r == GROUPS[g][0] + 1 else P
                dve.wait_ge(pthi_done, n + 1)
                dve.tensor_tensor(pt_lo[0:k, n % 3, :], ps[0:k, n % 3, :], pt_hi[0:k, n % 3, :], ALU.subtract).then_inc(ptlo_done, 1)

            for h in range(4):
                mask(0, h)
            for h in range(4):
                probabilities(0, h)
            for g, (blk, hg) in enumerate(GROUPS):
                low_part(g, 0)
                low_part(g, 1)
                for r in range(blk + 2):
                    if r + 2 < blk + 2:
                        low_part(g, r + 2)
                    for h in heads_at(g + 1, r):
                        mask(g + 1, h)
                    for h in heads_at(g + 1, r - 2):
                        probabilities(g + 1, h)
                dve.wait_ge(ohi_done, g + 1)
                dve.tensor_tensor(x_lo[:, 4 * hg:4 * hg + 4, P * blk:P * blk + P],
                                  ps[:, 3, :].rearrange("p (h t) -> p h t", h=4),
                                  x_hi[:, 4 * hg:4 * hg + 4, P * blk:P * blk + P], ALU.subtract).then_inc(olo_done, 1)
                for r in range(max(blk, 0), blk + 2):
                    for h in heads_at(g + 1, r):
                        probabilities(g + 1, h)
            dve.wait_ge(gate_used, 2 * KD)
            for m in range(KD):
                dve.wait_ge(g1_load[m % 2], 16 * (m // 2 + 1))
                for j, (t0, w) in enumerate(HALF):
                    n = 2 * m + j
                    dve.wait_ge(lin_full, TILE_AT[("wb", m), j] + 1)
                    if n >= 2:
                        dve.wait_ge(m_acc, n - 1)
                    dve.tensor_tensor(gy_s[:, n % 2, :], ps[:, bank(("wb", m), j), :], g1_s[:, m % 2, t0:t0 + w], ALU.mult).then_inc(gy_done, 1)
                    dve.wait_ge(gy_done, n + 1)
                    dve.tensor_tensor(mix[:, m, t0:t0 + w], mix[:, m, t0:t0 + w], gy_s[:, n % 2, :], ALU.add).then_inc(m_acc, 1)
            for j, (t0, w) in enumerate(HALF):
                for m in range(KD):
                    dve.wait_ge(mhi_done, KD * j + m + 1)
                    dve.tensor_tensor(x_lo[:, m, t0:t0 + w], mix[:, m, t0:t0 + w], x_hi[:, m, t0:t0 + w], ALU.subtract).then_inc(mlo_done, 1)

            def wide_rs(first):
                return ps[:, first:first + 2, :]

            def two(ap):
                return ap.rearrange("p (n w) -> p n w", n=2)

            def diagonal(which, out_):
                for b in range(NB):
                    dve.tensor_scalar(out_[:, P * b:P * b + P], ident[:, :], nst[:, which, b:b + 1], None, ALU.mult).then_inc(diag_done, 1)

            dve.wait_ge(sqa_done, KD)
            dve.wait_ge(acca_done, KD - 2)
            dve.tensor_tensor(n_acc[:, 0, :], n_acc[:, 0, :], n_sq[:, (KD - 1) % 2, 0, :], ALU.add).then_inc(acca_done, 1)
            dve.wait_ge(stat_full, 1)
            dve.tensor_scalar(nst[:, 0, :], ps[:, 4, 0:8], 1.0 / D, EPS, ALU.mult, ALU.add).then_inc(nst_step, 1)
            dve.wait_ge(nst_step, 1)
            dve.reciprocal(nst[:, 1, :], nst[:, 0, :]).then_inc(nst_step, 1)
            dve.wait_ge(nrt_done, 1)
            diagonal(4, n_diag)
            def ub(key):
                return 4 + UP_AT[key] % 4

            def lb(key, j):
                return LIN_AT[key, j] % 3

            def memory_low_part(m):
                dve.wait_ge(mkhi_done, MKHI_0 + m + 1)
                dve.tensor_tensor(mk_lo[:, m, :], ps[:, lb(("mk", m), 0), 0:MEM], mk_hi[:, m, :], ALU.subtract).then_inc(mklo_done, 1)

            def normed_chunks(i, gain, done, memory_at=()):
                def low(q):
                    m, (t0, w) = q % KD, HALF[q // KD]
                    dve.wait_ge(nhi_done, 2 * KD * i + q + 1)
                    dve.tensor_tensor(x_lo[:, m, t0:t0 + w], n_st[:, q % 4, :], x_hi[:, m, t0:t0 + w], ALU.subtract).then_inc(nlo_odd, 1)

                for q in range(2 * KD):
                    m, (t0, w) = q % KD, HALF[q // KD]
                    if q >= 4:
                        dve.wait_ge(nlo_odd if q % 2 else nlo_even, KD * i + (q - 4) // 2 + 1)
                    if q % KD == 0:
                        dve.wait_ge(rs_full, 2 * i + q // KD + 1)
                    dve.scalar_tensor_tensor(out=n_st[:, q % 4, :], in0=mix[:, m, t0:t0 + w], scalar=gain(m), in1=ps[:, 6 + q // KD, :],
                                             op0=ALU.mult, op1=ALU.mult).then_inc(done, 1)
                    if q % 2 == 0 and q:
                        low(q - 1)
                    if q in memory_at:
                        memory_low_part(memory_at[q])
                low(2 * KD - 1)

            normed_chunks(0, lambda m: v("norm2_g", m), upper_free)

            def gated_chunk(it, par, first=False):
                at = L0 if first else gu_at(it, par)
                for h, (t0, w) in enumerate(HALF):
                    dve.wait_ge(lin_full, at + (h + 3))
                    dve.wait_ge(silu_done, 4 * it + (2 * par + h + 1))
                    if not first:
                        dve.wait_ge(alo_done, 2 * it + par)
                    dve.tensor_tensor(a_f[:, t0:t0 + w], silu_s[:, t0:t0 + w], ps[:, 2 + h, :], ALU.mult).then_inc(af_done, 1)

            def sums(it, par, at, behind=None):
                for n in range(16):
                    m, (t0, w) = n // 2, HALF[n % 2]
                    dve.wait_ge(lin_full, at + (n + 1))
                    dve.wait_ge(upper_free, 32 * it + (16 * par + n + 2 * KD - 7))
                    dve.tensor_tensor(mix[:, m, t0:t0 + w], mix[:, m, t0:t0 + w], ps[:, 4 + n % 4, :], ALU.add).then_inc(upper_free, 1)
                    if behind is not None and n % 2:
                        behind(m - 1)

            def add_squares(m):
                if m < 1:
                    return
                dve.wait_ge(sqa_done, KD + m + 1)
                if m >= 2:
                    dve.wait_ge(acca_done, 7 + m - 1)
                dve.tensor_tensor(n_acc[:, 0, :], n_sq[:, 0, 0, :] if m == 1 else n_acc[:, 0, :], n_sq[:, m % 2, 0, :], ALU.add).then_inc(acca_done, 1)

            def memory_low():
                for n in range(4):
                    for c in range(2):
                        dve.wait_ge(memhi_done, MEMHI_0 + 2 * n + 2)
                        dve.scalar_tensor_tensor(out=memt_lo[:, 2 * n + c, :], in0=ps[:, ub(("mem", n)), MEM * c:MEM * c + MEM], scalar=v("mem_norm_g_2", 2 * n + c),
                                                 in1=memt_hi[:, 2 * n + c, :], op0=ALU.mult, op1=ALU.subtract).then_inc(memlo_done, 1)

            gated_chunk(0, 0, first=True)
            dve.wait_ge(msq_done, 2)
            dve.tensor_scalar(mem_ss[:, :], mem_ss[:, :], 1.0 / D, EPS, ALU.mult, ALU.add).then_inc(mst_step, 1)
            dve.wait_ge(mst_step, 1)
            dve.reciprocal(mem_ss[:, :], mem_ss[:, :]).then_inc(mst_step, 1)
            dve.wait_ge(mrt_done, 1)
            for r in range(2):
                dve.tensor_scalar(mem_tok[:, r, :], mem_tok[:, r, :], mem_ss[:, r:r + 1], None, ALU.mult).then_inc(ms_scaled, 1)
            dve.tensor_tensor(gfg[:, :], vec[:, VEC["final_g"]:VEC["final_g"] + KD], vec[:, VEC["pre_norm_g_2"]:VEC["pre_norm_g_2"] + KD], ALU.mult).then_inc(mst_step, 1)
            with dve.Fori(0, (FC - 2) // 2) as it:
                for par in range(2):
                    gated_chunk(it, par + 1)
                    sums(it, par, gu_at(it, par + 1) + 4)
            it_last = (FC - 2) // 2
            memory_low()
            gated_chunk(it_last, 1)
            sums(it_last, 0, L2 - 16, add_squares)
            add_squares(KD - 1)

            dve.wait_ge(stat_full, 2)
            dve.tensor_scalar(nst[:, 0, :], ps[:, 4, 0:8], 1.0 / D, EPS, ALU.mult, ALU.add).then_inc(nst_step, 1)
            dve.wait_ge(nst_step, 3)
            dve.reciprocal(nst[:, 1, :], nst[:, 0, :]).then_inc(nst_step, 1)
            dve.wait_ge(nst_step, 4)
            dve.scalar_tensor_tensor(out=nst[:, 2, :], in0=ps[:, 4, 8:16], scalar=1.0 / D, in1=nst[:, 1, :], op0=ALU.mult, op1=ALU.mult).then_inc(mst_step, 1)
            dve.wait_ge(mst_step, 4)
            dve.tensor_scalar(nst[:, 2, :], nst[:, 2, :], EPS, None, ALU.add).then_inc(mst_step, 1)
            dve.wait_ge(mst_step, 5)
            dve.reciprocal(nst[:, 3, :], nst[:, 2, :]).then_inc(nst_step, 1)
            dve.wait_ge(nrt_done, 2)
            dve.tensor_tensor(nst[:, 5, :], nst[:, 4, :], nst[:, 5, :], ALU.mult).then_inc(mst_step, 1)
            dve.wait_ge(mst_step, 6)
            diagonal(5, n_diag)
            diagonal(4, n_diag2)
            normed_chunks(1, lambda m: gfg[:, m:m + 1], xn_done, {2: 0, 4: 1})
            for m in range(KD):
                if m == 0:
                    dve.wait_ge(xn_done, XN_0 + 2 * KD)
                    dve.wait_ge(rs_full, 6)
                dve.scalar_tensor_tensor(out=two(mix[:, m, :]), in0=two(mix[:, m, :]), scalar=v("final_g", m), in1=wide_rs(4),
                                         op0=ALU.mult, op1=ALU.mult).then_inc(x2_done, 1)

            dve.wait_ge(wthi_done, WTHI_0 + 1)
            dve.tensor_tensor(wt_lo[:, :, :], ps[:, ub(("wsp", 0)), :].rearrange("p (g t) -> p g t", g=4), wt_hi[:, :, :], ALU.subtract).then_inc(wtlo_done, 1)

            dve.wait_ge(mvthi_done, MVTHI_0 + 1)
            dve.tensor_tensor(mv_lo[:, :, :], ps[:, ub(("mvt", 0)), :].rearrange("p (r d) -> p r d", r=2), mv_hi[:, :, :], ALU.subtract).then_inc(mvtlo_done, 1)

            def ln_stats(n):
                b = ub(("av", n))
                dve.wait_ge(up_full, UP_0 + UP_AT["av", n] + 1)
                if n >= 2:
                    dve.wait_ge(vn_sub, VSUB_0 + 4 * (n - 1))
                for g in range(4):
                    dve.bn_stats(bst[:, n % 2, g, :], ps[:, b, P * g:P * g + P]).then_inc(ln_step, 1)
                for g in range(4):
                    dve.wait_ge(ln_step, 6 * n + g + 1)
                    dve.bn_aggr(bag[:, n % 2, g, :], bst[:, n % 2, g, :]).then_inc(mx_step if g < 3 else vn_ready, 1)
                dve.wait_ge(vn_ready, n + 1)
                dve.tensor_scalar(vrs[:, n % 2, :], bag[:, n % 2, :, 1], EPS, None, ALU.add).then_inc(ln_step, 1)
                dve.wait_ge(ln_step, 6 * n + 5)
                dve.reciprocal(vrs[:, n % 2, :], vrs[:, n % 2, :]).then_inc(ln_step, 1)

            def ln_apply(n):
                b = ub(("av", n))
                dve.wait_ge(lnrt_done, LNRT_0 + n + 1)
                if n >= 2:
                    dve.wait_ge(vlnlo_done, VLNLO_0 + n - 1)
                for g in range(4):
                    dve.tensor_scalar(vn_s[:, n % 2, P * g:P * g + P], ps[:, b, P * g:P * g + P], bag[:, n % 2, g, 0:1], vrs[:, n % 2, g:g + 1],
                                      ALU.subtract, ALU.mult).then_inc(vn_sub, 1)
                dve.wait_ge(vn_sub, VSUB_0 + 4 * n + 4)
                dve.tensor_tensor(vn_s[:, n % 2, :], vn_s[:, n % 2, :], vgb[:, :], ALU.mult).then_inc(vn_done, 1)
                dve.wait_ge(vn_done, VN_0 + 2 * n + 1)
                dve.tensor_tensor(vn_s[:, n % 2, :], vn_s[:, n % 2, :], vbb[:, :], ALU.add).then_inc(vn_done, 1)

            dve.wait_ge(c2_load, 7 * 16)
            dve.wait_ge(nlo_even, 2 * KD)
            ln_stats(0)
            for n in range(NB):
                if n + 1 < NB:
                    ln_stats(n + 1)
                ln_apply(n)
            dve.wait_ge(au_done, AU_0 + 8)
            dve.wait_ge(vlnlo_done, VLNLO_0 + NB)
            for n in range(8):
                g, h = n // 2, n % 2
                dve.wait_ge(up_full, UP_0 + UP_AT["sp", n] + 1)
                if n >= 2:
                    dve.wait_ge(sp_done, SP_0 + n - 1)
                t = vn_s[:, n % 2, :].rearrange("p (b t) -> p b t", b=4)
                dve.tensor_tensor(t, ps[:, ub(("sp", n)), :].rearrange("p (b t) -> p b t", b=4),
                                  bsp[:, g, :].unsqueeze(1).broadcast_to([P, 4, P]), ALU.add).then_inc(sp_sum, 1)
                dve.wait_ge(sp_sum, SPSUM_0 + n + 1)
                dve.tensor_tensor(yz[:, g, BANK * h:BANK * h + BANK], yz[:, g, BANK * h:BANK * h + BANK], vn_s[:, n % 2, :], ALU.mult).then_inc(sp_done, 1)
            for n in range(2):
                for u in range(2):
                    dve.wait_ge(svhi_done, SVHI_0 + 2 * n + 2)
                    o = vd_hi[:, 4 * n:4 * n + 4, :, DH * u:DH * u + DH]
                    dve.tensor_tensor(vd_lo[:, 4 * n:4 * n + 4, :, DH * u:DH * u + DH],
                                      ps[:, ub(("svt", n)), :].rearrange("p (b c d) -> p b c d", b=4, c=2), o, ALU.subtract).then_inc(svlo_done, 1)
            for kind, hi, lo, hi_done, before, lo_done in (("sq", sq_hi, sq_lo, sqhi_done, SQHI_0, sqlo_done), ("mq", mq_hi, mq_lo, mqhi_done, MQHI_0, mqlo_done)):
                for m in range(2):
                    for j, (t0, w) in enumerate(HALF):
                        dve.wait_ge(hi_done, before + 2 * m + j + 1)
                        dve.tensor_tensor(lo[:, m, t0:t0 + w], ps[:, lb((kind, m), j), :], hi[:, m, t0:t0 + w], ALU.subtract).then_inc(lo_done, 1)

            dve.wait_ge(bias_done, BIAS_0 + 2)
            dve.wait_ge(sink_done, 1)
            MX = 3 * NB

            def maxima(n):
                blk, kind = UNITS2[n]
                s_ = n % 2
                k0 = P if n == 0 else 0
                first = MX + 4 * (n // 2) + (3 if kind else 0)
                dve.wait_ge(lg_full, LG_0 + n + 1)
                lg = ps[:, 4:6, :].rearrange("p u (c k) -> p (u c) k", c=2)
                if kind:
                    dve.tensor_reduce(mx2[:, s_, :], lg, mybir.AxisListType.X, ALU.max).then_inc(mx_step, 1)
                    dve.wait_ge(mx_step, first + 1)
                    dve.tensor_scalar(nm2[:, s_, :], mx2[:, s_, :], -(DH ** -0.5), None, ALU.mult).then_inc(nm2_done, 1)
                    return
                if n >= 2:
                    dve.wait_ge(pt_full, TURN_AT[n - 2, 1] + 1)
                dve.scalar_tensor_tensor(out=p_s[:, s_, :, k0:2 * P], in0=lg[:, :, k0:2 * P], scalar=DH ** -0.5, in1=bias[:, :, k0:2 * P],
                                         op0=ALU.mult, op1=ALU.add).then_inc(mx_step, 1)
                dve.wait_ge(mx_step, first + 1)
                dve.tensor_reduce(mx2[:, s_, :], p_s[:, s_, :, k0:2 * P], mybir.AxisListType.X, ALU.max).then_inc(mx_step, 1)
                dve.wait_ge(mx_step, first + 2)
                dve.tensor_tensor(mx2[:, s_, :], mx2[:, s_, :], sink[:, :], ALU.max).then_inc(mx_step, 1)
                dve.wait_ge(mx_step, first + 3)
                dve.tensor_tensor(se2[:, s_, :], sink[:, :], mx2[:, s_, :], ALU.subtract).then_inc(mx_step2, 1)
                dve.tensor_scalar(nm2[:, s_, :], mx2[:, s_, :], -1.0, None, ALU.mult).then_inc(nm2_done, 1)

            def normed(n):
                blk, kind = UNITS2[n]
                s_ = n % 2
                k0 = P if n == 0 else 0
                dve.wait_ge(e2_done, E2_0 + 4 * n + 4)
                if not kind:
                    dve.wait_ge(b_done, blk + 1)
                    dve.tensor_tensor(rs2[:, s_, :], rs2[:, s_, :], se2[:, s_, :], ALU.add).then_inc(pn_step, 1)
                    dve.wait_ge(pn_step, 3 * blk + 1)
                dve.reciprocal(rs2[:, s_, :], rs2[:, s_, :]).then_inc(pn_step, 1)
                dve.wait_ge(pn_step, 3 * blk + 2 + kind)
                for h in range(4):
                    dve.tensor_scalar(p_s[:, s_, h, k0:2 * P], p_s[:, s_, h, k0:2 * P], rs2[:, s_, h:h + 1], None, ALU.mult).then_inc(pn_done, 1)

            maxima(0)
            normed(0)
            dve.wait_ge(zs_done, ZS_0 + 8)
            for n, (blk, kind) in enumerate(UNITS2):
                if n + 1 < len(UNITS2):
                    maxima(n + 1)
                for kc in key_chunks(n):
                    t = TURN_AT[n, kc]
                    dve.wait_ge(p2hi_done, P2HI_0 + t + 1)
                    if n >= 1:
                        dve.wait_ge(pv_full, PV_0 + n)
                    dve.tensor_tensor(p2_lo[:, kc, :], ps[:, 6 + kc, :], p2_hi[:, kc, :], ALU.subtract).then_inc(p2lo_done, 1)
                if n + 1 < len(UNITS2):
                    normed(n + 1)
                if n % 2:
                    m, t0 = n // 4, BANK * (n // 2 % 2)
                    dve.wait_ge(zg_done, n // 2 + 1)
                    dve.tensor_tensor(yz[:, m, t0:t0 + BANK], yz[:, m, t0:t0 + BANK], z_s[:, :], ALU.mult).then_inc(zt_done, 1)
                dve.wait_ge(pv_full, PV_0 + n + 1)
                o = ps[:, 3, :].rearrange("p (c u t) -> p c u t", c=2, u=2)
                for u in range(2):
                    y = yz[DH * u:DH * u + DH, 4 + 2 * kind:6 + 2 * kind, P * blk:P * blk + P]
                    dve.tensor_tensor(y, y, o[DH * u:DH * u + DH, :, u, :], ALU.mult).then_inc(pvg_done, 1)
            for m in range(0, KD, 2):
                dve.wait_ge(yhi_done, YHI_0 + m + 1)
                dve.tensor_tensor(x_lo[:, m, 0:S], yz[:, m, :], x_hi[:, m, 0:S], ALU.subtract).then_inc(yloa_done, 1)
            dve.wait_ge(pg_load, 16)
            dve.wait_ge(x2_load, 16)
            for q in range(NB // 2):
                a, z = 2 * q, 2 * q + 2
                dve.wait_ge(ysq_done, YSQ_0 + z)
                dve.wait_ge(wysq_done, WYSQ_0 + z)
                dve.tensor_tensor(osum[:, 2, a:z], osum[:, 0, a:z], osum[:, 1, a:z], ALU.add).then_inc(os_step, 1)
                dve.wait_ge(os_step, 3 * q + 1)
                dve.tensor_scalar(osum[:, 2, a:z], osum[:, 2, a:z], 1.0 / D, EPS, ALU.mult, ALU.add).then_inc(os_step, 1)
                dve.wait_ge(os_step, 3 * q + 2)
                dve.reciprocal(osum[:, 2, a:z], osum[:, 2, a:z]).then_inc(os_step, 1)
                dve.wait_ge(osrt_done, q + 1)
                dve.wait_ge(ylob_done, YLOB_0 + 4)
                for b in range(a, z):
                    if b >= 4:
                        dve.wait_ge(o_store[b % 4], 16)
                    dve.scalar_tensor_tensor(out=o_s[:, b % 4, 0:BANK], in0=wy[:, b, :], scalar=osum[:, 2, b:b + 1], in1=pg[:, 0:BANK],
                                             op0=ALU.mult, op1=ALU.mult).then_inc(on_done, 1)
                    dve.scalar_tensor_tensor(out=o_s[:, b % 4, BANK:D], in0=ps[:, b, :], scalar=osum[:, 2, b:b + 1], in1=pg[:, BANK:D],
                                             op0=ALU.mult, op1=ALU.mult).then_inc(on_done, 1)
                    dve.wait_ge(on_done, 2 * b + 2)
                    dve.tensor_tensor(o_s[:, b % 4, BANK:D], o_s[:, b % 4, BANK:D], x2_tok[:, b, BANK:D], ALU.add).then_inc(oa_done, 1)

        @block.gpsimd
        def _(pool):
            pool.memset(ident[:, :], 0.0).then_inc(const_ready, 1)
            pool.memset(ones[:, :], 1.0).then_inc(const_ready, 1)
            pool.memset(causal[:, :], 0.0).then_inc(const_ready, 1)
            pool.memset(anti[:, :], 0.0).then_inc(rb_const, 1)
            pool.memset(relb[:, :], 0.0).then_inc(rb_const, 1)
            pool.wait_ge(const_ready, 3)
            pool.affine_select(out=ident[:, :], in_=ident[:, :], compare_op=ALU.not_equal, fill=1.0, base=0,
                               pattern=[[-1, P]], channel_multiplier=1).then_inc(const_ready, 1)
            pool.affine_select(out=causal[:, :], in_=causal[:, :], compare_op=ALU.is_ge, fill=FILL, base=0,
                               pattern=[[-1, P]], channel_multiplier=1).then_inc(const_ready, 1)

            pool.wait_ge(rb_const, 2)
            pool.affine_select(out=anti[:, :], in_=anti[:, :], compare_op=ALU.not_equal, fill=1.0, base=1 - P,
                               pattern=[[1, P]], channel_multiplier=1).then_inc(rb_const, 1)

            def split(p):
                if p >= PB2 + len(PANELS2):
                    return
                pool.wait_ge(whi_done, p + 1)
                n = width(p)
                pool.tensor_tensor(w_lo[:, p % 2, 0:n], w_raw[:, p % 2, 0:n], w_hi[:, p % 2, 0:n], ALU.subtract).then_inc(wlo_done, 1)

            def split_behind(key):
                split(PANEL_AT[key] + 2)

            split(0)
            split(1)
            split_behind(("c", 0))
            split_behind(("kw", 0))
            split_behind(("qi", 0))
            split_behind(("qi", 1))
            def sums(g):
                pool.wait_ge(u_done, 3 * (g + 1))
                if g >= 1:
                    pool.wait_ge(pooled_done, g)
                src, shift = u_s[:, g % 2], 1
                for i in range(g + 1):
                    dst, lead = sum_s[:, i % 2], 2 * shift - 1
                    if i:
                        pool.wait_ge(pool_step, SUMS_AT[g] + i)
                    pool.tensor_tensor(dst[:, lead:T], src[:, lead:T], src[:, lead - shift:T - shift], ALU.add).then_inc(pool_step, 1)
                    src, shift = dst, 2 * shift

            def less_itself(g):
                mean = sum_s[:, (g + 1) % 2, 0:S]
                pool.wait_ge(pool_step, SUMS_AT[g] + g + 1)
                pool.tensor_scalar(mean, sum_s[:, g % 2, META:T], 1.0 / 2 ** (g + 1), None, ALU.mult).then_inc(pool_step, 1)
                pool.wait_ge(pool_step, SUMS_AT[g] + g + 2)
                pool.tensor_tensor(mean, mean, u_s[:, g % 2, META:T], ALU.subtract).then_inc(pool_sub, 1)

            def pooled_parts(g):
                mean = sum_s[:, (g + 1) % 2, 0:S]
                if g == 1:
                    pool.wait_ge(cn_done, 1)
                if g == 2:
                    pool.wait_ge(cklo_done, 3)
                    pool.wait_ge(clo_done, 1)
                pool.wait_ge(pool_sub, g + 1)
                pool.tensor_copy(pool_hi[:, g, :], mean).then_inc(pool_step, 1)
                pool.wait_ge(pool_step, SUMS_AT[g] + g + 3)
                pool.tensor_tensor(pool_lo[:, g, :], mean, pool_hi[:, g, :], ALU.subtract).then_inc(pooled_done, 1)

            SUMS_AT = [sum(g + 3 for g in range(n)) for n in range(4)]
            split_behind(("u", 0))
            sums(0)
            less_itself(0)
            split_behind(("u", 1))
            pooled_parts(0)
            sums(1)
            split_behind(("u", 2))
            less_itself(1)
            split_behind(("u", 3))
            pooled_parts(1)
            split_behind(("q", 0))
            sums(2)
            split_behind(("q", 1))
            less_itself(2)
            split_behind(("q", 2))
            pooled_parts(2)
            split_behind(("q", 3))
            sums(3)
            split_behind(("q", 4))
            less_itself(3)
            split_behind(("q", 5))
            pooled_parts(3)
            split_behind(("q", 6))
            split_behind(("q", 7))
            for g in range(4):
                for j, (t0, w) in enumerate(HALF):
                    n = 2 * g + j
                    pool.wait_ge(brhi_done, n + 1)
                    pool.tensor_tensor(br_lo[:, g, t0:t0 + w], mix_s[:, n % 2, :], br_hi[:, g, t0:t0 + w], ALU.subtract).then_inc(brlo_done, 1)

            split_behind(("poolw", 0))

            def branch(g, w, base):
                for m in range(KD):
                    split_behind((g, m))
                    split_behind((w, m))
                    pool.wait_ge(gate_done, 2 * (base + m + 1))
                    pool.wait_ge(y_done, 2 * (base + m + 1))
                    if base == 0:
                        pool.tensor_tensor(mix[:, m, :], stage[:, m % 2, :], y_s[:, m % 2, :], ALU.mult).then_inc(gate_used, 1)
                        continue
                    pool.tensor_tensor(y_s[:, m % 2, :], stage[:, m % 2, :], y_s[:, m % 2, :], ALU.mult).then_inc(gated, 1)
                    pool.wait_ge(gated, m + 1)
                    pool.tensor_tensor(mix[:, m, :], mix[:, m, :], y_s[:, m % 2, :], ALU.add).then_inc(gate_used, 1)

            branch("g0", "wa", 0)
            for m in range(4):
                split_behind(("cc", m))
                split_behind(("cu", m))
                pool.wait_ge(cv_in, 8 * m + 6)
                pool.tensor_tensor(cv[:, 2, :], cv[:, 0, :], cv[:, 1, :], ALU.mult).then_inc(cv_v, 1)
                pool.wait_ge(cv_tap, 3 * m + 3)
                pool.tensor_tensor(cv[:, 3, 0:S], cv[:, 3, 0:S], cv[:, 4, 0:S], ALU.add).then_inc(cv_step, 1)
                pool.wait_ge(cv_step, 2 * m + 1)
                pool.tensor_tensor(cv[:, 3, 0:S], cv[:, 3, 0:S], cv[:, 0, 0:S], ALU.add).then_inc(cv_step, 1)
                split_behind(("cb", m))
                pool.wait_ge(cv_step, 2 * m + 2)
                pool.wait_ge(cv_in, 8 * m + 8)
                pool.tensor_tensor(cv[:, 1, 0:S], cv[:, 3, 0:S], cv[:, 5, 0:S], ALU.mult).then_inc(cv_sum, 1)
                pool.wait_ge(brhi_done, 8 + m + 1)
                pool.tensor_tensor(br_lo[:, m, :], cv[:, 1, 0:S], br_hi[:, m, :], ALU.subtract).then_inc(brlo_done, 1)
            branch("g2", "wc", KD)
            def queries(b):
                pool.wait_ge(qhi_done, b + 1)
                pool.tensor_tensor(q_lo[:, b % 2], q_f[:, :, :], q_hi[:, b % 2], ALU.subtract).then_inc(qlo_done, 1)

            def probabilities(g):
                nk = block_keys(GROUPS[g][0])
                pool.wait_ge(inv_step, 4 * g + 1)
                pool.tensor_scalar(logit[:, g % 2, 0, 0:nk], logit[:, g % 2, 0, 0:nk], inv_sum[:, g % 2, 0:1], None, ALU.mult).then_inc(pnorm_done, 1)

            for m in range(KD):
                split_behind(("g1", m))
                if m in (4, 6):
                    queries((m - 4) // 2)
            probabilities(0)
            for g, (blk, hg) in enumerate(GROUPS):
                if g + 1 < len(GROUPS):
                    probabilities(g + 1)
                if hg == 0 and blk + 2 < NB:
                    queries(blk + 2)
            for m in range(KD):
                split_behind(("wb", m))
            def behind2(key):
                split(AT2[key] + 2)

            def low_parts(i):
                for q in range(0, 2 * KD, 2):
                    if i and q in (2, 4, 6, 8):
                        behind2((("mk", 0), ("mk", 1), ("mv", 0), ("mv", 1))[q // 2 - 1])
                    m, (t0, w) = q % KD, HALF[q // KD]
                    pool.wait_ge(nhi_done, 2 * KD * i + q + 1)
                    pool.tensor_tensor(x_lo[:, m, t0:t0 + w], n_st[:, q % 4, :], x_hi[:, m, t0:t0 + w], ALU.subtract).then_inc(nlo_even, 1)

            for m in range(KD):
                split_behind(("wo", m))
                if 1 <= m < KD - 1:
                    pool.wait_ge(sqa_done, m + 1)
                    if m >= 2:
                        pool.wait_ge(acca_done, m - 1)
                    pool.tensor_tensor(n_acc[:, 0, :], n_sq[:, 0, 0, :] if m == 1 else n_acc[:, 0, :], n_sq[:, m % 2, 0, :], ALU.add).then_inc(acca_done, 1)
            low_parts(0)

            def split_mlp(it, off):
                sl = (PB + off) % 2
                pool.wait_ge(whi_done, panel_no(it, off) + 1)
                pool.tensor_tensor(w_lo[:, sl, :], w_raw[:, sl, :], w_hi[:, sl, :], ALU.subtract).then_inc(wlo_done, 1)

            def activations(it, par, first=False):
                off = 0 if first else 3 * par - 1
                split_mlp(it, off + 2)
                split_mlp(it, off + 3)
                pool.wait_ge(ahi_done, 2 * it + (par + 1))
                pool.tensor_tensor(a_lo[:, par % 2, :], a_f[:, :], a_hi[:, par % 2, :], ALU.subtract).then_inc(alo_done, 1)

            activations(0, 0, first=True)
            pool.wait_ge(c2_load, 7 * 16)
            pool.affine_select(out=w_sp[:, :, :], in_=w_sp[:, :, :], compare_op=ALU.is_ge, fill=0.0, base=0,
                               pattern=[[0, 4], [-1, P]], channel_multiplier=1).then_inc(wsp_done, 1)
            with pool.Fori(0, (FC - 2) // 2) as it:
                for par in range(2):
                    activations(it, par + 1)
                    split_mlp(it, 3 * par + 6)
            it_last = (FC - 2) // 2
            activations(it_last, 1)
            for m in range(1, KD):
                pool.wait_ge(sqb_done, m + 1)
                if m >= 2:
                    pool.wait_ge(accb_done, m - 1)
                pool.tensor_tensor(n_acc[:, 1, :], n_sq[:, 0, 1, :] if m == 1 else n_acc[:, 1, :], n_sq[:, m % 2, 1, :], ALU.add).then_inc(accb_done, 1)
            split_mlp(it_last, 6)
            split_mlp(it_last, 7)

            low_parts(1)
            for m in range(2):
                behind2(("au", m))
            for m in range(4):
                behind2(("av", m))
            for n in range(4):
                pool.wait_ge(x2_store[n], 32)
            for n in range(NB):
                if n in (3, 5):
                    behind2(("au", (n + 1) // 2))
                pool.wait_ge(vlnhi_done, VLNHI_0 + n + 1)
                pool.tensor_tensor(vln_lo[:, n, :], vn_s[:, n % 2, :], vln_hi[:, n, :], ALU.subtract).then_inc(vlnlo_done, 1)
            behind2(("sk", 0))
            behind2(("sv", 0))
            for kind in ("sq", "mq"):
                for m in range(2):
                    behind2((kind, m))
            pool.wait_ge(kdhi_done, KDHI_0 + 1)
            pool.tensor_tensor(kd_lo[:, :, :], kd_f[:, :, :], kd_hi[:, :, :], ALU.subtract).then_inc(kdlo_done, 1)
            for m in (4, 5, 6, 7, 0, 1, 2, 3):
                behind2(("z", m))
            for m in range(1, KD, 2):
                pool.wait_ge(yhi_done, YHI_0 + m + 1)
                pool.tensor_tensor(x_lo[:, m, 0:S], yz[:, m, :], x_hi[:, m, 0:S], ALU.subtract).then_inc(ylob_done, 1)
            for n in range(2 * KD):
                behind2(("wout", n))
            for b in range(NB):
                pool.wait_ge(x2_load, 16)
                pool.wait_ge(on_done, 2 * b + 1)
                pool.tensor_tensor(o_s[:, b % 4, 0:BANK], o_s[:, b % 4, 0:BANK], x2_tok[:, b, 0:BANK], ALU.add).then_inc(ob_done, 1)


_INS = ["x", "meta", "norm1_g", "w_in", "b_gate", "pool_w", "pool_scale", "w_a", "kv_norm_g", "w_b", "conv_w", "w_c", "w_o",
        "norm2_g", "w_gate_up", "w_down", "final_g", "mem_2", "pre_norm_g_2", "post_norm_g_2", "mem_norm_g_2",
        "w_in_2", "w_mem_kv_2", "v_norm_g_2", "v_norm_b_2", "w_spatial_2", "b_spatial_2", "attn_sinks_2", "rel_bias_2", "w_out_2"]


def kernel(**inputs):
    import concourse.bacc as bacc
    from concourse.bass_utils import run_bass_kernel_spmd

    nc = bacc.Bacc("TRN2", target_bir_lowering=False, num_devices=1, dynamic_dma_scratch_size=1024)
    arrays, I = {}, {}
    for name in _INS:
        a = np.ascontiguousarray(inputs[name])
        arrays[f"in_{name}"] = a
        I[name] = nc.dram_tensor(f"in_{name}", a.shape, mybir.dt.from_np(a.dtype), kind="ExternalInput").ap()
    arrays["in_bucket_table"] = bucket_table()
    I["bucket_table"] = nc.dram_tensor("in_bucket_table", (64, SWA_SPAN), F32, kind="ExternalInput").ap()
    out = nc.dram_tensor("out_0", (1, S, D), F32, kind="ExternalOutput").ap()
    scratch = {name: nc.dram_tensor(f"{name}_scratch", (KD, P, S), F32, kind="Internal").ap() for name in ("q", "g1")}
    scratch["x2"] = nc.dram_tensor("x2_scratch", (S, D), F32, kind="Internal").ap()
    scratch["rb"] = nc.dram_tensor("rb_scratch", (4, SWA_SPAN), F32, kind="Internal").ap()
    build(nc, I, out, scratch)
    return run_bass_kernel_spmd(nc, [arrays], core_ids=[0]).results[0]["out_0"]
```
